# Optimizing a Trainium2 kernel written in Bass

```python
import math
import jax, jax.numpy as jnp
from jax import lax
import numpy as np

D_MODEL = 1024
BATCH = 1
SEQ = 512
DEPTH = 2

N_MEM = 256
GRID_W = 64
EPS = 1e-6
FOURIER_GROUPS = 4
FOURIER_GROUP_DIM = D_MODEL // 8
FOURIER_WIDTH = FOURIER_GROUPS * FOURIER_GROUP_DIM
NA_HEADS = 4
NA_HEAD_DIM = D_MODEL // 8
NA_WIDTH = NA_HEADS * NA_HEAD_DIM
NA_KH = 8
NA_KW = 16
AB_IN_WIDTH = FOURIER_WIDTH + 3 * NA_WIDTH
AB_OUT_WIDTH = FOURIER_WIDTH + NA_WIDTH
CONV_WIDTH = 3
XA_HEADS = 4
XA_HEAD_DIM = D_MODEL // XA_HEADS
D_FF = 2 * D_MODEL
N_EVEN = (DEPTH + 1) // 2
N_ODD = DEPTH // 2


def rms_norm(x, g):
    xf = x.astype(jnp.float32)
    y = xf * lax.rsqrt(jnp.mean(xf * xf, axis=-1, keepdims=True) + EPS)
    return (y * g.astype(jnp.float32)).astype(x.dtype)

def dwconv3_centred(x, w):
    xp = jnp.pad(x, ((0, 0), (1, 1), (0, 0)))
    return xp[:, :-2] * w[0] + xp[:, 1:-1] * w[1] + xp[:, 2:] * w[2]

def fourier_mix(u):
    f = jnp.fft.fft2(u.astype(jnp.float32), axes=(1, 3), norm="ortho")
    return jnp.real(f).astype(u.dtype)

def neighborhood_attention(q, k, v, rpb):
    B, S, H, dh = q.shape
    rows = S // GRID_W
    kh = min(NA_KH, rows)
    kw = NA_KW
    qg = q.reshape(B, rows, GRID_W, H, dh)
    kg = k.reshape(B, rows, GRID_W, H, dh)
    vg = v.reshape(B, rows, GRID_W, H, dh)
    cols = jnp.arange(GRID_W)
    col_start = jnp.clip(cols - kw // 2, 0, GRID_W - kw)
    col_idx = col_start[:, None] + jnp.arange(kw)[None, :]
    col_off = col_idx - cols[:, None] + (NA_KW - 1)
    scale = dh ** -0.5

    def one_row(i):
        rs = jnp.clip(i - kh // 2, 0, rows - kh)
        q_i = lax.dynamic_index_in_dim(qg, i, axis=1, keepdims=False)
        k_blk = lax.dynamic_slice_in_dim(kg, rs, kh, axis=1)
        v_blk = lax.dynamic_slice_in_dim(vg, rs, kh, axis=1)
        k_win = k_blk[:, :, col_idx]
        v_win = v_blk[:, :, col_idx]
        s = jnp.einsum('bjhd,brjchd->bhjrc', q_i, k_win).astype(jnp.float32) * scale
        row_off = rs + jnp.arange(kh) - i + (NA_KH - 1)
        bias = rpb[:, row_off][:, :, col_off]
        s = s + jnp.transpose(bias, (0, 2, 1, 3)).astype(jnp.float32)[None]
        p = jax.nn.softmax(s.reshape(B, H, GRID_W, kh * kw), axis=-1)
        p = p.reshape(B, H, GRID_W, kh, kw).astype(v.dtype)
        return jnp.einsum('bhjrc,brjchd->bjhd', p, v_win)

    out = lax.map(one_row, jnp.arange(rows))
    return jnp.moveaxis(out, 0, 1).reshape(B, S, H, dh)

def fourier_na_mixer(h, w_in, rpb, w_out):
    B, S, _ = h.shape
    z = h @ w_in
    zf = z[..., :FOURIER_WIDTH]
    q = z[..., FOURIER_WIDTH:FOURIER_WIDTH + NA_WIDTH].reshape(B, S, NA_HEADS, NA_HEAD_DIM)
    k = z[..., FOURIER_WIDTH + NA_WIDTH:FOURIER_WIDTH + 2 * NA_WIDTH].reshape(B, S, NA_HEADS, NA_HEAD_DIM)
    v = z[..., FOURIER_WIDTH + 2 * NA_WIDTH:].reshape(B, S, NA_HEADS, NA_HEAD_DIM)
    yf = fourier_mix(zf.reshape(B, S, FOURIER_GROUPS, FOURIER_GROUP_DIM)).reshape(B, S, FOURIER_WIDTH)
    ya = neighborhood_attention(q, k, v, rpb).reshape(B, S, NA_WIDTH)
    return jnp.concatenate([yf, ya], axis=-1) @ w_out

def short_gated_conv_mixer(h, w_in, conv_w, w_out):
    z = h @ w_in
    gate_b = z[..., :D_MODEL]
    gate_c = z[..., D_MODEL:2 * D_MODEL]
    u = z[..., 2 * D_MODEL:]
    return (gate_b * dwconv3_centred(gate_c * u, conv_w)) @ w_out

def memory_cross_attention(h, m, wq, wkv, wo):
    B, S, D = h.shape
    q = (h @ wq).reshape(B, S, XA_HEADS, XA_HEAD_DIM)
    kv = m @ wkv
    k = kv[..., :D].reshape(B, -1, XA_HEADS, XA_HEAD_DIM)
    v = kv[..., D:].reshape(B, -1, XA_HEADS, XA_HEAD_DIM)
    s = jnp.einsum('bshd,bmhd->bhsm', q, k).astype(jnp.float32) * (XA_HEAD_DIM ** -0.5)
    p = jax.nn.softmax(s, axis=-1).astype(v.dtype)
    o = jnp.einsum('bhsm,bmhd->bshd', p, v).reshape(B, S, D)
    return o @ wo

def conv_ffn(h, w_up, conv_w, conv_b, w_down):
    z = h @ w_up
    u = z[..., :D_FF]
    g = dwconv3_centred(z[..., D_FF:], conv_w) + conv_b
    return (jax.nn.gelu(g, approximate=False) * u) @ w_down

def first_inputs(seed: int = 0) -> dict:
    key = jax.random.key(seed)
    ks = jax.random.split(key, 24)
    f32 = jnp.float32
    nrm = lambda k, shape, fan_in: jax.random.normal(k, shape, f32) * (fan_in ** -0.5)
    gain = lambda k, shape: 1.0 + 0.1 * jax.random.normal(k, shape, f32)
    D = D_MODEL
    return {
        "x": jax.random.normal(ks[0], (BATCH, SEQ, D), f32),
        "mem": jax.random.normal(ks[1], (BATCH, N_MEM, D), f32),
        "mem_norm_g": gain(ks[2], (D,)),
        "mix_norm_g": gain(ks[3], (DEPTH, D)),
        "w_in_ab": nrm(ks[4], (N_EVEN, D, AB_IN_WIDTH), D),
        "rpb": 0.02 * jax.random.normal(ks[5], (N_EVEN, NA_HEADS, 2 * NA_KH - 1, 2 * NA_KW - 1), f32),
        "w_out_ab": nrm(ks[6], (N_EVEN, AB_OUT_WIDTH, D), AB_OUT_WIDTH),
        "w_in_c": nrm(ks[7], (N_ODD, D, 3 * D), D),
        "conv_c": nrm(ks[8], (N_ODD, CONV_WIDTH, D), CONV_WIDTH),
        "w_out_c": nrm(ks[9], (N_ODD, D, D), D),
        "xa_norm_g": gain(ks[10], (DEPTH, D)),
        "xa_wq": nrm(ks[11], (DEPTH, D, D), D),
        "xa_wkv": nrm(ks[12], (DEPTH, D, 2 * D), D),
        "xa_wo": nrm(ks[13], (DEPTH, D, D), D),
        "ffn_norm_g": gain(ks[14], (DEPTH, D)),
        "ffn_w_up": nrm(ks[15], (DEPTH, D, 2 * D_FF), D),
        "ffn_conv_w": nrm(ks[16], (DEPTH, CONV_WIDTH, D_FF), CONV_WIDTH),
        "ffn_conv_b": 0.02 * jax.random.normal(ks[17], (DEPTH, D_FF), f32),
        "ffn_w_down": nrm(ks[18], (DEPTH, D_FF, D), D_FF),
        "final_norm_g": gain(ks[19], (D,)),
    }

def first_block(x, mem, mem_norm_g, mix_norm_g, w_in_ab, rpb, w_out_ab, w_in_c, conv_c, w_out_c,
              xa_norm_g, xa_wq, xa_wkv, xa_wo, ffn_norm_g, ffn_w_up, ffn_conv_w, ffn_conv_b,
              ffn_w_down, final_norm_g):
    m = rms_norm(mem, mem_norm_g)
    h = x
    for layer in range(DEPTH):
        hn = rms_norm(h, mix_norm_g[layer])
        if layer % 2 == 0:
            j = layer // 2
            h = h + fourier_na_mixer(hn, w_in_ab[j], rpb[j], w_out_ab[j])
        else:
            j = layer // 2
            h = h + short_gated_conv_mixer(hn, w_in_c[j], conv_c[j], w_out_c[j])
        h = h + memory_cross_attention(rms_norm(h, xa_norm_g[layer]), m,
                                       xa_wq[layer], xa_wkv[layer], xa_wo[layer])
        h = h + conv_ffn(rms_norm(h, ffn_norm_g[layer]), ffn_w_up[layer],
                         ffn_conv_w[layer], ffn_conv_b[layer], ffn_w_down[layer])
    return rms_norm(h, final_norm_g)


DEPTH_2 = 1

RET_HEADS = 8
RET_DK = 64
RET_DV = 128
DN_HEADS = 8
DN_DK = 128
DN_DV = 128
CHUNK = 128
SHORT_CONV = 4
FFN_CONV = 3
D_FF_2 = 2816
ROPE_BASE = 10000.0
GN_EPS = 1e-5

RET_QK = RET_HEADS * RET_DK
RET_V = RET_HEADS * RET_DV
DN_QK = DN_HEADS * DN_DK
DN_V = DN_HEADS * DN_DV
SPLITS = (RET_QK, RET_QK, RET_V, RET_V, DN_QK, DN_QK, DN_V, DN_V, DN_HEADS, DN_HEADS, D_MODEL, D_MODEL)
D_IN = sum(SPLITS)
DN_CONV_CH = 2 * DN_QK + DN_V


def rmsnorm(x, g):
    xf = x.astype(jnp.float32)
    r = lax.rsqrt(jnp.mean(xf * xf, axis=-1, keepdims=True) + EPS)
    return (xf * r) * g

def l2norm(x):
    xf = x.astype(jnp.float32)
    return xf * lax.rsqrt(jnp.sum(xf * xf, axis=-1, keepdims=True) + EPS)

def rotary(x):
    T, d = x.shape[1], x.shape[-1]
    inv = ROPE_BASE ** (-jnp.arange(0, d, 2, dtype=jnp.float32) / d)
    ang = jnp.arange(T, dtype=jnp.float32)[:, None] * inv[None, :]
    cos = jnp.cos(ang)[None, :, None, :]
    sin = jnp.sin(ang)[None, :, None, :]
    x1, x2 = x[..., : d // 2], x[..., d // 2:]
    return jnp.concatenate([x1 * cos - x2 * sin, x1 * sin + x2 * cos], axis=-1)

def causal_dwconv(x, w):
    K, T = w.shape[0], x.shape[1]
    xp = jnp.pad(x, ((0, 0), (K - 1, 0), (0, 0)))
    y = xp[:, K - 1:K - 1 + T] * w[K - 1]
    for k in range(K - 1):
        y = y + xp[:, k:k + T] * w[k]
    return y

def retention_chunkwise(q, k, v):
    B, T, H, dk = q.shape
    dv = v.shape[-1]
    N = T // CHUNK
    f32 = jnp.float32
    gamma = 1.0 - 2.0 ** (-5.0 - jnp.arange(H, dtype=f32))
    log_g = jnp.log(gamma)
    idx = jnp.arange(CHUNK, dtype=f32)
    qc = q.astype(f32).reshape(B, N, CHUNK, H, dk)
    kc = k.astype(f32).reshape(B, N, CHUNK, H, dk)
    vc = v.astype(f32).reshape(B, N, CHUNK, H, dv)
    diff = idx[:, None] - idx[None, :]
    causal = diff >= 0
    dmat = jnp.where(causal[None], jnp.exp(log_g[:, None, None] * jnp.where(causal, diff, 0.0)[None]), 0.0)
    scores = jnp.einsum('bnihd,bnjhd->bnhij', qc, kc) * dmat
    inner = jnp.einsum('bnhij,bnjhv->bnihv', scores, vc)
    zeta = jnp.exp(log_g[:, None] * (CHUNK - 1.0 - idx)[None, :])
    kv = jnp.einsum('bnjhd,hj,bnjhv->bnhdv', kc, zeta, vc)
    chunk_decay = jnp.exp(log_g * CHUNK)[:, None, None]

    def step(S, kv_n):
        return S * chunk_decay + kv_n, S

    _, s_prev = lax.scan(step, jnp.zeros((B, H, dk, dv), f32), jnp.moveaxis(kv, 1, 0))
    xi = jnp.exp(log_g[:, None] * (idx + 1.0)[None, :])
    cross = jnp.einsum('bnihd,nbhdv,hi->bnihv', qc, s_prev, xi)
    return (inner + cross).reshape(B, T, H, dv)

def gated_delta_chunkwise(q, k, v, g, beta):
    B, T, H, dk = q.shape
    dv = v.shape[-1]
    N = T // CHUNK
    f32 = jnp.float32

    def to_chunks(t):
        return jnp.moveaxis(t.astype(f32).reshape((B, N, CHUNK, H) + t.shape[3:]), 3, 1)

    qc = to_chunks(q) * (dk ** -0.5)
    kc = to_chunks(k)
    vc = to_chunks(v)
    gc = to_chunks(g)
    bc = to_chunks(beta)
    G = jnp.cumsum(gc, axis=-1)
    idx = jnp.arange(CHUNK)
    causal = idx[:, None] >= idx[None, :]
    strict = idx[:, None] > idx[None, :]
    diff = G[..., :, None] - G[..., None, :]
    L = jnp.where(causal, jnp.exp(jnp.where(causal, diff, 0.0)), 0.0)
    k_beta = kc * bc[..., None]
    A = jnp.where(strict, jnp.einsum('bhnid,bhnjd->bhnij', k_beta, kc) * L, 0.0)
    eye = jnp.eye(CHUNK, dtype=f32)
    rhs = jnp.concatenate([vc * bc[..., None], k_beta * jnp.exp(G)[..., None]], axis=-1)
    sol = lax.linalg.triangular_solve(eye + A, rhs, left_side=True, lower=True, unit_diagonal=True)
    u, w = sol[..., :dv], sol[..., dv:]
    attn = jnp.where(causal, jnp.einsum('bhnid,bhnjd->bhnij', qc, kc) * L, 0.0)
    q_dec = qc * jnp.exp(G)[..., None]
    k_dec = kc * jnp.exp(G[..., -1:] - G)[..., None]
    chunk_dec = jnp.exp(G[..., -1])

    def step(S, inp):
        u_n, w_n, q_n, k_n, a_n, d_n = inp
        v_new = u_n - jnp.einsum('bhcd,bhdv->bhcv', w_n, S)
        o = jnp.einsum('bhcd,bhdv->bhcv', q_n, S) + jnp.einsum('bhij,bhjv->bhiv', a_n, v_new)
        S = S * d_n[..., None, None] + jnp.einsum('bhcd,bhcv->bhdv', k_n, v_new)
        return S, o

    xs = tuple(jnp.moveaxis(t, 2, 0) for t in (u, w, q_dec, k_dec, attn, chunk_dec))
    _, o = lax.scan(step, jnp.zeros((B, H, dk, dv), f32), xs)
    return o.transpose(1, 0, 3, 2, 4).reshape(B, T, H, dv)

def second_inputs(seed: int = 0) -> dict:
    key = jax.random.key(seed)
    ks = jax.random.split(key, 20)
    f32 = jnp.float32
    nrm = lambda k, shape, s: jax.random.normal(k, shape, f32) * s
    dt = jnp.exp(jax.random.uniform(ks[6], (DEPTH_2, DN_HEADS), f32, np.log(1e-3), np.log(1e-1)))
    return {
        "x": jax.random.normal(ks[0], (BATCH, SEQ, D_MODEL), f32),
        "g_mix": 1.0 + nrm(ks[1], (DEPTH_2, D_MODEL), 0.05),
        "w_in": nrm(ks[2], (DEPTH_2, D_MODEL, D_IN), D_MODEL ** -0.5),
        "ret_norm_g": 1.0 + nrm(ks[3], (DEPTH_2, RET_V), 0.05),
        "dn_conv_w": nrm(ks[4], (DEPTH_2, SHORT_CONV, DN_CONV_CH), SHORT_CONV ** -0.5),
        "dn_a_log": jnp.log(jax.random.uniform(ks[5], (DEPTH_2, DN_HEADS), f32, 1.0, 16.0)),
        "dn_dt_bias": dt + jnp.log(-jnp.expm1(-dt)),
        "dn_norm_g": 1.0 + nrm(ks[7], (DEPTH_2, DN_DV), 0.05),
        "w_ret_br": nrm(ks[8], (DEPTH_2, RET_V, D_MODEL), RET_V ** -0.5),
        "w_dn_br": nrm(ks[9], (DEPTH_2, DN_V, D_MODEL), DN_V ** -0.5),
        "w_o": nrm(ks[10], (DEPTH_2, D_MODEL, D_MODEL), D_MODEL ** -0.5),
        "g_ffn": 1.0 + nrm(ks[11], (DEPTH_2, D_MODEL), 0.05),
        "w_up": nrm(ks[12], (DEPTH_2, D_MODEL, 2 * D_FF_2), D_MODEL ** -0.5),
        "ffn_conv_w": nrm(ks[13], (DEPTH_2, FFN_CONV, 2 * D_FF_2), FFN_CONV ** -0.5),
        "ffn_conv_b": nrm(ks[14], (DEPTH_2, 2 * D_FF_2), 0.01),
        "w_down": nrm(ks[15], (DEPTH_2, D_FF_2, D_MODEL), D_FF_2 ** -0.5),
        "g_final": 1.0 + nrm(ks[16], (D_MODEL,), 0.05),
    }

def second_block(x, g_mix, w_in, ret_norm_g, dn_conv_w, dn_a_log, dn_dt_bias, dn_norm_g,
              w_ret_br, w_dn_br, w_o, g_ffn, w_up, ffn_conv_w, ffn_conv_b, w_down, g_final):
    B, T, _ = x.shape
    h = x.astype(jnp.float32)
    split_at = np.cumsum(SPLITS)[:-1].tolist()
    for l in range(DEPTH_2):
        u = rmsnorm(h, g_mix[l])
        proj = u @ w_in[l]
        (rq, rk, rv, rgate, dq, dk_, dv_, dz, db, da, gate_r, gate_d) = jnp.split(proj, split_at, axis=-1)

        rq = rotary(rq.reshape(B, T, RET_HEADS, RET_DK))
        rk = rotary(rk.reshape(B, T, RET_HEADS, RET_DK)) * (RET_DK ** -0.5)
        ro = retention_chunkwise(rq, rk, rv.reshape(B, T, RET_HEADS, RET_DV))
        mu = jnp.mean(ro, axis=-1, keepdims=True)
        var = jnp.mean(jnp.square(ro - mu), axis=-1, keepdims=True)
        ro = ((ro - mu) * lax.rsqrt(var + GN_EPS)).reshape(B, T, RET_V) * ret_norm_g[l]
        y_ret = (jax.nn.silu(rgate) * ro) @ w_ret_br[l]

        qkv = jax.nn.silu(causal_dwconv(jnp.concatenate([dq, dk_, dv_], axis=-1), dn_conv_w[l]))
        cq, ck, cv = jnp.split(qkv, [DN_QK, 2 * DN_QK], axis=-1)
        cq = l2norm(cq.reshape(B, T, DN_HEADS, DN_DK))
        ck = l2norm(ck.reshape(B, T, DN_HEADS, DN_DK))
        cv = cv.reshape(B, T, DN_HEADS, DN_DV)
        g = -jnp.exp(dn_a_log[l]) * jax.nn.softplus(da.astype(jnp.float32) + dn_dt_bias[l])
        beta = jax.nn.sigmoid(db.astype(jnp.float32))
        do = gated_delta_chunkwise(cq, ck, cv, g, beta)
        do = do * lax.rsqrt(jnp.mean(do * do, axis=-1, keepdims=True) + EPS) * dn_norm_g[l]
        do = do.reshape(B, T, DN_V) * jax.nn.silu(dz)
        y_dn = do @ w_dn_br[l]

        merged = jax.nn.sigmoid(gate_r) * y_ret + jax.nn.sigmoid(gate_d) * y_dn
        h = h + merged @ w_o[l]

        u2 = rmsnorm(h, g_ffn[l])
        up = causal_dwconv(u2 @ w_up[l], ffn_conv_w[l]) + ffn_conv_b[l]
        a, b = jnp.split(up, 2, axis=-1)
        h = h + (jax.nn.silu(a) * b) @ w_down[l]
    return rmsnorm(h, g_final).astype(x.dtype)


def setup_inputs(seed=0):
    out = dict(first_inputs(seed))
    for name, value in second_inputs(seed + 1).items():
        if name != "x":
            out[name + "_2"] = value
    return out


def reference(
    x, mem, mem_norm_g, mix_norm_g, w_in_ab, rpb, w_out_ab, w_in_c, conv_c, w_out_c, xa_norm_g,
    xa_wq, xa_wkv, xa_wo, ffn_norm_g, ffn_w_up, ffn_conv_w, ffn_conv_b, ffn_w_down,
    final_norm_g, g_mix_2, w_in_2, ret_norm_g_2, dn_conv_w_2, dn_a_log_2, dn_dt_bias_2,
    dn_norm_g_2, w_ret_br_2, w_dn_br_2, w_o_2, g_ffn_2, w_up_2, ffn_conv_w_2, ffn_conv_b_2,
    w_down_2, g_final_2,
):
    x = first_block(
        x, mem, mem_norm_g, mix_norm_g, w_in_ab, rpb, w_out_ab, w_in_c, conv_c, w_out_c,
        xa_norm_g, xa_wq, xa_wkv, xa_wo, ffn_norm_g, ffn_w_up, ffn_conv_w, ffn_conv_b,
        ffn_w_down, final_norm_g,
    )
    return second_block(
        x, g_mix_2, w_in_2, ret_norm_g_2, dn_conv_w_2, dn_a_log_2, dn_dt_bias_2, dn_norm_g_2,
        w_ret_br_2, w_dn_br_2, w_o_2, g_ffn_2, w_up_2, ffn_conv_w_2, ffn_conv_b_2, w_down_2,
        g_final_2,
    )


_drawn_inputs = setup_inputs


def setup_inputs(seed=0):
    import zlib

    import numpy as np

    out = dict(_drawn_inputs(seed))
    spreads = {}
    factors = {'rpb': 8.0,
     'ffn_conv_b': 2.687,
     'ret_norm_g_2': 3.455,
     'dn_norm_g_2': 3.848,
     'ffn_conv_b_2': 8.0}
    for name, (base, spread) in spreads.items():
        noise = np.random.default_rng([zlib.crc32(name.encode()), seed]).standard_normal(out[name].shape)
        drawn = base * np.exp(spread * noise) if base else spread * noise
        out[name] = __import__('jax').numpy.asarray(drawn.astype(out[name].dtype))
    for name, factor in factors.items():
        out[name] = (out[name] * factor).astype(out[name].dtype)
    return out
```

```python
from contextlib import ExitStack

import concourse.bass as bass
import numpy as np
from concourse import mybir

F32 = mybir.dt.float32
F32R = mybir.dt.float32r
ACT = mybir.ActivationFunctionType
ALU = mybir.AluOpType
AX = mybir.AxisListType

P = 128
D = 1024
KT = D // P
T = 512
NMEM = 256
EPS = 1e-6
GN_EPS = 1e-5
UC = 512
RING = 4
LO_RING = 4
KB = 1024

NA_H = 4
GRID_W = 64
ROWS = T // GRID_W
NA_KH, NA_KW = 8, 16
RPB_W = 2 * NA_KW - 1
RPB_PAD = GRID_W - NA_KW
RPB_PW = RPB_W + 2 * RPB_PAD
NA_ROWS = 2 * NA_KH - 2
XA_H = 4
FF1 = 2048
RET_H = 8
FF2 = 2816
DN_H = 8
NCH = T // P

BIG_SLOTS = 2 * FF2 // P
TAIL = 26 * KB

PARAM_COLS = {}


def _cols(name, n):
    start = sum(c for _, c in PARAM_COLS.values())
    PARAM_COLS[name] = (start, n)


for _n in ("mem", "mix0", "xa0", "ffn0", "mix1", "xa1", "ffn1", "final1", "mix2", "ffn2", "final2"):
    _cols(_n, KT)
_cols("conv_c", 3 * KT)
for _l in range(2):
    _cols(f"ffn_w{_l}", 3 * FF1 // P)
    _cols(f"ffn_b{_l}", FF1 // P)
_cols("ret_g", RET_H)
_cols("dn_conv", 4 * 3 * DN_H)
_cols("dn_g", 1)
_cols("ffn_w2", 3 * 2 * FF2 // P)
_cols("ffn_b2", 2 * FF2 // P)
_cols("a_log", 1)
_cols("dt_bias", 1)
N_PARAMS = sum(c for _, c in PARAM_COLS.values())

CONSTS = {"ident": 0, "ones": 1, "rot": 2, "causal": 3}
N_CONST = len(CONSTS)
LEVELS = (1, 2, 4, 8, 16, 32, 64)


def program(nc, ins, out, stop=None):
    ctx = ExitStack()
    with ctx:
        def sb(name, shape, dt=F32):
            return ctx.enter_context(nc.sbuf_tensor(name, shape, dt))

        def sem(name):
            return ctx.enter_context(nc.semaphore(name))

        H = sb("H", [P, KT, T])
        XH = sb("XH", [P, KT, T], F32R)
        XL = sb("XL", [P, KT, T], F32R)
        w_raw = sb("w_raw", [P, RING, 2, UC])
        w_hi = sb("w_hi", [P, RING, 2, UC], F32R)
        w_lo = sb("w_lo", [P, LO_RING, 2, UC], F32R)
        R = sb("R", [P, T])
        LNT = sb("LNT", [P, T])
        RC = sb("RC", [P, NCH])
        LNC = sb("LNC", [P, NCH])
        ACC = sb("ACC", [P, T])
        SQ = sb("SQ", [P, T])
        par = sb("par", [P, N_PARAMS])
        cst = sb("cst", [P, N_CONST, P])
        eps_c = sb("eps_c", [P, 2])
        sm = sb("sm", [P, 128])
        base_before = (nc.sbuf_base + 31) // 32 * 32
        arena = sb("arena", [P, (BIG_SLOTS * T * 4 + TAIL) // 4])
        ps = ctx.enter_context(nc.psum_tensor("ps", [P, 8, T], F32))
        a0 = base_before

        def at(name, kb, shape, dt=F32):
            return nc.alloc_sbuf_tensor_at(name, shape, dt, offset=a0 + int(kb * KB))

        ident = cst[:, CONSTS["ident"], :]
        ones = cst[:, CONSTS["ones"], :]

        def backwards(ap):
            return bass.AP(ap.tensor, ap.offset + P - 1, [list(ap.ap[0]), [P, T // P], [-1, P]])

        def pcol(name, i=0, n=1):
            c = PARAM_COLS[name][0] + i
            return par[:, c:c + n]

        HID = at("HID", 0, [P, BIG_SLOTS, T], F32R)
        Y0, SCR, TL = 0, 32, 88
        YH = HID[:, 0:KT, :]
        YL = HID[:, KT:2 * KT, :]
        Q = at("Q", SCR, [P, NA_H, T])
        K = at("K", SCR + 8, [P, NA_H, T])
        V = at("V", SCR + 16, [P, NCH, NA_H * P])
        ZC = at("ZC", SCR + 24, [P, NA_H * NCH * 2 * P])
        FC = at("FC", SCR + 40, [P, NCH, 2, T])
        GC = at("GC", TL + 14, [P, 2 * P])
        B2 = at("B2", TL, [P, NA_H, NA_ROWS, GRID_W])
        Z = at("Z", TL + 16, [P, NA_H, T])
        S = at("S", SCR + 24, [P, 2, T])
        PR = at("PR", SCR + 28, [P, 2, T])
        PT = at("PT", SCR + 32, [P, 2, NCH, T])
        KX = at("KX", TL, [P, KT, NMEM])
        VX = at("VX", TL + 8, [P, 2, D])
        M = at("M", TL + 16, [P, KT, NMEM])
        QX = at("QX", SCR, [P, KT, T])
        PX = at("PX", SCR + 16, [P, 2, NCH, NMEM])
        PTX = at("PTX", SCR + 24, [P, 2, 2, T])
        MSQ = at("MSQ", SCR, [P, KT, NMEM])
        MACC = at("MACC", SCR + 8, [P, NMEM])
        ML = at("ML", SCR + 9, [P, NMEM])
        MR = at("MR", SCR + 10, [P, NMEM])
        F1 = 64
        GP = at("GP", F1, [P, 2, T + 2])
        CV = at("CV", F1 + 4.5, [P, 2, T])
        EG = at("EG", F1 + 8.5, [P, 2, T])
        UU = at("UU", F1 + 12.5, [P, 2, T])
        HF = at("HF", F1 + 16.5, [P, 2, T])
        CS = at("CS", SCR, [P, 4, T])
        VP = at("VP", SCR + 8, [P, 4, T + 2])
        CVC = at("CVC", SCR + 17, [P, 4, T])
        TY = at("TY", SCR + 25, [P, 4, T])

        RQ = at("RQ", SCR, [P, 4, T])
        RK = at("RK", SCR + 8, [P, 4, T])
        RV = at("RV", SCR + 16, [P, NCH, RET_H * P])
        RO = at("RO", SCR + 32, [P, RET_H, T])
        RT = at("RT", 0, [P, 4, T])
        SCO = at("SCO", 80, [P, 2, 1280])
        DEC = at("DEC", 90, [P, 2, T])
        COS = at("COS", 94, [P, T])
        SIN = at("SIN", 96, [P, T])
        AGE = at("AGE", 98, [P, T])
        RSQ = at("RSQ", 100, [P, T])
        RLN = at("RLN", 102, [P, T])
        RN = at("RN", 104, [P, T])
        RVM = at("RVM", 106, [P, NCH, RET_H])
        TG = at("TG", SCR, [P, 4, T])
        SG = at("SG", SCR + 8, [P, 4, T])
        MG = at("MG", 96, [P, KT, T])
        DO = at("DO", 80, [P, DN_H, T])
        QN = at("QN", 0, [P, 4, T])
        KN = at("KN", 8, [P, 4, T])
        VB = at("VB", 16, [P, 4, T])
        MT = at("MT", 24, [P, 4, T])
        ATT = at("ATT", 32, [P, 4, T])
        KD = at("KD", 40, [P, 4, T])
        GP3 = at("GP3", 48, [P, 4, T + 3])
        SQq, LNq = at("SQq", 24, [P, 4, T]), at("LNq", 32, [P, 4, T])
        SQk, LNk = at("SQk", 56.5, [P, 4, T]), at("LNk", 40, [P, 4, T])
        DL = at("DL", 48, [P, 2, T])
        AT = at("AT", 52, [P, 2, T])
        MM = at("MM", 56, [P, 2, T])
        T1 = at("T1", 60, [P, 2, T])
        SQo, LNo = at("SQo", 48, [P, 4, T]), at("LNo", 56, [P, 4, T])
        EGA = [at("EGA0", 64, [P, T]), at("EGA1", 69.5, [P, T])]
        LVM = at("LVM", 66, [P, len(LEVELS), P])
        YS = at("YS", 69.5, [P, 4, P])
        VS = at("VS", 71.5, [P, 4, P])
        SS = at("SS", 73.5, [P, 4, P])
        GR = at("GR", 75.5, [DN_H, T])
        BR = at("BR", 77.5, [DN_H, T])
        TC = at("TC", 79.5, [P, 4, NCH, DN_H])
        rows = [at(f"row{i}", 48 + 2 * i, [DN_H, T]) for i in range(8)]
        SGD = H
        TZ = at("TZ", SCR + 16, [P, 4, T])
        GP4 = at("GP4", TL, [P, 4, T + 2])
        CV4 = at("CV4", TL + 8.25, [P, 4, T])
        SA = at("SA", TL + 16.25, [P, 2, T])
        HF2 = at("HF2", TL + 20.25, [P, 2, T])

        def cols(*starts):
            return [[(c, UC)] for c in starts]

        def halves(a, b, n):
            return [[(a + 256 * j, 256), (b + 256 * j, 256)] for j in range(n)]

        W = ins
        phases = [("in0", W["w_in_ab"][0], KT, cols(*range(0, 2048, UC))),
                  ("out0", W["w_out_ab"][0], KT, cols(0, UC))]
        for l in range(2):
            if l == 1:
                phases += [("in1", W["w_in_c"][0], KT,
                            cols(1024, 2048, 0, 1024 + UC, 2048 + UC, UC)),
                           ("out1", W["w_out_c"][0], KT, cols(0, UC))]
            phases += [(f"q{l}", W["xa_wq"][l], KT, cols(0, UC)),
                       (f"wo{l}", W["xa_wo"][l], KT, cols(0, UC)),
                       (f"up{l}", W["ffn_w_up"][l], KT, halves(0, FF1, FF1 // 256)),
                       (f"down{l}", W["ffn_w_down"][l], FF1 // P, cols(0, UC))]
        W2 = W["w_in_2"][0]
        phases += [("rqk", W2, KT, cols(0, 512)), ("rv", W2, KT, cols(1024, 1536)),
                   ("rgate", W2, KT, cols(2048, 2560)), ("gater", W2, KT, cols(C_GR, C_GR + UC)),
                   ("retbr", W["w_ret_br_2"][0], KT, cols(0, UC)),
                   ("dab", W2, 2, [[(C_DB, 32), (C_DA, 32), (C_GR, 64)]]),
                   ("dvqk0", W2, KT, cols(5120, 3072, 4096)), ("gated0", W2, KT, cols(C_GD)),
                   ("dvqk1", W2, KT, cols(5120 + UC, 3072 + UC, 4096 + UC)), ("gated1", W2, KT, cols(C_GD + UC)),
                   ("dz", W2, KT, cols(6144, 6144 + UC)),
                   ("dnbr", W["w_dn_br_2"][0], KT, cols(0, UC)), ("wo2", W["w_o_2"][0], KT, cols(0, UC)),
                   ("up2", W["w_up_2"][0], KT, halves(0, FF2, FF2 // 256)),
                   ("down2", W["w_down_2"][0], FF2 // P, cols(0, UC))]
        if stop is not None:
            names = [p[0] for p in phases]
            phases = phases[:names.index(stop) + 1]
        first, count = {}, {}
        n_units = 0
        unit = []
        for name, mat, nk, groups in phases:
            first[name] = n_units
            for g, pieces in enumerate(groups):
                for k in range(nk // 2):
                    unit.append((name, mat, k, pieces))
            n_units = len(unit)
            count[name] = n_units - first[name]
        kv_after = {}
        for l in range(2):
            if f"q{l}" in first:
                kv_after[first[f"q{l}"] + RING] = l
        load_value, at_slot = {}, [0] * RING
        kv_value = {}
        for u in range(n_units + 1):
            if u in kv_after:
                for i in range(16):
                    at_slot[i % RING] += 16
                    kv_value[kv_after[u], i] = at_slot[i % RING]
            if u < n_units:
                at_slot[u % RING] += 16 * len(unit[u][3])
                load_value[u] = at_slot[u % RING]

        w_loaded = [sem(f"w_loaded{s}") for s in range(RING)]
        hi_done = sem("hi_done")
        lo_done = sem("lo_done")
        w_used = sem("w_used")
        kv_used = sem("kv_used")
        x_loaded = [sem(f"x_loaded{i}") for i in range(KT // 2)]
        c_loaded = sem("c_loaded")
        m_loaded = sem("m_loaded")
        f_loaded = sem("f_loaded")
        b_loaded = sem("b_loaded")
        out_stored = sem("out_stored")
        h_upd = sem("h_upd")
        sq_done = sem("sq_done")
        x_hi = sem("x_hi")
        x_lo = sem("x_lo")
        acc_done = sem("acc_done")
        st_done = sem("st_done")
        ln_done = sem("ln_done")
        r_done = sem("r_done")
        in0_z = sem("in0_z")
        f1_done = sem("f1_done")
        f1_out = sem("f1_out")
        f2_done = sem("f2_done")
        na_s, na_add, na_mn, na_exp, na_rr, na_p, na_t, na_pt, na_pv = [
            sem(f"na_{x}") for x in ("s", "add", "mn", "exp", "rr", "p", "t", "pt", "pv")]
        y0_hi, y0_lo = sem("y0_hi"), sem("y0_lo")
        b2_sel = sem("b2_sel")
        m_sq, m_acc, m_st, m_ln, m_r, m_done = [sem(f"m_{x}") for x in ("sq", "acc", "st", "ln", "r", "done")]
        kv_out = sem("kv_out")
        q_out = sem("q_out")
        xa_s, xa_mx, xa_nm, xa_exp, xa_rr, xa_p, xa_t, xa_pt, xa_pv, xa_hi, xa_lo = [
            sem(f"xa_{x}") for x in ("s", "mx", "nm", "exp", "rr", "p", "t", "pt", "pv", "hi", "lo")]
        ffn_dve = sem("ffn_dve")
        ffn_act = sem("ffn_act")
        cm_dve = sem("cm_dve")
        cm_act = sem("cm_act")
        pad_zero = sem("pad_zero")
        pad_d = sem("pad_d")

        t_loaded = sem("t_loaded")
        l_loaded = sem("l_loaded")
        rqk_out, rv_out, rot_done, rot_out = [sem(x) for x in ("rqk_out", "rv_out", "rot_done", "rot_out")]
        ret_s, ret_sc, ret_dec, ret_o, ret_sq, ret_v, ret_ln, ret_rn, ret_ro = [
            sem(f"ret_{x}") for x in ("s", "sc", "dec", "o", "sq", "v", "ln", "rn", "ro")]
        rg_dve, rg_act, gr_dve, gr_act, rb_dve = [sem(x) for x in ("rg_dve", "rg_act", "gr_dve", "gr_act", "rb_dve")]
        ab_dve, ab_act, ab_t = sem("ab_dve"), sem("ab_act"), sem("ab_t")
        dq_dve, dq_act = sem("dq_dve"), sem("dq_act")
        l2_sq, l2_st, l2_ln, l2_r, l2_n = [sem(f"l2_{x}") for x in ("sq", "st", "ln", "r", "n")]
        dp_bc, dp_tr, dp_eg, dp_lt, dp_a, dp_dve = [sem(f"dp_{x}") for x in ("bc", "tr", "eg", "lt", "a", "dve")]
        lv_pe, lv_dve = sem("lv_pe"), sem("lv_dve")
        sc_ks, sc_vn, sc_su, sc_o, sc_y, sc_s, sc_vc = [sem(f"sc_{x}") for x in ("ks", "vn", "su", "o", "y", "s", "vc")]
        do_sq, do_st, do_ln, do_r, do_n = [sem(f"do_{x}") for x in ("sq", "st", "ln", "r", "n")]
        h_saved = sem("h_saved")
        h_back = sem("h_back")
        ga_dve, ga_act, dz_dve, dz_act, dn_dve, dn_act = [
            sem(x) for x in ("ga_dve", "ga_act", "dz_dve", "dz_act", "dn_dve", "dn_act")]
        up2_dve, up2_act = sem("up2_dve"), sem("up2_act")
        fin_dve = sem("fin_dve")

        two = "rqk" in first
        RPS = [n for n in ("out0", "wo0", "down0", "out1", "wo1", "down1") if n in first] + two * ["bnorm", "wo2", "down2"]
        rp_index = {n: i for i, n in enumerate(RPS)}
        gain_after = {"out0": "xa0", "wo0": "ffn0", "down0": "mix1", "out1": "xa1", "wo1": "ffn1", "down1": "final1",
                      "bnorm": "mix2", "wo2": "ffn2", "down2": "final2"}
        norm_of = {"in0": 0, "q0": 1, "up0": 2, "in1": 3, "q1": 4, "up1": 5,
                   "bnorm": 6, "rqk": 7, "up2": 8, "final": 9}
        FD = 10
        FA = 3
        FD2, FA2 = 15, 2

        def pair_step(p, k):
            return 3 * p + k if k <= 3 else 6 + 9 * p + k - 3

        h_dram = nc.dram_tensor("h_dram", (P, KT * T), F32, kind="Internal").ap()
        block = ctx.enter_context(nc.Block())

        @block.sync
        def _(sp):
            def load(mat, k, c_of, slot, freed):
                for s, v in freed:
                    sp.wait_ge(s, v)
                view = mat.rearrange("(k p) n -> p k n", p=P)
                at_col = 0
                for c, width in c_of:
                    sp.dma_start(w_raw[:, slot, :, at_col:at_col + width],
                                 view[:, 2 * k:2 * k + 2, c if isinstance(c, slice) else bass.ds(c, width)]
                                 ).then_inc(w_loaded[slot], 16)
                    at_col += width

            def load_kv(l):
                view = W["xa_wkv"][l].rearrange("(k p) n -> p k n", p=P)
                u0 = first[f"q{l}"] + RING
                for i in range(16):
                    if i < RING:
                        sp.wait_ge(lo_done, u0 - RING + i + 1)
                    else:
                        sp.wait_ge(kv_used, 16 * l + i - RING + 1)
                    sp.dma_start(w_raw[:, i % RING, :, :],
                                 view[:, 2 * (i % 4):2 * (i % 4) + 2, (i // 4) * UC:(i // 4 + 1) * UC]
                                 ).then_inc(w_loaded[i % RING], 16)

            xv = ins["xT"].rearrange("(k p) t -> p k t", p=P)
            sp.dma_start(par[:, :], ins["params"]).then_inc(c_loaded, 16)
            sp.dma_start(H[:, 0:2, :], xv[:, 0:2, :]).then_inc(x_loaded[0], 16)
            sp.dma_start(cst[:, :, :], ins["consts"]).then_inc(c_loaded, 16)
            for name, mat, nk, groups in phases:
                u0, per = first[name], nk // 2
                if name == "rqk":
                    sp.wait_ge(h_upd, KT * (rp_index["wo1"] + 1))
                    for tab, src in ((COS, "rot_cos"), (SIN, "rot_sin"), (AGE, "age")):
                        sp.dma_start(tab[:, :], ins[src]).then_inc(t_loaded, 16)
                if name == "dab":
                    u = u0
                    sp.wait_ge(lo_done, u - RING + 1)
                    view = mat.rearrange("(k p) n -> p k n", p=P)
                    dst = w_raw[:, u % RING, :, :].rearrange("p a (b c) -> p (a b) c", c=P)
                    at_col = 0
                    for c, width in groups[0]:
                        sp.dma_start(dst[:, :, at_col:at_col + width], view[:, :, c:c + width]
                                     ).then_inc(w_loaded[u % RING], 16)
                        at_col += width
                    sp.wait_ge(rg_dve, 6)
                    sp.dma_start(LVM[:, :, :], ins["levels"]).then_inc(l_loaded, 16)
                    continue
                if name == "rv":
                    sp.wait_ge(h_upd, KT * (rp_index["bnorm"] + 1))
                    sp.dma_start(h_dram, H[:, :, :].rearrange("p k t -> p (k t)")).then_inc(h_saved, 16)
                for g in range(1 if name.startswith("up") else len(groups)):
                    if name == "wo2" and g == 1:
                        sp.wait_ge(dn_dve, 4)
                        sp.wait_ge(h_saved, 16)
                        sp.dma_start(H[:, :, :].rearrange("p k t -> p (k t)"), h_dram).then_inc(h_back, 16)
                    for k in range(per):
                        u = u0 + g * per + k
                        if u in kv_after:
                            load_kv(kv_after[u])
                        kv = [l for b, l in kv_after.items() if 0 <= u - b < RING]
                        freed = [] if u < RING else [(kv_used, 16 * kv[0] + 12 + (u - first[f"q{kv[0]}"] - RING) + 1)] if kv \
                            else [(lo_done, u - RING + 1)]
                        load(mat, k, groups[g], u % RING, freed)
                        if u < KT // 2 - 1:
                            c = 2 * u + 2
                            sp.dma_start(H[:, c:c + 2, :], xv[:, c:c + 2, :]).then_inc(x_loaded[u + 1], 16)
                    if name == "in0" and g == 1:
                        sp.dma_start(FC[:, :, :, :], ins["fourier_seq"]).then_inc(f_loaded, 16)
                        sp.dma_start(GC[:, :], ins["fourier_grp"]).then_inc(f_loaded, 16)
                        rp = ins["rpb"]
                        for h in range(NA_H):
                            for i in range(2):
                                src = bass.AP(rp.tensor, (h * 15 + i) * RPB_PW, [[1, GRID_W], [RPB_PW, NA_ROWS], [1, GRID_W]])
                                sp.dma_start(B2[GRID_W * i:GRID_W * (i + 1), h, :, :], src).then_inc(b_loaded, 16)
                if name.startswith("up"):
                    with sp.Fori(1, len(groups)) as i:
                        for k in range(per):
                            load(mat, k, [(groups[0][q][0] + i * 256, 256) for q in range(2)],
                                 (u0 + k) % RING, [(lo_done, i * per + (u0 + k - RING + 1))])
                if name == "out0":
                    sp.wait_ge(f1_done, 8)
                    mv = ins["memT"].rearrange("(k p) t -> p k t", p=P)
                    sp.dma_start(M[:, :, :], mv).then_inc(m_loaded, 16)
            ov = out.rearrange("(k p) t -> p k t", p=P)
            n = len(RPS)
            for k in range(KT):
                if two:
                    sp.wait_ge(fin_dve, k + 1)
                else:
                    sp.wait_ge(h_upd, KT * (n - 1) + k + 1)
                sp.dma_start(ov[:, k, :], H[:, k, :]).then_inc(out_stored, 16)
            sp.wait_ge(out_stored, 16 * KT)

        @block.gpsimd
        def _(pool):
            nc.gpsimd.memset(eps_c[:, 0:1], EPS)
            nc.gpsimd.memset(eps_c[:, 1:2], GN_EPS).then_inc(pad_zero, 1)

            def lo(u, slot):
                pool.wait_ge(hi_done, u + 1)
                nc.gpsimd.tensor_tensor(w_lo[:, slot % LO_RING, :, :], w_raw[:, slot, :, :],
                                        w_hi[:, slot, :, :].bitcast(F32), ALU.subtract).then_inc(lo_done, 1)

            early = 4 * RING
            for u in range(early):
                if u >= LO_RING:
                    pool.wait_ge(w_used, u - LO_RING + 1)
                lo(u, u % RING)
            pool.wait_ge(b_loaded, 16 * 2 * NA_H)
            n = 0
            for i in range(2):
                half = B2[GRID_W * i:GRID_W * (i + 1), :, :, :].rearrange("p h s c -> p (h s) c")
                lowc = half[:, :, 0:GRID_W - NA_KW]
                nc.gpsimd.affine_select(out=lowc, in_=lowc, compare_op=ALU.is_ge, fill=-1e30,
                                        base=NA_KW // 2 - (GRID_W - 1),
                                        pattern=[[0, NA_H * NA_ROWS], [1, GRID_W - NA_KW]],
                                        channel_multiplier=1).then_inc(b2_sel, 1)
                n += 1
                pool.wait_ge(b2_sel, n)
                high = half[:, :, NA_KW:GRID_W]
                nc.gpsimd.affine_select(out=high, in_=high, compare_op=ALU.is_ge, fill=-1e30,
                                        base=NA_KW // 2 - 1 - NA_KW + GRID_W - 1,
                                        pattern=[[0, NA_H * NA_ROWS], [-1, GRID_W - NA_KW]],
                                        channel_multiplier=-1).then_inc(b2_sel, 1)
                n += 1
                pool.wait_ge(b2_sel, n)
            whole = n_units // RING
            with pool.Fori(early // RING, whole) as i:
                for s in range(RING):
                    pool.wait_ge(w_used, i * RING + (s - LO_RING + 1))
                    lo(i * RING + s, s)
            for u in range(whole * RING, n_units):
                pool.wait_ge(w_used, u - LO_RING + 1)
                lo(u, u % RING)

        @block.scalar
        def _(act):
            state = {"split": 0}

            def split(u, slot, loaded):
                act.wait_ge(w_loaded[slot], loaded)
                nc.scalar.activation(w_hi[:, slot, :, :], w_raw[:, slot, :, :], ACT.Copy).then_inc(hi_done, 1)

            def split_to(end):
                while state["split"] < min(end, n_units):
                    u = state["split"]
                    if u >= RING:
                        act.wait_ge(w_used, u - RING + 1)
                    split(u, u % RING, load_value[u])
                    state["split"] += 1

            def norm_inputs(j, c, gain):
                nc.scalar.activation(ACC[:, :] if c == 0 else SQ[:, :], H[:, c, :], ACT.Square).then_inc(sq_done, 1)
                nc.scalar.activation(XH[:, c, :], H[:, c, :], ACT.Copy, scale=pcol(gain, c)).then_inc(x_hi, 1)

            def residual(name):
                j = rp_index[name]
                for g in range(2):
                    if name in first:
                        split_to(first[name] + count[name] // 2 * (g + 1) + RING)
                    for c in range(4 * g, 4 * g + 4):
                        act.wait_ge(h_upd, KT * j + c + 1)
                        if c >= 2:
                            act.wait_ge(acc_done, 7 * (j + 1) + c - 1)
                        norm_inputs(j + 1, c, gain_after[name])

            def rms(name, columns=False):
                n = norm_of[name]
                if name in first:
                    split_to(first[name] + RING)
                bank = STAT_BANK
                act.wait_ge(st_done, n + 1)
                nc.scalar.activation(LNT[:, :], ps[:, bank, :], ACT.Ln, bias=eps_c[:, 0:1]).then_inc(ln_done, 1)
                act.wait_ge(ln_done, 2 * n + 1)
                nc.scalar.activation(LNC[:, :], ps[:, bank + 1, 0:NCH], ACT.Ln, bias=eps_c[:, 0:1]).then_inc(ln_done, 1)
                nc.scalar.activation(R[:, :], LNT[:, :], ACT.Exp, scale=-0.5).then_inc(r_done, 1)
                act.wait_ge(ln_done, 2 * n + 2)
                nc.scalar.activation(RC[:, :], LNC[:, :], ACT.Exp, scale=-0.5).then_inc(r_done, 1)

            act.wait_ge(c_loaded, 32)
            act.wait_ge(pad_zero, 1)
            for c in range(KT):
                act.wait_ge(x_loaded[c // 2], 16)
                if c >= 2:
                    act.wait_ge(acc_done, c - 1)
                norm_inputs(0, c, "mix0")
                if c % 2:
                    split_to(c // 2 + 1)
            rms("in0")
            split_to(first["in0"] + count["in0"] + RING)

            for b in range(8):
                act.wait_ge(f1_done, b + 1)
                nc.scalar.activation(ZC[:, b * T:(b + 1) * T], ps[:, b, :], ACT.Copy).then_inc(f1_out, 1)
            for g in range(NA_H):
                act.wait_ge(f2_done, g + 1)
                nc.scalar.activation(YH[:, g, :], ps[:, g, :], ACT.Copy).then_inc(y0_hi, 1)

            def na_e(i):
                act.wait_ge(na_mn, i + 1)
                if i >= 2:
                    act.wait_ge(na_t, i - 1)
                nc.scalar.activation(PR[:, i % 2, :], S[:, i % 2, :], ACT.Exp, bias=sm[:, i:i + 1], scale=-1.0,
                                     accum_out=sm[:, 16 + i:17 + i]).then_inc(na_exp, 1)

            na_e(0)
            for i in range(16):
                if i + 1 < 16:
                    na_e(i + 1)
                h, t = i // 4, i % 4
                act.wait_ge(na_t, i + 1)
                if h >= 2:
                    act.wait_ge(na_pv, h - 1)
                nc.scalar.activation(PT[:, h % 2, :, t * P:(t + 1) * P],
                                     ps[:, 6 + i % 2, :].rearrange("p (k q) -> p k q", k=NCH),
                                     ACT.Copy).then_inc(na_pt, 1)
                if t == 3:
                    act.wait_ge(na_pv, h + 1)
                    nc.scalar.activation(YH[:, NA_H + h, :].rearrange("p (t q) -> p t q", q=P), backwards(ps[:, h, :]),
                                         ACT.Copy).then_inc(y0_hi, 1)

            def kv_evac(l):
                for g in range(2):
                    act.wait_ge(kv_used, 16 * l + 4 * g + 4)
                    b = 4 * g
                    nc.scalar.activation(KX[:, 4 * g:4 * g + 4, :], ps[:, b:b + 4, 0:NMEM], ACT.Copy).then_inc(kv_out, 1)
                for g in range(2):
                    act.wait_ge(kv_used, 16 * l + 8 + 4 * g + 4)
                    b = 4 * g
                    nc.scalar.activation(VX[:, :, g * T:(g + 1) * T], ps[:, b:b + 2, :], ACT.Copy).then_inc(kv_out, 1)

            def cross(l):
                def xe(h):
                    n = 4 * l + h
                    act.wait_ge(xa_nm, n + 1)
                    if h >= 2:
                        act.wait_ge(xa_t, n - 1)
                    for t in range(NCH):
                        b = 2 * (h % 2) + t // 2
                        nc.scalar.activation(PX[:, h % 2, t, :], ps[:, b, (t % 2) * NMEM:(t % 2 + 1) * NMEM],
                                             ACT.Exp, bias=sm[:, 48 + 4 * (h % 2) + t:49 + 4 * (h % 2) + t],
                                             scale=SCALE_X,
                                             accum_out=sm[:, 56 + 4 * (h % 2) + t:57 + 4 * (h % 2) + t]
                                             ).then_inc(xa_exp, 1)
                def out_hi(h):
                    act.wait_ge(xa_pv, 4 * l + h + 1)
                    b = 4 + 2 * (h % 2)
                    nc.scalar.activation(YH[:, 2 * h:2 * h + 2, :], ps[:, b:b + 2, :], ACT.Copy).then_inc(xa_hi, 1)

                xe(0)
                for h in range(XA_H):
                    n = 4 * l + h
                    if h + 1 < XA_H:
                        xe(h + 1)
                    act.wait_ge(xa_t, n + 1)
                    if h >= 2:
                        act.wait_ge(xa_pv, n - 1)
                    b = 4 + 2 * (h % 2)
                    nc.scalar.activation(PTX[:, h % 2, :, :], ps[:, b:b + 2, :], ACT.Copy).then_inc(xa_pt, 1)
                    if h >= 1:
                        out_hi(h - 1)
                out_hi(XA_H - 1)

            def ffn(l):
                name = f"up{l}"
                u0, ng = first[name], FF1 // 256
                nd = FD * ng * l

                def group(g, inner):
                    if inner:
                        for k in range(4):
                            u = g * 4 + (u0 + 4 + k)
                            act.wait_ge(w_used, g * 4 + (u0 + k + 1))
                            split(u, (u0 + k) % RING, g * 32 + (load_value[u0 + k] + 32))
                    for q in range(2):
                        act.wait_ge(ffn_dve, g * FD + (nd + 6 + q))
                        act_bar()
                        nc.scalar.activation(EG[:, q, :], CV[:, q, :], ACT.Gelu,
                                             bias=par[:, bass.ds(g * 2 + (PARAM_COLS[f"ffn_b{l}"][0] + q), 1)]
                                             ).then_inc(ffn_act, 1)
                    act.wait_ge(ffn_dve, g * FD + (nd + 9))
                    act_bar()
                    nc.scalar.activation(HID[:, bass.ds(g * 2, 2), :], HF[:, :, :], ACT.Copy).then_inc(ffn_act, 1)

                def act_bar():
                    act.wait_ge(c_loaded, 32)

                with act.Fori(0, ng - 1) as g:
                    group(g, True)
                state["split"] = u0 + 4 * ng
                split_to(u0 + 4 * ng + RING)
                group(ng - 1, False)

            def conv_mixer():
                u0 = first["in1"]
                for q in range(2):
                    for g in range(3):
                        split_to(u0 + 4 * (3 * q + g + 1) + RING)
                    act.wait_ge(cm_dve, 18 * q + 17)
                    nc.scalar.activation(YH[:, 4 * q:4 * q + 4, :], TY[:, :, :], ACT.Copy).then_inc(cm_act, 1)

            act.wait_ge(m_loaded, 16)
            nc.scalar.activation(MSQ[:, :, :], M[:, :, :], ACT.Square).then_inc(m_sq, 1)
            split_to(first["out0"] + count["out0"] // 2 + RING)
            act.wait_ge(m_st, 1)
            nc.scalar.activation(ML[:, :], ps[:, MEM_BANK, 0:NMEM], ACT.Ln, bias=eps_c[:, 0:1]).then_inc(m_ln, 1)
            act.wait_ge(m_ln, 1)
            nc.scalar.activation(MR[:, :], ML[:, :], ACT.Exp, scale=-0.5).then_inc(m_r, 1)
            residual("out0")
            for l in range(2):
                if l == 1 and "in1" in first:
                    rms("in1")
                    conv_mixer()
                    residual("out1")
                if f"q{l}" not in first:
                    break
                kv_evac(l)
                rms(f"q{l}")
                split_to(first[f"q{l}"] + count[f"q{l}"] + RING)
                cross(l)
                if f"wo{l}" not in first:
                    break
                residual(f"wo{l}")
                if f"up{l}" not in first:
                    break
                rms(f"up{l}")
                ffn(l)
                residual(f"down{l}")

            def retention():
                def decay(h):
                    if h >= 2:
                        act.wait_ge(ret_sc, 4 * (h - 1))
                    nc.scalar.activation(DEC[:, h % 2, :], AGE[:, :], ACT.Exp, scale=LOG_GAMMA[h]).then_inc(ret_dec, 1)
                act.wait_ge(t_loaded, 48)
                decay(0)
                decay(1)
                for h in range(RET_H):
                    act.wait_ge(ret_o, h + 1)
                    if h >= 1:
                        act.wait_ge(ret_v, h)
                    nc.scalar.activation(RSQ[:, :], ps[:, 6 + h % 2, :], ACT.Square).then_inc(ret_sq, 1)
                    if h + 2 < RET_H:
                        decay(h + 2)
                    act.wait_ge(ret_v, h + 1)
                    nc.scalar.activation(RLN[:, :], ps[:, 3 * (h % 2) + 1, :], ACT.Ln, scale=float(D) / P,
                                         bias=eps_c[:, 1:2]).then_inc(ret_ln, 1)
                    act.wait_ge(ret_ln, h + 1)
                    if h >= 1:
                        act.wait_ge(ret_ro, h)
                    nc.scalar.activation(RN[:, :], RLN[:, :], ACT.Exp, scale=-0.5).then_inc(ret_rn, 1)

            def decay_rows():
                B1, A1, A3, SPR, BEG, EGL, EG8 = [rows[i][:, :] for i in (0, 1, 2, 3, 4, 5, 6)]
                act.wait_ge(ab_dve, 1)
                nc.scalar.activation(BR[:, :], B1, ACT.Sigmoid).then_inc(ab_act, 1)
                act.wait_ge(ab_dve, 3)
                nc.scalar.activation(A3, A1, ACT.Abs).then_inc(ab_act, 1)
                act.wait_ge(ab_act, 2)
                nc.scalar.activation(A3, A3, ACT.Exp, scale=-1.0).then_inc(ab_act, 1)
                act.wait_ge(ab_act, 3)
                nc.scalar.activation(A3, A3, ACT.Ln, bias=1.0).then_inc(ab_act, 1)
                nc.scalar.activation(sm[0:DN_H, 80:81], pcol("a_log")[0:DN_H, :], ACT.Exp).then_inc(ab_act, 1)
                act.wait_ge(ab_dve, 9)
                nc.scalar.activation(EG8, GR[:, :], ACT.Exp).then_inc(ab_act, 1)
                act.wait_ge(ab_dve, 14)
                nc.scalar.activation(EGL, EGL, ACT.Exp).then_inc(ab_act, 1)
                act.wait_ge(ab_t, 1)
                nc.scalar.activation(TC[:, :, :, :], ps[:, 1, 0:4 * NCH * DN_H].rearrange("p (a n h) -> p a n h", a=4, n=NCH),
                                     ACT.Copy).then_inc(ab_act, 1)

            def delta(q):
                u0 = first[f"dvqk{q}"]

                def silu(i, x):
                    act.wait_ge(dq_dve, 51 * q + 17 * i + 17)
                    nc.scalar.activation(x[:, :, :], x[:, :, :], ACT.Silu).then_inc(dq_act, 1)

                def square(i, x, sq):
                    act.wait_ge(dq_act, 3 * q + i + 2)
                    nc.scalar.activation(sq[:, :, :], x[:, :, :], ACT.Square).then_inc(l2_sq, 1)

                def inverse_norm(i, ln):
                    b = 0 if q == 0 else 4
                    act.wait_ge(l2_st, 2 * q + i + 1)
                    nc.scalar.activation(ln[:, :, :], ps[:, b:b + 4, :], ACT.Ln, scale=float(D),
                                         bias=eps_c[:, 0:1]).then_inc(l2_ln, 1)
                    act.wait_ge(l2_ln, 2 * q + i + 1)
                    nc.scalar.activation(ln[:, :, :], ln[:, :, :], ACT.Exp, scale=-0.5).then_inc(l2_r, 1)

                split_to(u0 + 4 + RING)
                silu(0, VB)
                split_to(u0 + 8 + RING)
                silu(1, QN)
                square(0, QN, SQq)
                split_to(u0 + 12 + RING)
                inverse_norm(0, LNq)
                silu(2, KN)
                square(1, KN, SQk)
                split_to(u0 + 16 + RING)
                inverse_norm(1, LNk)
                for pr in range(2):
                    m = 4 * q + 2 * pr
                    n = 24 * (2 * q + pr)
                    for p in range(2):
                        act.wait_ge(dp_bc, m + p + 1)
                        nc.scalar.activation(EGA[p][:, :], ps[:, 4 * p, :], ACT.Exp).then_inc(dp_eg, 1)
                        act.wait_ge(dp_dve, n + pair_step(p, 3))
                        nc.scalar.activation(DL[:, p, :], DL[:, p, :], ACT.Exp).then_inc(dp_lt, 1)
                for n in range(NCH):
                    for hh in range(4):
                        act.wait_ge(sc_vn, 16 * q + 4 * n + hh + 1)
                        nc.scalar.activation(VS[:, hh, :], ps[:, hh, P:2 * P], ACT.Copy).then_inc(sc_vc, 1)
                act.wait_ge(sc_o, q + 1)
                nc.scalar.activation(SQo[:, :, :], ps[:, 4:8, :], ACT.Square).then_inc(do_sq, 1)
                nc.scalar.activation(DO[:, 4 * q:4 * q + 4, :], ps[:, 4:8, :], ACT.Copy).then_inc(do_sq, 1)
                act.wait_ge(do_st, q + 1)
                nc.scalar.activation(LNo[:, :, :], ps[:, 4:8, :], ACT.Ln, scale=float(D) / P,
                                     bias=eps_c[:, 0:1]).then_inc(do_ln, 1)
                act.wait_ge(do_ln, q + 1)
                nc.scalar.activation(LNo[:, :, :], LNo[:, :, :], ACT.Exp, scale=-0.5).then_inc(do_r, 1)

            def ffn2():
                u0, ng = first["up2"], FF2 // 256

                def group(g, inner):
                    if inner:
                        for k in range(4):
                            act.wait_ge(w_used, g * 4 + (u0 + k + 1))
                            split(g * 4 + (u0 + 4 + k), (u0 + k) % RING, g * 32 + (load_value[u0 + k] + 32))
                    act.wait_ge(up2_dve, g * FD2 + 11)
                    nc.scalar.activation(SA[:, :, :], CV4[:, 0:2, :], ACT.Silu).then_inc(up2_act, 1)
                    act.wait_ge(up2_dve, g * FD2 + 14)
                    act.wait_ge(c_loaded, 32)
                    nc.scalar.activation(HID[:, bass.ds(g * 2, 2), :], HF2[:, :, :], ACT.Copy).then_inc(up2_act, 1)

                with act.Fori(0, ng - 1) as g:
                    group(g, True)
                state["split"] = u0 + 4 * ng
                split_to(u0 + 4 * ng + RING)
                group(ng - 1, False)

            def block2():
                rms("bnorm")
                residual("bnorm")
                rms("rqk")
                split_to(first["rv"] + count["rv"] + RING)
                retention()
                for g in range(2):
                    split_to(first["rgate"] + 4 * (g + 1) + RING)
                    act.wait_ge(rg_dve, 3 * g + 1)
                    nc.scalar.activation(SG[:, :, :], TG[:, :, :], ACT.Silu).then_inc(rg_act, 1)
                    act.wait_ge(rg_dve, 3 * g + 2)
                    nc.scalar.activation(YH[:, 4 * g:4 * g + 4, :], TG[:, :, :], ACT.Copy).then_inc(rg_act, 1)
                for g in range(2):
                    split_to(first["gater"] + 4 * (g + 1) + RING)
                    act.wait_ge(gr_dve, g + 1)
                    nc.scalar.activation(MG[:, 4 * g:4 * g + 4, :], MG[:, 4 * g:4 * g + 4, :],
                                         ACT.Sigmoid).then_inc(gr_act, 1)
                split_to(first["dab"] + 1 + RING)
                decay_rows()
                delta(0)
                delta(1)
                for g in range(2):
                    act.wait_ge(ga_dve, g + 1)
                    nc.scalar.activation(SGD[:, 4 * g:4 * g + 4, :], SGD[:, 4 * g:4 * g + 4, :],
                                         ACT.Sigmoid).then_inc(ga_act, 1)
                for g in range(2):
                    split_to(first["dz"] + 4 * (g + 1) + RING)
                    act.wait_ge(dz_dve, 2 * g + 1)
                    nc.scalar.activation(TZ[:, :, :], TZ[:, :, :], ACT.Silu).then_inc(dz_act, 1)
                for g in range(2):
                    act.wait_ge(dz_dve, 4)
                    nc.scalar.activation(XH[:, 4 * g:4 * g + 4, :], DO[:, 4 * g:4 * g + 4, :], ACT.Copy).then_inc(dz_act, 1)
                for g in range(2):
                    split_to(first["dnbr"] + 4 * (g + 1) + RING)
                    act.wait_ge(dn_dve, 3 * g + 2)
                    nc.scalar.activation(YH[:, 4 * g:4 * g + 4, :], MG[:, 4 * g:4 * g + 4, :], ACT.Copy).then_inc(dn_act, 1)
                residual("wo2")
                rms("up2")
                ffn2()
                residual("down2")
                rms("final")

            if two:
                block2()

        @block.tensor
        def _(pe):
            def products(u, slot, k, bank, x_hi_t, x_lo_t, tokens_out, start, stop):
                pe.wait_ge(lo_done, u + 1)
                for m in range(4):
                    for j in range(2):
                        kt = 2 * k + j
                        for n in range(3):
                            wt = w_lo[:, slot % LO_RING, j, :] if n == 2 else w_hi[:, slot, j, :]
                            xt = x_lo_t[:, kt, :] if n == 1 else x_hi_t[:, kt, :]
                            if tokens_out:
                                a, b = xt[:, m * P:(m + 1) * P], wt
                            else:
                                a, b = wt[:, m * P:(m + 1) * P], xt
                            mm = nc.tensor.matmul(ps[:, bank + m, :], a, b, start=start and j == 0 and n == 0,
                                                  stop=stop and j == 1 and n == 2)
                mm.then_inc(w_used, 1)

            def group(u0, units, bank, xh, xl, ready=None, tokens_out=False, after=None):
                for k in range(units):
                    if ready is not None:
                        for kt in (2 * k, 2 * k + 1):
                            for s, v in ready(kt):
                                pe.wait_ge(s, v)
                    products(u0 + k, (u0 + k) % RING, k, bank, xh, xl, tokens_out, k == 0, k == units - 1)
                    if after is not None and k == 2:
                        after()

            def stats(name):
                n = norm_of[name]

                def emit():
                    pe.wait_ge(acc_done, 7 * (n + 1))
                    nc.tensor.matmul(ps[:, STAT_BANK, :], ones, ACC[:, :], start=True, stop=True)
                    for t in range(NCH):
                        mm = nc.tensor.matmul(ps[:, STAT_BANK + 1, t:t + 1], ACC[:, t * P:(t + 1) * P], ones[:, 0:1],
                                              start=True, stop=True)
                    mm.then_inc(st_done, 1)
                return emit

            def x_ready(name):
                before = {"up0": "wo0", "up1": "wo1", "up2": "wo2", "in1": "down0"}.get(name)
                first_half = [(h_upd, KT * rp_index[before] + 4)] if before else []
                return lambda kt: (first_half if kt == 0 else []) + [(x_lo, KT * norm_of[name] + kt + 1)]

            def stat_read(name):
                pe.wait_ge(ln_done, 2 * norm_of[name] + 2)

            pe.wait_ge(c_loaded, 32)
            u0 = first["in0"]
            group(u0, 4, 0, XH, XL, x_ready("in0"), after=stats("in0"))
            stat_read("in0")
            group(u0 + 4, 4, 4, XH, XL)
            pe.wait_ge(in0_z, 1)
            group(u0 + 8, 4, 0, XH, XL)
            pe.wait_ge(in0_z, 2)
            group(u0 + 12, 4, 4, XH, XL, tokens_out=True)
            pe.wait_ge(f_loaded, 32)
            pe.wait_ge(in0_z, 7)
            for g in range(NA_H):
                for t in range(NCH):
                    i = g * NCH + t
                    mm = nc.tensor.matmul(ps[:, i // 2, (i % 2) * 256:(i % 2 + 1) * 256],
                                          Z[:, g, t * P:(t + 1) * P], GC[:, :], start=True, stop=True)
                    if i % 2:
                        mm.then_inc(f1_done, 1)
            for g in range(NA_H):
                pe.wait_ge(f1_out, 2 * g + 2)
                for t in range(NCH):
                    for cs in range(2):
                        a = ((g * NCH + t) * 2 + cs) * P
                        mm = nc.tensor.matmul(ps[:, g, :], ZC[:, a:a + P], FC[:, t, cs, :],
                                              start=t == 0 and cs == 0, stop=t == NCH - 1 and cs == 1)
                mm.then_inc(f2_done, 1)

            def scores(i):
                h, t = i // 4, i % 4
                if i >= 2:
                    pe.wait_ge(na_add, i - 1)
                nc.tensor.matmul(ps[:, 4 + i % 2, :], Q[:, h, t * P:(t + 1) * P], K[:, h, :],
                                 start=True, stop=True).then_inc(na_s, 1)

            pe.wait_ge(f1_out, 8)
            scores(0)
            scores(1)
            for i in range(16):
                h = i // 4
                if i + 2 < 16:
                    scores(i + 2)
                pe.wait_ge(na_p, i + 1)
                if i >= 2:
                    pe.wait_ge(na_pt, i - 1)
                for k in range(NCH):
                    mm = nc.tensor.transpose(ps[:, 6 + i % 2, k * P:(k + 1) * P], PR[:, i % 2, k * P:(k + 1) * P], ident)
                mm.then_inc(na_t, 1)
                if i % 4 == 3:
                    pe.wait_ge(na_pt, i + 1)
                    pe.wait_ge(y0_lo, h + 1)
                    for k in range(NCH):
                        mm = nc.tensor.matmul(ps[:, h, :], V[:, k, h * P:(h + 1) * P], PT[:, h % 2, k, :],
                                              start=k == 0, stop=k == NCH - 1)
                    mm.then_inc(na_pv, 1)

            def residual(name, units, xh, xl, ready, between=None):
                u = first[name]
                group(u, units, 0, xh, xl, ready)
                if between is not None:
                    between()
                group(u + units, units, 4, xh, xl)

            def mem_stat():
                pe.wait_ge(m_acc, 1)
                nc.tensor.matmul(ps[:, MEM_BANK, 0:NMEM], ones, MACC[:, :], start=True, stop=True).then_inc(m_st, 1)
                pe.wait_ge(m_ln, 1)

            def kv(l):
                u0 = first[f"q{l}"] + RING
                rp = KT * (rp_index[f"out{l}"] + 1)
                pe.wait_ge(m_done, 1)
                for i in range(16):
                    g, k, s = i // 4, i % 4, i % RING
                    if i == 0:
                        pe.wait_ge(h_upd, rp - 4)
                    elif i == 4:
                        pe.wait_ge(h_upd, rp)
                    elif k == 0:
                        pe.wait_ge(kv_out, 4 * l + g - 1)
                    pe.wait_ge(w_loaded[s], kv_value[l, i])
                    for m in range(4 if g < 2 else 2):
                        for j in range(2):
                            kt = 2 * k + j
                            if g < 2:
                                mm = nc.tensor.matmul(ps[:, 4 * g + m, 0:NMEM], w_raw[:, s, j, m * P:(m + 1) * P],
                                                      M[:, kt, :], start=kt == 0, stop=kt == KT - 1)
                            else:
                                mm = nc.tensor.matmul(ps[:, 4 * (g - 2) + m, :], M[:, kt, m * P:(m + 1) * P],
                                                      w_raw[:, s, j, :], start=kt == 0, stop=kt == KT - 1)
                    mm.then_inc(kv_used, 1)

            def cross(l):
                def xs(h):
                    n = 4 * l + h
                    if h >= 2:
                        pe.wait_ge(xa_exp, 4 * (n - 1))
                    for t in range(NCH):
                        for c in range(2):
                            mm = nc.tensor.matmul(ps[:, 2 * (h % 2) + t // 2, (t % 2) * NMEM:(t % 2 + 1) * NMEM],
                                                  QX[:, 2 * h + c, t * P:(t + 1) * P], KX[:, 2 * h + c, :],
                                                  start=c == 0, stop=c == 1)
                    mm.then_inc(xa_s, 1)

                def xt(h):
                    n = 4 * l + h
                    pe.wait_ge(xa_p, n + 1)
                    if h >= 2:
                        pe.wait_ge(xa_lo, n - 1)
                    for k in range(2):
                        for t in range(NCH):
                            mm = nc.tensor.transpose(ps[:, 4 + 2 * (h % 2) + k, t * P:(t + 1) * P],
                                                     PX[:, h % 2, t, k * P:(k + 1) * P], ident)
                    mm.then_inc(xa_t, 1)

                def xv(h):
                    n = 4 * l + h
                    pe.wait_ge(xa_pt, n + 1)
                    for c in range(2):
                        for k in range(2):
                            a = h * 2 * P + c * P
                            mm = nc.tensor.matmul(ps[:, 4 + 2 * (h % 2) + c, :], VX[:, k, a:a + P], PTX[:, h % 2, k, :],
                                                  start=k == 0, stop=k == 1)
                    mm.then_inc(xa_pv, 1)

                pe.wait_ge(kv_out, 4 * l + 4)
                pe.wait_ge(q_out, 2 * l + 2)
                xs(0)
                xs(1)
                for h in range(XA_H):
                    if h + 2 < XA_H:
                        xs(h + 2)
                    xt(h)
                    if h >= 1:
                        xv(h - 1)
                xv(XA_H - 1)

            def ffn(l):
                name = f"up{l}"
                u0, ng = first[name], FF1 // 256
                nd = FD * ng * l
                group(u0, 4, 0, XH, XL, x_ready(name), after=stats(name))
                stat_read(name)
                group(u0 + 4, 4, 4, XH, XL)
                with pe.Fori(1, ng // 2) as i:
                    for g in range(2):
                        pe.wait_ge(ffn_dve, i * (2 * FD) + (nd + FD * (g - 2) + 8))
                        for k in range(4):
                            products(i * 8 + (u0 + 4 * g + k), k, k, 4 * g, XH, XL, False, k == 0, k == 3)
                u0 = first[f"down{l}"]
                nf = FF1 // P
                pe.wait_ge(ffn_dve, nd + FD * (ng - 2) + 8)
                group(u0, nf // 2, 0, HID[:, 0:nf, :], HID[:, nf:2 * nf, :],
                      lambda kt: [(ffn_dve, nd + FD * (kt // 2 + 1))])
                group(u0 + nf // 2, nf // 2, 4, HID[:, 0:nf, :], HID[:, nf:2 * nf, :])

            for l in range(2):
                if l == 0:
                    pe.wait_ge(na_pt, 16)
                    residual("out0", 4, YH, YL, lambda kt: [(y0_lo, 8)], between=mem_stat)
                else:
                    if "in1" not in first:
                        break
                    u0 = first["in1"]
                    for g in range(6):
                        if g == 0:
                            group(u0, 4, 0, XH, XL, x_ready("in1"), after=stats("in1"))
                            stat_read("in1")
                        else:
                            if g >= 2:
                                pe.wait_ge(cm_dve, 18 * ((g - 2) // 3) + (1, 2, 16)[(g - 2) % 3])
                            group(u0 + 4 * g, 4, 4 * (g % 2), XH, XL)
                    pe.wait_ge(cm_dve, 18 + 16)
                    residual("out1", 4, YH, YL, lambda kt: [(cm_dve, 18 * (kt // 4) + 18)])
                if f"q{l}" not in first:
                    break
                kv(l)
                pe.wait_ge(kv_out, 4 * l + 4)
                u0 = first[f"q{l}"]
                group(u0, 4, 0, XH, XL, x_ready(f"q{l}"), after=stats(f"q{l}"))
                stat_read(f"q{l}")
                group(u0 + 4, 4, 4, XH, XL)
                cross(l)
                if f"wo{l}" not in first:
                    break
                residual(f"wo{l}", 4, YH, YL, lambda kt: [(xa_lo, 4 * l + 4)])
                if f"up{l}" not in first:
                    break
                ffn(l)

            def retention():
                pe.wait_ge(rv_out, 11)
                for b, x in enumerate((RQ, RK)):
                    pe.wait_ge(rqk_out, b + 1)
                    for c in range(4):
                        mm = nc.tensor.matmul(ps[:, 4 * b + c, :], cst[:, CONSTS["rot"], :], x[:, c, :],
                                              start=True, stop=True)
                    mm.then_inc(rot_done, 1)

                def s(h):
                    c, r = h // 2, (h % 2) * 64
                    if h >= 2:
                        pe.wait_ge(ret_ln, h - 1)
                    for j in range(NCH):
                        w = T - j * P
                        b, o = ((0, 0), (1, 0), (2, 0), (2, 256))[j]
                        mm = nc.tensor.matmul(ps[:, 3 * (h % 2) + b, o:o + w], RK[r:r + 64, c, j * P:(j + 1) * P],
                                              RQ[r:r + 64, c, j * P:T], start=True, stop=True)
                        if j != 2:
                            mm.then_inc(ret_s, 1)

                def o(h):
                    pe.wait_ge(rv_out, 14)
                    if h >= 2:
                        pe.wait_ge(ret_ro, h - 1)
                    for j in range(NCH):
                        w = T - j * P
                        a = (0, 512, 896, 1152)[j]
                        pe.wait_ge(ret_sc, 4 * h + j + 1)
                        mm = nc.tensor.matmul(ps[:, 6 + h % 2, j * P:T], RV[:, j, h * P:(h + 1) * P],
                                              SCO[:, h % 2, a:a + w], start=j == 0, stop=j == NCH - 1)
                    mm.then_inc(ret_o, 1)

                def v(h):
                    pe.wait_ge(ret_sq, h + 1)
                    nc.tensor.matmul(ps[:, 3 * (h % 2) + 1, :], ones, RSQ[:, :], start=True, stop=True).then_inc(ret_v, 1)

                pe.wait_ge(rot_out, 6)
                s(0)
                s(1)
                for h in range(RET_H):
                    if h >= 1:
                        v(h - 1)
                    o(h)
                    if 1 <= h < RET_H - 1:
                        s(h + 1)
                v(RET_H - 1)

            def delta(q):
                u0 = first[f"dvqk{q}"]
                bv, bq = (4, 0) if q == 0 else (0, 4)
                if q == 0:
                    pe.wait_ge(rb_dve, 2)
                group(u0, 4, bv, XH, XL, after=decay_columns if q == 0 else out_stats(0))
                if q == 0:
                    pe.wait_ge(ab_act, 8)
                else:
                    pe.wait_ge(do_ln, 1)
                group(u0 + 4, 4, bq, XH, XL)
                pe.wait_ge(dq_dve, 51 * q + 1)
                group(u0 + 8, 4, bv, XH, XL)

                def l2(i, sq):
                    pe.wait_ge(l2_sq, 2 * q + i + 1)
                    for c in range(4):
                        mm = nc.tensor.matmul(ps[:, bq + c, :], ones, sq[:, c, :], start=True, stop=True)
                    mm.then_inc(l2_st, 1)

                pe.wait_ge(dq_dve, 51 * q + 18)
                l2(0, SQq)
                pe.wait_ge(dq_dve, 51 * q + 35)
                group(first[f"gated{q}"], 4, bv, XH, XL)
                pe.wait_ge(l2_ln, 2 * q + 1)
                l2(1, SQk)
                pe.wait_ge(ga_dve, q + 1)
                pe.wait_ge(l2_n, 2 * q + 2)
                pe.wait_ge(dq_act, 3 * q + 3)
                for pr in range(2):
                    m = 4 * q + 2 * pr
                    nd = 24 * (2 * q + pr)
                    nl = 34 * (2 * q + pr)
                    for p in range(2):
                        h, hh = m + p, 2 * pr + p
                        if pr == 1:
                            pe.wait_ge(lv_dve, nl)
                        pick = ident[0:DN_H, h:h + 1].broadcast_to([DN_H, P])
                        nc.tensor.matmul(ps[:, 4 * p, :], pick, GR[:, :], start=True, stop=True)
                        nc.tensor.matmul(ps[:, 4 * p + 1, :], pick, BR[:, :], start=True, stop=True).then_inc(dp_bc, 1)
                        for n in range(NCH):
                            nc.tensor.transpose(ps[:, 4 * p + 2, n * P:(n + 1) * P], KN[:, hh, n * P:(n + 1) * P], ident)
                            mm = nc.tensor.transpose(ps[:, 4 * p + 3, n * P:(n + 1) * P], VB[:, hh, n * P:(n + 1) * P], ident)
                        mm.then_inc(dp_tr, 1)
                    for p in range(2):
                        hh = 2 * pr + p
                        pe.wait_ge(dp_dve, nd + pair_step(p, 2))
                        pe.wait_ge(dp_eg, m + p + 1)
                        for n in range(NCH):
                            cols_ = slice(n * P, (n + 1) * P)
                            nc.tensor.matmul(ps[:, 4 * p + 1, cols_], KN[:, hh, cols_], T1[:, p, cols_], start=True, stop=True)
                            mm = nc.tensor.matmul(ps[:, 4 * p, cols_], KN[:, hh, cols_], QN[:, hh, cols_], start=True, stop=True)
                        mm.then_inc(dp_a, 1)
                    for li, b in enumerate(LEVELS[1:]):
                        for p in range(2):
                            if li == 0:
                                pe.wait_ge(dp_dve, nd + pair_step(p, 10))
                            else:
                                pe.wait_ge(lv_dve, nl + 6 * (li - 1) + 4 + 2 * p)
                            for n in range(NCH):
                                cols_ = slice(n * P, (n + 1) * P)
                                mm = nc.tensor.matmul(ps[:, 4 * p + 2, cols_], AT[:, p, cols_], MM[:, p, cols_],
                                                      start=True, stop=True)
                            mm.then_inc(lv_pe, 1)
                        for p in range(2):
                            hh = 2 * pr + p
                            pe.wait_ge(lv_dve, nl + 6 * li + p + 1)
                            for n in range(NCH):
                                cols_ = slice(n * P, (n + 1) * P)
                                if b == 32:
                                    nc.tensor.matmul(ps[:, 4 * p + 1, cols_], MT[:, hh, cols_], T1[:, p, cols_],
                                                     start=True, stop=True)
                                mm = nc.tensor.matmul(ps[:, 4 * p + 3, cols_], T1[:, p, cols_], MT[:, hh, cols_],
                                                      start=True, stop=True)
                            mm.then_inc(lv_pe, 1)
                pe.wait_ge(lv_dve, 34 * (2 * q + 2))
                pe.wait_ge(dp_dve, 24 * (2 * q + 2))
                for n in range(NCH):
                    cols_ = slice(n * P, (n + 1) * P)
                    if n:
                        for hh in range(4):
                            pe.wait_ge(sc_s, 12 * q + 4 * (n - 1) + hh + 1)
                            nc.tensor.matmul(ps[:, hh, 0:P], KN[:, hh, cols_], SS[:, hh, :],
                                             start=True, stop=True).then_inc(sc_ks, 1)
                    for hh in range(4):
                        if n:
                            pe.wait_ge(sc_y, 12 * q + 4 * (n - 1) + hh + 1)
                            pe.wait_ge(sc_vc, 16 * q + 4 * (n - 1) + hh + 1)
                        nc.tensor.matmul(ps[:, hh, P:2 * P], MT[:, hh, cols_],
                                         YS[:, hh, :] if n else VB[:, hh, cols_], start=True, stop=True).then_inc(sc_vn, 1)
                    for hh in range(4):
                        pe.wait_ge(sc_vc, 16 * q + 4 * n + hh + 1)
                        if n:
                            nc.tensor.matmul(ps[:, 4 + hh, cols_], SS[:, hh, :], QN[:, hh, cols_], start=True, stop=False)
                        mm = nc.tensor.matmul(ps[:, 4 + hh, cols_], VS[:, hh, :], ATT[:, hh, cols_], start=n == 0, stop=True)
                        if n < NCH - 1:
                            nc.tensor.matmul(ps[:, hh, 2 * P:3 * P], KD[:, hh, cols_], VS[:, hh, :],
                                             start=True, stop=True).then_inc(sc_su, 1)
                mm.then_inc(sc_o, 1)

            def out_stats(q):
                def emit():
                    pe.wait_ge(do_sq, 2 * q + 2)
                    for c in range(4):
                        mm = nc.tensor.matmul(ps[:, 4 + c, :], ones, SQo[:, c, :], start=True, stop=True)
                    mm.then_inc(do_st, 1)
                return emit

            def decay_columns():
                pe.wait_ge(ab_act, 7)
                pe.wait_ge(ab_dve, 14)
                for a, row in enumerate((BR, GR, rows[4], rows[5])):
                    for n in range(NCH):
                        o = (a * NCH + n) * DN_H
                        mm = nc.tensor.transpose(ps[:, 1, o:o + DN_H], row[:, n * P:(n + 1) * P], ident[0:DN_H, 0:DN_H])
                mm.then_inc(ab_t, 1)

            def ffn2():
                u0, ng = first["up2"], FF2 // 256
                group(u0, 4, 0, XH, XL, x_ready("up2"), after=stats("up2"))
                stat_read("up2")
                group(u0 + 4, 4, 4, XH, XL)
                with pe.Fori(1, ng // 2) as i:
                    for g in range(2):
                        pe.wait_ge(up2_dve, i * (2 * FD2) + (FD2 * (g - 2) + 1))
                        for k in range(4):
                            products(i * 8 + (u0 + 4 * g + k), (u0 + k) % RING, k, 4 * g, XH, XL, False, k == 0, k == 3)
                pe.wait_ge(up2_dve, FD2 * (ng - 3) + 1)
                group(u0 + 4 * (ng - 1), 4, 0, XH, XL)
                u0 = first["down2"]
                nf = FF2 // P
                pe.wait_ge(up2_dve, FD2 * (ng - 2) + 1)
                ready = lambda kt: [(up2_dve, FD2 * (kt // 2 + 1))]
                group(u0, nf // 2, 4, HID[:, 0:nf, :], HID[:, nf:2 * nf, :], ready)
                group(u0 + nf // 2, nf // 2, 0, HID[:, 0:nf, :], HID[:, nf:2 * nf, :])

            def pair(name, freed, xh=XH, xl=XL, ready=None, after=None):
                for g in range(2):
                    for s, v in freed[g]:
                        pe.wait_ge(s, v)
                    group(first[name] + 4 * g, 4, 4 * g, xh, xl, ready, after=after if g == 0 else None)

            def block2():
                stats("bnorm")()
                pe.wait_ge(h_upd, KT * rp_index["bnorm"])
                u0 = first["rqk"]
                group(u0, 4, 0, XH, XL, x_ready("rqk"), after=stats("rqk"))
                stat_read("rqk")
                group(u0 + 4, 4, 4, XH, XL)
                for g in range(2):
                    pe.wait_ge(rqk_out, g + 1)
                    group(first["rv"] + 4 * g, 4, 4 * g, XH, XL, tokens_out=True)
                retention()
                pair("rgate", [[(ret_ln, 8)], [(ret_ro, 8)]])
                pair("gater", [[(rg_dve, 1)], [(rg_dve, 4)]])
                pair("retbr", [[(gr_dve, 1)], [(gr_dve, 2)]], YH, YL, lambda kt: [(rg_dve, 3 * (kt // 4) + 3)])
                u = first["dab"]
                pe.wait_ge(lo_done, u + 1)
                pe.wait_ge(rb_dve, 1)
                hi = w_hi[:, u % RING, :, :].rearrange("p a (b c) -> p (a b) c", c=P)
                lo = w_lo[:, u % RING, :, :].rearrange("p a (b c) -> p (a b) c", c=P)
                for kt in range(KT):
                    for n, (a, b) in enumerate(((hi, XH), (hi, XL), (lo, XH))):
                        mm = nc.tensor.matmul(ps[:, 0, :], a[:, kt, :], b[:, kt, :], start=kt == 0 and n == 0,
                                              stop=kt == KT - 1 and n == 2)
                mm.then_inc(w_used, 1)
                delta(0)
                delta(1)
                pair("dz", [[], [(do_ln, 2)]], after=out_stats(1))
                pair("dnbr", [[(dz_dve, 1)], [(dz_dve, 3)]], ready=lambda kt: [(dz_dve, 5 + kt // 4)])
                pair("wo2", [[(dn_dve, 1)], [(dn_dve, 4)]], YH, YL, lambda kt: [(dn_dve, 3 * (kt // 4) + 3)])
                ffn2()
                stats("final")()

            if two:
                block2()

        @block.vector
        def _(dve):
            def over(ap, n):
                return ap.unsqueeze(1).broadcast_to([P, n, ap.shape[-1]])

            def add_square(j, c):
                dve.wait_ge(sq_done, KT * j + c + 1)
                if c >= 2:
                    dve.wait_ge(acc_done, 7 * j + c - 1)
                nc.vector.tensor_tensor(ACC[:, :], ACC[:, :], SQ[:, :], ALU.add).then_inc(acc_done, 1)

            def norm_inputs(j, c, gain):
                if c >= 1:
                    add_square(j, c)
                dve.wait_ge(x_hi, KT * j + c + 1)
                nc.vector.scalar_tensor_tensor(out=XL[:, c, :], in0=H[:, c, :], scalar=pcol(gain, c),
                                               in1=XH[:, c, :].bitcast(F32), op0=ALU.mult,
                                               op1=ALU.subtract).then_inc(x_lo, 1)

            def residual(name, flip=0):
                j = rp_index[name]
                for g in range(2):
                    if name in first:
                        dve.wait_ge(w_used, first[name] + count[name] // 2 * (g + 1))
                    for c in range(4 * g, 4 * g + 4):
                        if name in first:
                            nc.vector.tensor_tensor(H[:, c, :], ps[:, (c + flip) % 8, :], H[:, c, :],
                                                    ALU.add).then_inc(h_upd, 1)
                        else:
                            nc.vector.scalar_tensor_tensor(out=H[:, c, :], in0=H[:, c, :], scalar=pcol("final1", c),
                                                           in1=R[:, :], op0=ALU.mult, op1=ALU.mult).then_inc(h_upd, 1)
                        if c > 4 * g:
                            norm_inputs(j + 1, c - 1, gain_after[name])
                    norm_inputs(j + 1, 4 * g + 3, gain_after[name])

            dve.wait_ge(c_loaded, 32)
            for c in range(KT):
                dve.wait_ge(x_loaded[c // 2], 16)
                norm_inputs(0, c, "mix0")
            u0 = first["in0"]
            dve.wait_ge(r_done, 2)
            for g, dst in enumerate((Z, Q, K)):
                dve.wait_ge(w_used, u0 + 4 * g + 4)
                b = 4 * (g % 2)
                if dst is not Q:
                    nc.vector.tensor_tensor(dst[:, :, :], ps[:, b:b + 4, :], over(R[:, :], 4), ALU.mult).then_inc(in0_z, 1)
                    continue
                for h in range(NA_H):
                    q_done = nc.vector.tensor_tensor(backwards(Q[:, h, :]), ps[:, b + h, :].rearrange("p (t q) -> p t q", q=P),
                                                     R[:, :].rearrange("p (t q) -> p t q", q=P), ALU.mult)
                q_done.then_inc(in0_z, 1)
            dve.wait_ge(w_used, u0 + 16)
            for t in range(NCH):
                nc.vector.tensor_scalar(V[:, t, :], ps[:, 4 + t, :], RC[:, t:t + 1], None, ALU.mult).then_inc(in0_z, 1)
            for g in range(NA_H):
                dve.wait_ge(y0_hi, g + 1)
                nc.vector.tensor_tensor(YL[:, g, :], ps[:, g, :], YH[:, g, :].bitcast(F32),
                                        ALU.subtract).then_inc(y0_lo, 1)

            def na_a(i):
                h, t = i // 4, i % 4
                dve.wait_ge(na_s, i + 1)
                if i >= 2:
                    dve.wait_ge(na_exp, i - 1)
                s0 = NA_KH - 2 - 2 * t
                nc.vector.scalar_tensor_tensor(out=S[:, i % 2, :], in0=ps[:, 4 + i % 2, :], scalar=-SCALE_NA,
                                               in1=B2[:, h, s0:s0 + ROWS, :].rearrange("p r c -> p (r c)"),
                                               op0=ALU.mult, op1=ALU.subtract).then_inc(na_add, 1)
                dve.wait_ge(na_add, i + 1)
                nc.vector.tensor_reduce(sm[:, i:i + 1], S[:, i % 2, :], AX.X, ALU.min).then_inc(na_mn, 1)

            dve.wait_ge(b2_sel, 4)
            na_a(0)
            for i in range(16):
                if i + 1 < 16:
                    na_a(i + 1)
                dve.wait_ge(na_exp, i + 1)
                nc.vector.reciprocal(sm[:, 32 + i:33 + i], sm[:, 16 + i:17 + i]).then_inc(na_rr, 1)
                dve.wait_ge(na_rr, i + 1)
                nc.vector.tensor_scalar(PR[:, i % 2, :], PR[:, i % 2, :], sm[:, 32 + i:33 + i], None,
                                        ALU.mult).then_inc(na_p, 1)
                if i % 4 == 3:
                    h = i // 4
                    dve.wait_ge(y0_hi, NA_H + h + 1)
                    nc.vector.tensor_tensor(YL[:, NA_H + h, :].rearrange("p (t q) -> p t q", q=P), backwards(ps[:, h, :]),
                                            YH[:, NA_H + h, :].bitcast(F32).rearrange("p (t q) -> p t q", q=P),
                                            ALU.subtract).then_inc(y0_lo, 1)
            dve.wait_ge(m_sq, 1)
            nc.vector.tensor_reduce(MACC[:, :], MSQ[:, :, :].rearrange("p k t -> p t k"), AX.X, ALU.add).then_inc(m_acc, 1)
            dve.wait_ge(m_r, 1)
            for k in range(KT):
                mm = nc.vector.scalar_tensor_tensor(out=M[:, k, :], in0=M[:, k, :], scalar=pcol("mem", k),
                                                    in1=MR[:, :], op0=ALU.mult, op1=ALU.mult)
            mm.then_inc(m_done, 1)

            def cross(l):
                u0 = first[f"q{l}"]
                for g in range(2):
                    dve.wait_ge(r_done, 2 * norm_of[f"q{l}"] + 2)
                    dve.wait_ge(w_used, u0 + 4 * g + 4)
                    nc.vector.tensor_tensor(QX[:, 4 * g:4 * g + 4, :], ps[:, 4 * g:4 * g + 4, :], over(R[:, :], 4),
                                            ALU.mult).then_inc(q_out, 1)

                def mx(h):
                    n = 4 * l + h
                    dve.wait_ge(xa_s, n + 1)
                    b = 2 * (h % 2)
                    c = 4 * (h % 2)
                    nc.vector.tensor_reduce(sm[:, 72 + c:76 + c], ps[:, b:b + 2, :].rearrange("p b (t m) -> p (b t) m", t=2),
                                            AX.X, ALU.max).then_inc(xa_mx, 1)
                    dve.wait_ge(xa_mx, n + 1)
                    if h >= 2:
                        dve.wait_ge(xa_exp, 4 * (n - 1))
                    nc.vector.tensor_scalar(sm[:, 48 + c:52 + c], sm[:, 72 + c:76 + c], -SCALE_X, None,
                                            ALU.mult).then_inc(xa_nm, 1)
                def out_lo(h):
                    dve.wait_ge(xa_hi, 4 * l + h + 1)
                    b = 4 + 2 * (h % 2)
                    nc.vector.tensor_tensor(YL[:, 2 * h:2 * h + 2, :], ps[:, b:b + 2, :],
                                            YH[:, 2 * h:2 * h + 2, :].bitcast(F32), ALU.subtract).then_inc(xa_lo, 1)

                mx(0)
                for h in range(XA_H):
                    n = 4 * l + h
                    c = 4 * (h % 2)
                    if h + 1 < XA_H:
                        mx(h + 1)
                    dve.wait_ge(xa_exp, 4 * n + 4)
                    nc.vector.reciprocal(sm[:, 64 + c:68 + c], sm[:, 56 + c:60 + c]).then_inc(xa_rr, 1)
                    dve.wait_ge(xa_rr, n + 1)
                    nc.vector.tensor_tensor(PX[:, h % 2, :, :], PX[:, h % 2, :, :],
                                            sm[:, 64 + c:68 + c].unsqueeze(2).broadcast_to([P, NCH, NMEM]),
                                            ALU.mult).then_inc(xa_p, 1)
                    if h >= 1:
                        out_lo(h - 1)
                out_lo(XA_H - 1)

            def ffn(l):
                name = f"up{l}"
                u0, ng = first[name], FF1 // 256
                nd, na = FD * ng * l, FA * ng * l
                w0, nf = PARAM_COLS[f"ffn_w{l}"][0], FF1 // P

                def group(g, bank):
                    def tap(i, q):
                        return par[:, bass.ds(g * 2 + (w0 + i * nf + q), 1)]

                    def step(n):
                        dve.wait_ge(ffn_dve, g * FD + (nd + n))
                    dve.wait_ge(w_used, g * 4 + (u0 + 4))
                    nc.vector.tensor_tensor(GP[:, :, 1:T + 1], ps[:, bank + 2:bank + 4, :], over(R[:, :], 2),
                                            ALU.mult).then_inc(ffn_dve, 1)
                    for q in range(2):
                        step(1)
                        nc.vector.tensor_scalar(CV[:, q, :], GP[:, q, 0:T], tap(0, q), None,
                                                ALU.mult).then_inc(ffn_dve, 1)
                    for i in (1, 2):
                        for q in range(2):
                            step(2 * i + q)
                            nc.vector.scalar_tensor_tensor(out=CV[:, q, :], in0=GP[:, q, i:T + i], scalar=tap(i, q),
                                                           in1=CV[:, q, :], op0=ALU.mult,
                                                           op1=ALU.add).then_inc(ffn_dve, 1)
                    nc.vector.tensor_tensor(UU[:, :, :], ps[:, bank:bank + 2, :], over(R[:, :], 2),
                                            ALU.mult).then_inc(ffn_dve, 1)
                    step(8)
                    dve.wait_ge(ffn_act, g * FA + (na + 2))
                    nc.vector.tensor_tensor(HF[:, :, :], UU[:, :, :], EG[:, :, :], ALU.mult).then_inc(ffn_dve, 1)
                    dve.wait_ge(ffn_act, g * FA + (na + 3))
                    nc.vector.tensor_tensor(HID[:, bass.ds(g * 2 + nf, 2), :], HF[:, :, :],
                                            HID[:, bass.ds(g * 2, 2), :].bitcast(F32),
                                            ALU.subtract).then_inc(ffn_dve, 1)

                nc.vector.memset(GP[:, :, 0:1], 0.0)
                nc.vector.memset(GP[:, :, T + 1:T + 2], 0.0).then_inc(pad_d, 1)
                dve.wait_ge(pad_d, 2 * l + 1)
                dve.wait_ge(r_done, 2 * norm_of[name] + 2)
                with dve.Fori(0, ng // 2) as i:
                    for s in range(2):
                        group(i * 2 + s, 4 * s)

            def conv_mixer():
                u0 = first["in1"]
                nc.vector.memset(VP[:, :, 0:1], 0.0)
                nc.vector.memset(VP[:, :, T + 1:T + 2], 0.0).then_inc(pad_d, 1)
                dve.wait_ge(pad_d, 2)
                dve.wait_ge(r_done, 2 * norm_of["in1"] + 2)
                for q in range(2):
                    n = 18 * q

                    def bank(g):
                        b = 4 * ((3 * q + g) % 2)
                        return ps[:, b:b + 4, :]

                    def used(g):
                        dve.wait_ge(w_used, u0 + 4 * (3 * q + g) + 4)
                    used(0)
                    nc.vector.tensor_tensor(CS[:, :, :], bank(0), over(R[:, :], 4), ALU.mult).then_inc(cm_dve, 1)
                    used(1)
                    nc.vector.tensor_tensor(VP[:, :, 1:T + 1], bank(1), over(R[:, :], 4), ALU.mult).then_inc(cm_dve, 1)
                    dve.wait_ge(cm_dve, n + 2)
                    nc.vector.tensor_tensor(VP[:, :, 1:T + 1], VP[:, :, 1:T + 1], CS[:, :, :], ALU.mult).then_inc(cm_dve, 1)
                    dve.wait_ge(cm_dve, n + 3)
                    for i in range(3):
                        for c in range(4):
                            tap = pcol("conv_c", i * KT + 4 * q + c)
                            if i == 0:
                                nc.vector.tensor_scalar(CVC[:, c, :], VP[:, c, 0:T], tap, None,
                                                        ALU.mult).then_inc(cm_dve, 1)
                            else:
                                dve.wait_ge(cm_dve, n + 4 * i + c)
                                nc.vector.scalar_tensor_tensor(out=CVC[:, c, :], in0=VP[:, c, i:T + i], scalar=tap,
                                                               in1=CVC[:, c, :], op0=ALU.mult,
                                                               op1=ALU.add).then_inc(cm_dve, 1)
                    used(2)
                    nc.vector.tensor_tensor(TY[:, :, :], bank(2), over(R[:, :], 4), ALU.mult).then_inc(cm_dve, 1)
                    dve.wait_ge(cm_dve, n + 16)
                    nc.vector.tensor_tensor(TY[:, :, :], TY[:, :, :], CVC[:, :, :], ALU.mult).then_inc(cm_dve, 1)
                    dve.wait_ge(cm_act, q + 1)
                    nc.vector.tensor_tensor(YL[:, 4 * q:4 * q + 4, :], TY[:, :, :],
                                            YH[:, 4 * q:4 * q + 4, :].bitcast(F32), ALU.subtract).then_inc(cm_dve, 1)

            residual("out0")
            for l in range(2):
                if l == 1 and "in1" in first:
                    conv_mixer()
                    residual("out1")
                if f"q{l}" not in first:
                    break
                cross(l)
                if f"wo{l}" not in first:
                    break
                residual(f"wo{l}")
                if f"up{l}" not in first:
                    break
                ffn(l)
                residual(f"down{l}")

            def banks(b):
                return ps[:, b:b + 4, :]

            def scaled(dst, b, done):
                nc.vector.tensor_tensor(dst, banks(b), over(R[:, :], 4), ALU.mult).then_inc(done, 1)

            def retention():
                dve.wait_ge(r_done, 2 * norm_of["rqk"] + 2)
                dve.wait_ge(w_used, first["rqk"] + 4)
                scaled(RQ[:, :, :], 0, rqk_out)
                dve.wait_ge(w_used, first["rqk"] + 8)
                nc.vector.scalar_tensor_tensor(out=RK[:, :, :], in0=banks(4), scalar=0.125, in1=over(R[:, :], 4),
                                               op0=ALU.mult, op1=ALU.mult).then_inc(rqk_out, 1)
                for g in range(2):
                    dve.wait_ge(w_used, first["rv"] + 4 * g + 4)
                    part = RV[:, :, g * T:(g + 1) * T]
                    for t in range(NCH):
                        nc.vector.tensor_scalar(part[:, t, :], ps[:, 4 * g + t, :], RC[:, t:t + 1], None,
                                                ALU.mult).then_inc(rv_out, 1)
                    v4 = part.rearrange("p t (h d) -> p t h d", d=P)
                    mean = RVM[:, :, 4 * g:4 * g + 4]
                    dve.wait_ge(rv_out, 7 * g + 4)
                    nc.vector.tensor_reduce(mean, v4, AX.X, ALU.add).then_inc(rv_out, 1)
                    dve.wait_ge(rv_out, 7 * g + 5)
                    nc.vector.tensor_scalar(mean, mean, -1.0 / P, None, ALU.mult).then_inc(rv_out, 1)
                    dve.wait_ge(rv_out, 7 * g + 6)
                    for t in range(NCH):
                        ins_ = nc.vector.tensor_tensor(v4[:, t], v4[:, t], mean[:, t].unsqueeze(2).broadcast_to([P, 4, P]),
                                                       ALU.add)
                    ins_.then_inc(rv_out, 1)
                dve.wait_ge(t_loaded, 48)
                for b, x in enumerate((RQ, RK)):
                    dve.wait_ge(rot_done, b + 1)
                    if b:
                        dve.wait_ge(rot_out, 3)
                    nc.vector.tensor_tensor(RT[:, :, :], banks(4 * b), over(SIN[:, :], 4), ALU.mult).then_inc(rot_out, 1)
                    nc.vector.tensor_tensor(x[:, :, :], x[:, :, :], over(COS[:, :], 4), ALU.mult).then_inc(rot_out, 1)
                    dve.wait_ge(rot_out, 3 * b + 2)
                    nc.vector.tensor_tensor(x[:, :, :], x[:, :, :], RT[:, :, :], ALU.add).then_inc(rot_out, 1)

                def norm(h):
                    dve.wait_ge(ret_rn, h + 1)
                    nc.vector.scalar_tensor_tensor(out=RO[:, h, :], in0=ps[:, 6 + h % 2, :], scalar=pcol("ret_g", h),
                                                   in1=RN[:, :], op0=ALU.mult, op1=ALU.mult).then_inc(ret_ro, 1)

                for h in range(RET_H):
                    dve.wait_ge(ret_dec, h + 1)
                    if h >= 2:
                        dve.wait_ge(ret_o, h - 1)
                    for j in range(NCH):
                        w = T - j * P
                        dve.wait_ge(ret_s, 3 * h + min(j, 2) + 1)
                        b, o = ((0, 0), (1, 0), (2, 0), (2, 256))[j]
                        a = (0, 512, 896, 1152)[j]
                        nc.vector.tensor_tensor(SCO[:, h % 2, a:a + w], ps[:, 3 * (h % 2) + b, o:o + w],
                                                DEC[:, h % 2, 0:w], ALU.mult).then_inc(ret_sc, 1)
                    if h >= 2:
                        norm(h - 2)
                norm(RET_H - 2)
                norm(RET_H - 1)

            def decay_rows():
                B1, A1, A3, SPR, BEG, EGL, EG8, ONE = [rows[i][:, :] for i in range(8)]
                step = lambda n: dve.wait_ge(ab_dve, n)
                dve.wait_ge(w_used, first["dab"] + 1)
                nc.vector.tensor_tensor(B1, ps[0:DN_H, 0, :], R[0:DN_H, :], ALU.mult).then_inc(ab_dve, 1)
                nc.vector.tensor_tensor(A1, ps[32:32 + DN_H, 0, :], R[32:32 + DN_H, :], ALU.mult).then_inc(ab_dve, 1)
                step(2)
                nc.vector.tensor_scalar(A1, A1, pcol("dt_bias")[0:DN_H, :], None, ALU.add).then_inc(ab_dve, 1)
                nc.vector.memset(ONE, 1.0)
                dve.wait_ge(ab_act, 4)
                step(3)
                nc.vector.scalar_tensor_tensor(out=SPR, in0=A1, scalar=0.0, in1=A3, op0=ALU.max,
                                               op1=ALU.add).then_inc(ab_dve, 1)
                dve.wait_ge(ab_act, 5)
                step(4)
                nc.vector.tensor_scalar(SPR, SPR, sm[0:DN_H, 80:81], -1.0, ALU.mult, ALU.mult).then_inc(ab_dve, 1)
                step(5)
                for n in range(NCH):
                    c = slice(n * P, (n + 1) * P)
                    nc.vector.tensor_tensor_scan(GR[:, c], ONE[:, c], SPR[:, c], 0.0, ALU.mult, ALU.add).then_inc(ab_dve, 1)
                step(9)
                for n in range(NCH):
                    c = slice(n * P, (n + 1) * P)
                    nc.vector.tensor_scalar(EGL[:, c], GR[:, c], GR[:, (n + 1) * P - 1:(n + 1) * P], -1.0,
                                            ALU.subtract, ALU.mult).then_inc(ab_dve, 1)
                dve.wait_ge(ab_act, 6)
                nc.vector.scalar_tensor_tensor(out=BEG, in0=EG8, scalar=-1.0, in1=BR[:, :], op0=ALU.mult,
                                               op1=ALU.mult).then_inc(ab_dve, 1)

            def delta(q):
                u0 = first[f"dvqk{q}"]
                nd = 51 * q
                bv, bq = (4, 0) if q == 0 else (0, 4)
                if q == 0:
                    dve.wait_ge(ab_act, 8)
                nc.vector.memset(GP3[:, :, 0:3], 0.0).then_inc(pad_d, 1)
                dve.wait_ge(pad_d, 4 + q)
                for i, (g, dst, bank) in enumerate(((2, VB, bv), (0, QN, bq), (1, KN, bv))):
                    dve.wait_ge(w_used, u0 + 4 * i + 4)
                    if nd + i:
                        dve.wait_ge(dq_dve, nd + 17 * i)
                    nc.vector.tensor_tensor(GP3[:, :, 3:T + 3], banks(bank), over(R[:, :], 4),
                                            ALU.mult).then_inc(dq_dve, 1)
                    for j in range(4):
                        for c in range(4):
                            tap = pcol("dn_conv", j * 3 * DN_H + g * DN_H + 4 * q + c)
                            dve.wait_ge(dq_dve, nd + 17 * i + max(1, 4 * j - 2 + c))
                            if j == 0:
                                nc.vector.tensor_scalar(dst[:, c, :], GP3[:, c, 0:T], tap, None, ALU.mult).then_inc(dq_dve, 1)
                            else:
                                nc.vector.scalar_tensor_tensor(out=dst[:, c, :], in0=GP3[:, c, j:T + j], scalar=tap,
                                                               in1=dst[:, c, :], op0=ALU.mult, op1=ALU.add).then_inc(dq_dve, 1)

                def normalise(i, x, ln, scale):
                    dve.wait_ge(l2_r, 2 * q + i + 1)
                    nc.vector.scalar_tensor_tensor(out=x[:, :, :], in0=x[:, :, :], scalar=scale, in1=ln[:, :, :],
                                                   op0=ALU.mult, op1=ALU.mult).then_inc(l2_n, 1)

                normalise(0, QN, LNq, float(P) ** -0.5)
                dve.wait_ge(w_used, first[f"gated{q}"] + 4)
                dve.wait_ge(h_saved, 16)
                dve.wait_ge(x_lo, KT * (norm_of["rqk"] + 1))
                scaled(SGD[:, 4 * q:4 * q + 4, :], bv, ga_dve)
                normalise(1, KN, LNk, 1.0)
                dve.wait_ge(l_loaded, 16)

                def chunks(ap):
                    return ap.rearrange("p (n c) -> p n c", n=NCH)

                def column(a, h):
                    return TC[:, a, :, h:h + 1].broadcast_to([P, NCH, P])

                for pr in range(2):
                    m = 4 * q + 2 * pr
                    n0 = 24 * (2 * q + pr)
                    for p in range(2):
                        h, hh = m + p, 2 * pr + p
                        step = lambda k: dve.wait_ge(dp_dve, n0 + pair_step(p, k))
                        dve.wait_ge(dp_bc, m + p + 1)
                        if p == 0:
                            dve.wait_ge(l2_n, 2 * q + 2)
                        nc.vector.tensor_tensor(T1[:, p, :], KN[:, hh, :], ps[:, 4 * p + 1, :], ALU.mult).then_inc(dp_dve, 1)
                        dve.wait_ge(dp_eg, m + p + 1)
                        nc.vector.tensor_tensor(chunks(DL[:, p, :]), chunks(ps[:, 4 * p, :]), column(1, h),
                                                ALU.subtract).then_inc(dp_dve, 1)
                        step(2)
                        nc.vector.scalar_tensor_tensor(out=chunks(DL[:, p, :]), in0=chunks(DL[:, p, :]), scalar=0.0,
                                                       in1=over(cst[:, CONSTS["causal"], :], NCH), op0=ALU.min,
                                                       op1=ALU.add).then_inc(dp_dve, 1)
                    for p in range(2):
                        h, hh = m + p, 2 * pr + p
                        step = lambda k: dve.wait_ge(dp_dve, n0 + pair_step(p, k))
                        dve.wait_ge(dp_a, m + p + 1)
                        dve.wait_ge(dp_lt, m + p + 1)
                        nc.vector.tensor_tensor(AT[:, p, :], ps[:, 4 * p + 1, :], DL[:, p, :], ALU.mult).then_inc(dp_dve, 1)
                        nc.vector.tensor_tensor(ATT[:, hh, :], ps[:, 4 * p, :], DL[:, p, :], ALU.mult).then_inc(dp_dve, 1)
                        dve.wait_ge(dp_tr, m + p + 1)
                        nc.vector.tensor_tensor(chunks(KD[:, hh, :]), chunks(ps[:, 4 * p + 2, :]), column(3, h),
                                                ALU.mult).then_inc(dp_dve, 1)
                        nc.vector.tensor_tensor(chunks(VB[:, hh, :]), chunks(ps[:, 4 * p + 3, :]), column(0, h),
                                                ALU.mult).then_inc(dp_dve, 1)
                        step(4)
                        nc.vector.tensor_tensor(chunks(MT[:, hh, :]), chunks(AT[:, p, :]), over(LVM[:, 0, :], NCH),
                                                ALU.mult).then_inc(dp_dve, 1)
                        step(8)
                        nc.vector.tensor_tensor(chunks(MT[:, hh, :]), chunks(MT[:, hh, :]), over(ident, NCH),
                                                ALU.add).then_inc(dp_dve, 1)
                        step(9)
                        nc.vector.transpose(MM[:, p, :], MT[:, hh, :]).then_inc(dp_dve, 1)
                        dve.wait_ge(dp_eg, m + p + 1)
                        nc.vector.tensor_tensor(QN[:, hh, :], QN[:, hh, :], EGA[p][:, :], ALU.mult).then_inc(dp_dve, 1)
                        nc.vector.tensor_copy(sm[:, 84 + 4 * hh:88 + 4 * hh], EGA[p][:, P - 1:T:P]).then_inc(dp_dve, 1)
                    nl, npe = 34 * (2 * q + pr), 24 * (2 * q + pr)
                    for li, b in enumerate(LEVELS[1:]):
                        for p in range(2):
                            dve.wait_ge(lv_pe, npe + 4 * li + p + 1)
                            nc.vector.tensor_tensor(chunks(T1[:, p, :]), chunks(ps[:, 4 * p + 2, :]),
                                                    over(LVM[:, li + 1, :], NCH), ALU.mult).then_inc(lv_dve, 1)
                        for p in range(2):
                            hh = 2 * pr + p
                            dve.wait_ge(lv_pe, npe + 4 * li + 3 + p)
                            if li == 0:
                                dve.wait_ge(dp_dve, n0 + 24)
                            else:
                                dve.wait_ge(lv_dve, nl + 6 * li)
                            nc.vector.tensor_tensor(MT[:, hh, :], MT[:, hh, :], ps[:, 4 * p + 3, :],
                                                    ALU.subtract).then_inc(lv_dve, 1)
                            if b <= 16:
                                dve.wait_ge(lv_dve, nl + 6 * li + 3 + 2 * p)
                                nc.vector.transpose(MM[:, p, :], MT[:, hh, :]).then_inc(lv_dve, 1)
                            elif b == 32:
                                nc.vector.tensor_tensor(MM[:, p, :], MM[:, p, :], ps[:, 4 * p + 1, :],
                                                        ALU.subtract).then_inc(lv_dve, 1)
                for n in range(NCH):
                    for hh in range(4):
                        h = 4 * q + hh
                        if n:
                            dve.wait_ge(sc_ks, 12 * q + 4 * (n - 1) + hh + 1)
                            nc.vector.scalar_tensor_tensor(out=YS[:, hh, :], in0=ps[:, hh, 0:P],
                                                           scalar=TC[:, 2, n, h:h + 1], in1=VB[:, hh, n * P:(n + 1) * P],
                                                           op0=ALU.mult, op1=ALU.add).then_inc(sc_y, 1)
                    if n == NCH - 1:
                        continue
                    for hh in range(4):
                        dve.wait_ge(sc_su, 12 * q + 4 * n + hh + 1)
                        if n == 0:
                            nc.vector.tensor_copy(SS[:, hh, :], ps[:, hh, 2 * P:3 * P]).then_inc(sc_s, 1)
                        else:
                            dve.wait_ge(sc_s, 12 * q + 4 * (n - 1) + hh + 1)
                            nc.vector.scalar_tensor_tensor(out=SS[:, hh, :], in0=SS[:, hh, :],
                                                           scalar=sm[:, 84 + 4 * hh + n:85 + 4 * hh + n],
                                                           in1=ps[:, hh, 2 * P:3 * P], op0=ALU.mult,
                                                           op1=ALU.add).then_inc(sc_s, 1)
                dve.wait_ge(do_r, q + 1)
                nc.vector.scalar_tensor_tensor(out=DO[:, 4 * q:4 * q + 4, :], in0=DO[:, 4 * q:4 * q + 4, :], scalar=pcol("dn_g"),
                                               in1=LNo[:, :, :], op0=ALU.mult, op1=ALU.mult).then_inc(do_n, 1)

            def ffn2():
                u0, ng = first["up2"], FF2 // 256
                w0, b0, nf = PARAM_COLS["ffn_w2"][0], PARAM_COLS["ffn_b2"][0], FF2 // P
                nc.vector.memset(GP4[:, :, 0:2], 0.0).then_inc(pad_d, 1)
                dve.wait_ge(pad_d, 6)
                dve.wait_ge(r_done, 2 * norm_of["up2"] + 2)

                def group(g, bank):
                    def of(col, q):
                        return par[:, bass.ds(g * 2 + (col + (q // 2) * nf + q % 2), 1)]

                    def step(n):
                        dve.wait_ge(up2_dve, g * FD2 + n)
                    dve.wait_ge(w_used, g * 4 + (u0 + 4))
                    nc.vector.tensor_tensor(GP4[:, :, 2:T + 2], banks(bank), over(R[:, :], 4), ALU.mult).then_inc(up2_dve, 1)
                    for q in range(4):
                        step(1)
                        nc.vector.tensor_scalar(CV4[:, q, :], GP4[:, q, 0:T], of(w0, q), of(b0, q),
                                                ALU.mult, ALU.add).then_inc(up2_dve, 1)
                    for i in (1, 2):
                        for q in range(4):
                            step(4 * i - 2 + q)
                            nc.vector.scalar_tensor_tensor(out=CV4[:, q, :], in0=GP4[:, q, i:T + i],
                                                           scalar=of(w0 + 2 * nf * i, q), in1=CV4[:, q, :],
                                                           op0=ALU.mult, op1=ALU.add).then_inc(up2_dve, 1)
                    step(13)
                    dve.wait_ge(up2_act, g * FA2 + 1)
                    nc.vector.tensor_tensor(HF2[:, :, :], SA[:, :, :], CV4[:, 2:4, :], ALU.mult).then_inc(up2_dve, 1)
                    dve.wait_ge(up2_act, g * FA2 + 2)
                    nc.vector.tensor_tensor(HID[:, bass.ds(g * 2 + nf, 2), :], HF2[:, :, :],
                                            HID[:, bass.ds(g * 2, 2), :].bitcast(F32),
                                            ALU.subtract).then_inc(up2_dve, 1)

                with dve.Fori(0, ng // 2) as i:
                    for s in range(2):
                        group(i * 2 + s, 4 * s)
                group(ng - 1, 0)

            def block2():
                dve.wait_ge(r_done, 2 * norm_of["bnorm"] + 2)
                residual("bnorm")
                retention()
                for g in range(2):
                    dve.wait_ge(w_used, first["rgate"] + 4 * g + 4)
                    if g:
                        dve.wait_ge(rg_act, 2)
                        dve.wait_ge(rg_dve, 3)
                    scaled(TG[:, :, :], 4 * g, rg_dve)
                    dve.wait_ge(rg_act, 2 * g + 1)
                    nc.vector.tensor_tensor(TG[:, :, :], SG[:, :, :], RO[:, 4 * g:4 * g + 4, :], ALU.mult).then_inc(rg_dve, 1)
                    dve.wait_ge(rg_act, 2 * g + 2)
                    nc.vector.tensor_tensor(YL[:, 4 * g:4 * g + 4, :], TG[:, :, :], YH[:, 4 * g:4 * g + 4, :].bitcast(F32),
                                            ALU.subtract).then_inc(rg_dve, 1)
                for g in range(2):
                    dve.wait_ge(w_used, first["gater"] + 4 * g + 4)
                    scaled(MG[:, 4 * g:4 * g + 4, :], 4 * g, gr_dve)
                for g in range(2):
                    dve.wait_ge(w_used, first["retbr"] + 4 * g + 4)
                    dve.wait_ge(gr_act, g + 1)
                    nc.vector.tensor_tensor(MG[:, 4 * g:4 * g + 4, :], MG[:, 4 * g:4 * g + 4, :], banks(4 * g),
                                            ALU.mult).then_inc(rb_dve, 1)
                decay_rows()
                delta(0)
                delta(1)
                for g in range(2):
                    dve.wait_ge(w_used, first["dz"] + 4 * g + 4)
                    if g:
                        dve.wait_ge(dz_dve, 2)
                    scaled(TZ[:, :, :], 4 * g, dz_dve)
                    dve.wait_ge(dz_act, g + 1)
                    nc.vector.tensor_tensor(DO[:, 4 * g:4 * g + 4, :], DO[:, 4 * g:4 * g + 4, :], TZ[:, :, :],
                                            ALU.mult).then_inc(dz_dve, 1)
                for g in range(2):
                    dve.wait_ge(dz_act, 3 + g)
                    nc.vector.tensor_tensor(XL[:, 4 * g:4 * g + 4, :], DO[:, 4 * g:4 * g + 4, :],
                                            XH[:, 4 * g:4 * g + 4, :].bitcast(F32), ALU.subtract).then_inc(dz_dve, 1)
                for g in range(2):
                    part = slice(4 * g, 4 * g + 4)
                    dve.wait_ge(w_used, first["dnbr"] + 4 * g + 4)
                    dve.wait_ge(ga_act, 2)
                    dve.wait_ge(dn_dve, 3 * g) if g else dve.wait_ge(dz_dve, 6)
                    nc.vector.tensor_tensor(TZ[:, :, :], SGD[:, part, :], banks(4 * g), ALU.mult).then_inc(dn_dve, 1)
                    dve.wait_ge(dn_dve, 3 * g + 1)
                    dve.wait_ge(rb_dve, 2)
                    nc.vector.tensor_tensor(MG[:, part, :], MG[:, part, :], TZ[:, :, :], ALU.add).then_inc(dn_dve, 1)
                    dve.wait_ge(dn_act, g + 1)
                    nc.vector.tensor_tensor(YL[:, part, :], MG[:, part, :], YH[:, part, :].bitcast(F32),
                                            ALU.subtract).then_inc(dn_dve, 1)
                dve.wait_ge(h_back, 16)
                residual("wo2")
                ffn2()
                residual("down2", flip=4)
                dve.wait_ge(r_done, 2 * norm_of["final"] + 2)
                for c in range(KT):
                    nc.vector.scalar_tensor_tensor(out=H[:, c, :], in0=H[:, c, :], scalar=pcol("final2", c),
                                                   in1=R[:, :], op0=ALU.mult, op1=ALU.mult).then_inc(fin_dve, 1)

            if two:
                block2()


def shape_constants():
    c = {}
    ident = np.eye(P)
    half = P // 4
    m = np.arange(P)
    upper = m % (2 * half) >= half
    rot = np.zeros((P, P))
    rot[np.where(upper, m - half, m + half), m] = np.where(upper, 1.0, -1.0)
    causal = np.where(np.arange(P)[None, :] >= np.arange(P)[:, None], 0.0, -1e30)
    tiles = {"ident": ident, "ones": np.full((P, P), 1.0 / D), "rot": rot, "causal": causal}
    c["consts"] = np.stack([tiles[n] for n in CONSTS], axis=1).astype(np.float32)
    inv = 10000.0 ** (-np.arange(half, dtype=np.float32) * 2 / (2 * half))
    ang = (np.arange(T, dtype=np.float32)[None, :] * inv.astype(np.float32)[m % half][:, None]).astype(np.float32)
    c["rot_cos"] = np.cos(ang.astype(np.float64)).astype(np.float32)
    c["rot_sin"] = np.sin(ang.astype(np.float64)).astype(np.float32)
    age = np.arange(T)[None, :] - np.arange(P)[:, None]
    c["age"] = np.where(age >= 0, age, 1e9).astype(np.float32)
    i, j = np.arange(P)[:, None], np.arange(P)[None, :]
    lv = [np.where((i // (2 * b) == j // (2 * b)) & (i % (2 * b) >= b) & (j % (2 * b) < b), 1.0, 0.0) for b in LEVELS]
    lv[0] = -lv[0].T
    c["levels"] = np.stack(lv, axis=1).astype(np.float32)
    s = np.arange(T)
    ang = 2 * np.pi * ((s[:, None] * s[None, :]) % T) / T
    seq = np.stack([np.cos(ang), -np.sin(ang)], axis=1)
    c["fourier_seq"] = seq.reshape(NCH, P, 2, T).transpose(1, 0, 2, 3).astype(np.float32)
    g = np.arange(P)
    ang = 2 * np.pi * ((g[:, None] * g[None, :]) % P) / P
    c["fourier_grp"] = (np.concatenate([np.cos(ang), np.sin(ang)], axis=1) / np.sqrt(T * P)).astype(np.float32)
    return {k: np.ascontiguousarray(v) for k, v in c.items()}


def lay_out(inputs):
    a = {k: np.asarray(v) for k, v in inputs.items()}
    feat = lambda v: v.reshape(-1, P).T
    f = {"mem": feat(a["mem_norm_g"]), "final1": feat(a["final_norm_g"]), "mix2": feat(a["g_mix_2"][0]),
         "ffn2": feat(a["g_ffn_2"][0]), "final2": feat(a["g_final_2"]), "conv_c": feat(a["conv_c"][0]),
         "ret_g": feat(a["ret_norm_g_2"][0]), "dn_conv": feat(a["dn_conv_w_2"][0]), "dn_g": feat(a["dn_norm_g_2"][0]),
         "ffn_w2": feat(a["ffn_conv_w_2"][0]), "ffn_b2": feat(a["ffn_conv_b_2"][0]),
         "a_log": np.pad(a["dn_a_log_2"].T, ((0, P - DN_H), (0, 0))),
         "dt_bias": np.pad(a["dn_dt_bias_2"].T, ((0, P - DN_H), (0, 0)))}
    for l in range(2):
        f[f"mix{l}"] = feat(a["mix_norm_g"][l])
        f[f"xa{l}"] = feat(a["xa_norm_g"][l])
        f[f"ffn{l}"] = feat(a["ffn_norm_g"][l])
        f[f"ffn_w{l}"] = feat(a["ffn_conv_w"][l])
        f[f"ffn_b{l}"] = feat(a["ffn_conv_b"][l])
    out = {"xT": a["x"][0].T, "memT": a["mem"][0].T,
           "params": np.concatenate([f[n] for n in PARAM_COLS], axis=1),
           "rpb": np.pad(a["rpb"][0], ((0, 0), (0, 0), (RPB_PAD, RPB_PAD)))}
    for n in WEIGHTS:
        out[n] = a[n]
    out.update(shape_constants())
    return {k: np.ascontiguousarray(v) for k, v in out.items()}


WEIGHTS = ("w_in_ab", "w_out_ab", "w_in_c", "w_out_c", "xa_wq", "xa_wkv", "xa_wo", "ffn_w_up", "ffn_w_down",
           "w_in_2", "w_ret_br_2", "w_dn_br_2", "w_o_2", "w_up_2", "w_down_2")
C_DB, C_DA, C_GR, C_GD = 7168, 7176, 7184, 8208
LOG_GAMMA = [float(np.log(1.0 - 2.0 ** (-5.0 - h))) for h in range(RET_H)]
SCALE_NA = float(P) ** -0.5
SCALE_X = float(2 * P) ** -0.5
STAT_BANK = 4
MEM_BANK = 6


def build(nc, arrays, stop=None):
    ins = {n: nc.dram_tensor(n, a.shape, F32, kind="ExternalInput").ap() for n, a in arrays.items()}
    out = nc.dram_tensor("outT", (D, T), F32, kind="ExternalOutput").ap()
    program(nc, ins, out, stop)


def kernel(**inputs):
    import concourse.bacc as _bacc
    from concourse.bass_utils import run_bass_kernel_spmd as _run

    arrays = lay_out(inputs)
    nc = _bacc.Bacc("TRN2", target_bir_lowering=False, num_devices=1, dynamic_dma_scratch_size=1024)
    build(nc, arrays)
    r = _run(nc, [arrays], core_ids=[0])
    return np.ascontiguousarray(r.results[0]["outT"].T)[None]
```

```python
from contextlib import ExitStack

import concourse.bass as bass
import numpy as np
from concourse import mybir

F32 = mybir.dt.float32
F32R = mybir.dt.float32r
ACT = mybir.ActivationFunctionType
ALU = mybir.AluOpType
AX = mybir.AxisListType

P = 128
D = 1024
KT = D // P
T = 512
NMEM = 256
EPS = 1e-6
GN_EPS = 1e-5
UC = 512
RING = 4
LO_RING = 2
KB = 1024

NA_H = 4
GRID_W = 64
ROWS = T // GRID_W
NA_KH, NA_KW = 8, 16
RPB_W = 2 * NA_KW - 1
RPB_PAD = GRID_W - NA_KW
RPB_PW = RPB_W + 2 * RPB_PAD
NA_ROWS = 2 * NA_KH - 2
XA_H = 4
FF1 = 2048
RET_H = 8
FF2 = 2816
DN_H = 8
NCH = T // P

BIG_SLOTS = 2 * FF2 // P
TAIL = 34 * KB

PARAM_COLS = {}


def _cols(name, n):
    start = sum(c for _, c in PARAM_COLS.values())
    PARAM_COLS[name] = (start, n)


for _n in ("mem", "mix0", "xa0", "ffn0", "mix1", "xa1", "ffn1", "final1", "mix2", "ffn2", "final2"):
    _cols(_n, KT)
_cols("conv_c", 3 * KT)
for _l in range(2):
    _cols(f"ffn_w{_l}", 3 * FF1 // P)
    _cols(f"ffn_b{_l}", FF1 // P)
_cols("ret_g", RET_H)
_cols("dn_conv", 4 * 3 * DN_H)
_cols("dn_g", 1)
_cols("ffn_w2", 3 * 2 * FF2 // P)
_cols("ffn_b2", 2 * FF2 // P)
_cols("a_log", 1)
_cols("dt_bias", 1)
N_PARAMS = sum(c for _, c in PARAM_COLS.values())

CONSTS = {"ident": 0, "ones": 1, "causal": 2}
N_CONST = len(CONSTS)
LEVELS = (1, 2, 4, 8, 16, 32, 64)


def program(nc, ins, out):
    ctx = ExitStack()
    with ctx:
        def sb(name, shape, dt=F32):
            return ctx.enter_context(nc.sbuf_tensor(name, shape, dt))

        def sem(name):
            return ctx.enter_context(nc.semaphore(name))

        H = sb("H", [P, KT, T])
        XH = sb("XH", [P, KT, T], F32R)
        XL = sb("XL", [P, KT, T], F32R)
        w_raw = sb("w_raw", [P, RING, 2, UC])
        w_hi = sb("w_hi", [P, RING, 2, UC], F32R)
        w_lo = sb("w_lo", [P, LO_RING, 2, UC], F32R)
        R = sb("R", [P, T])
        LNT = sb("LNT", [P, T])
        RC = sb("RC", [P, NCH])
        LNC = sb("LNC", [P, NCH])
        ACC = sb("ACC", [P, T])
        SQ = sb("SQ", [P, T])
        par = sb("par", [P, N_PARAMS])
        cst = sb("cst", [P, N_CONST, P])
        eps_c = sb("eps_c", [P, 2])
        sm = sb("sm", [P, 128])
        base_before = (nc.sbuf_base + 31) // 32 * 32
        arena = sb("arena", [P, (BIG_SLOTS * T * 4 + TAIL) // 4])
        ps = ctx.enter_context(nc.psum_tensor("ps", [P, 8, T], F32))
        a0 = base_before

        def at(name, kb, shape, dt=F32):
            return nc.alloc_sbuf_tensor_at(name, shape, dt, offset=a0 + int(kb * KB))

        ident = cst[:, CONSTS["ident"], :]
        ones = cst[:, CONSTS["ones"], :]

        def backwards(ap):
            return bass.AP(ap.tensor, ap.offset + P - 1, [list(ap.ap[0]), [P, T // P], [-1, P]])

        def pcol(name, i=0, n=1):
            c = PARAM_COLS[name][0] + i
            return par[:, c:c + n]

        HID = at("HID", 0, [P, BIG_SLOTS, T], F32R)
        Y0, SCR, TL = 0, 32, 88
        YH = HID[:, 0:KT, :]
        YL = HID[:, KT:2 * KT, :]
        Q = at("Q", SCR, [P, NA_H, T])
        K = at("K", SCR + 8, [P, NA_H, T])
        V = at("V", SCR + 16, [P, NCH, NA_H * P])
        ZC = at("ZC", SCR + 24, [P, NA_H * NCH * 2 * P])
        FC = at("FC", SCR + 40, [P, NCH, 2, T])
        GC = at("GC", TL + 14, [P, 2 * P])
        B2 = at("B2", TL, [P, NA_H, NA_ROWS, GRID_W])
        Z = at("Z", TL + 16, [P, NA_H, T])
        S = at("S", SCR + 24, [P, 2, T])
        PR = at("PR", SCR + 28, [P, 2, T])
        PT = at("PT", SCR + 32, [P, 2, NCH, T])
        KX = at("KX", TL, [P, KT, NMEM])
        VX = at("VX", TL + 8, [P, 2, D])
        M = at("M", TL + 16, [P, KT, NMEM])
        ML = at("ML", TL + 16, [P, KT, NMEM], F32R)
        MH = at("MH", TL + 26, [P, KT, NMEM], F32R)
        QX = at("QX", SCR, [P, KT, T])
        PX = at("PX", SCR + 16, [P, 2, NCH, NMEM])
        PTX = at("PTX", SCR + 24, [P, 2, 2, T])
        MSQ = at("MSQ", SCR, [P, KT, NMEM])
        MACC = at("MACC", SCR + 8, [P, NMEM])
        MLN = at("MLN", SCR + 9, [P, NMEM])
        MR = at("MR", SCR + 10, [P, NMEM])
        F1 = 64
        GP = at("GP", F1, [P, 2, T + 2])
        CV = at("CV", F1 + 4.5, [P, 2, T])
        EG = at("EG", F1 + 8.5, [P, 2, T])
        UU = at("UU", F1 + 12.5, [P, 2, T])
        HF = at("HF", F1 + 16.5, [P, 2, T])
        CS = at("CS", SCR, [P, 4, T])
        VP = at("VP", SCR + 8, [P, 4, T + 2])
        CVC = at("CVC", SCR + 17, [P, 4, T])
        TY = at("TY", SCR + 25, [P, 4, T])

        ACC2, SQ2 = at("ACC2", TL, [P, T]), at("SQ2", TL + 2, [P, T])
        RQ = at("RQ", SCR, [P, 4, T])
        RK = at("RK", SCR + 8, [P, 4, T])
        RV = at("RV", SCR + 16, [P, NCH, RET_H * P])
        RO = at("RO", SCR + 32, [P, RET_H, T])
        RT = at("RT", 0, [P, 4, T])
        SCO = at("SCO", 80, [P, 2, 1280])
        DEC = at("DEC", 90, [P, 2, T])
        COS = at("COS", 94, [P, T])
        SIN = at("SIN", 96, [P, T])
        AGE = at("AGE", 98, [P, T])
        RSQ = at("RSQ", 100, [P, T])
        RLN = at("RLN", 102, [P, T])
        RN = at("RN", 104, [P, T])
        RVM = at("RVM", 106, [P, NCH, RET_H])
        RG = H
        TG = at("TG", SCR, [P, KT, T])
        MG = at("MG", 96, [P, KT, T])
        DO = at("DO", 80, [P, DN_H, T])
        QN = at("QN", 0, [P, 4, T])
        KN = at("KN", 8, [P, 4, T])
        VB = at("VB", 16, [P, 4, T])
        MT = at("MT", 24, [P, 4, T])
        ATT = at("ATT", 32, [P, 4, T])
        KD = at("KD", 40, [P, 4, T])
        GP3 = at("GP3", 48, [P, 4, T + 3])
        SQq, LNq = at("SQq", 24, [P, 4, T]), at("LNq", 32, [P, 4, T])
        SQk, LNk = at("SQk", 56.5, [P, 4, T]), at("LNk", 40, [P, 4, T])
        DL = at("DL", 48, [P, 2, T])
        AT = at("AT", 52, [P, 2, T])
        MM = at("MM", 56, [P, 2, T])
        T1 = at("T1", 60, [P, 2, T])
        SQo, LNo = at("SQo", 48, [P, 4, T]), at("LNo", 56, [P, 4, T])
        EGA = [at("EGA0", 64, [P, T]), at("EGA1", 69.5, [P, T])]
        GB = at("GB", TL + 26, [P, 2, 2, T])
        LVM = at("LVM", 66, [P, len(LEVELS), P])
        YS = at("YS", 69.5, [P, 4, P])
        VS = at("VS", 71.5, [P, 4, P])
        SS = at("SS", 73.5, [P, 4, P])
        GR = at("GR", 75.5, [DN_H, T])
        BR = at("BR", 77.5, [DN_H, T])
        TC = at("TC", 79.5, [P, 4, NCH, DN_H])
        rows = [at(f"row{i}", 48 + 2 * i, [DN_H, T]) for i in range(8)]
        SGD = H
        TZ = at("TZ", 64, [P, 4, T])
        NH, NL = HID[:, 2 * KT:3 * KT, :], HID[:, 3 * KT:4 * KT, :]
        GP4 = at("GP4", TL, [P, 4, T + 2])
        CV4 = at("CV4", TL + 8.25, [P, 4, T])
        SA = at("SA", TL + 16.25, [P, 2, T])
        HF2 = at("HF2", TL + 20.25, [P, 2, T])

        def cols(*starts):
            return [[(c, UC)] for c in starts]

        def halves(a, b, n):
            return [[(a + 256 * j, 256), (b + 256 * j, 256)] for j in range(n)]

        W = ins
        phases = [("in0", W["w_in_ab"][0], KT, cols(*range(0, 2048, UC))),
                  ("out0", W["w_out_ab"][0], KT, cols(0, UC))]
        for l in range(2):
            if l == 1:
                phases += [("in1", W["w_in_c"][0], KT,
                            cols(1024, 2048, 0, 1024 + UC, 2048 + UC, UC)),
                           ("out1", W["w_out_c"][0], KT, cols(0, UC))]
            phases += [(f"kv{l}", W["xa_wkv"][l], KT, cols(0, UC, 2 * UC, 3 * UC)),
                       (f"q{l}", W["xa_wq"][l], KT, cols(0, UC)),
                       (f"wo{l}", W["xa_wo"][l], KT, cols(0, UC)),
                       (f"up{l}", W["ffn_w_up"][l], KT, halves(0, FF1, FF1 // 256)),
                       (f"down{l}", W["ffn_w_down"][l], FF1 // P, cols(0, UC))]
        W2 = W["w_in_2"][0]
        phases += [("rqk", W2, KT, cols(0, 512)), ("rv", W2, KT, cols(1024, 1536)),
                   ("rgate", W2, KT, cols(2048, 2560)), ("gater", W2, KT, cols(C_GR, C_GR + UC)),
                   ("retbr", W["w_ret_br_2"][0], KT, cols(0, UC)),
                   ("dab", W2, 2, [[(C_DB, 32), (C_DA, 32), (C_GR, 64)]]),
                   ("dvqk0", W2, KT, cols(5120, 3072, 4096)), ("gated0", W2, KT, cols(C_GD)),
                   ("dvqk1", W2, KT, cols(5120 + UC, 3072 + UC, 4096 + UC)), ("gated1", W2, KT, cols(C_GD + UC)),
                   ("dz", W2, KT, cols(6144, 6144 + UC)),
                   ("dnbr", W["w_dn_br_2"][0], KT, cols(0, UC)), ("wo2", W["w_o_2"][0], KT, cols(0, UC)),
                   ("up2", W["w_up_2"][0], KT, halves(0, FF2, FF2 // 256)),
                   ("down2", W["w_down_2"][0], FF2 // P, cols(0, UC))]
        first, count = {}, {}
        n_units = 0
        unit = []
        for name, mat, nk, groups in phases:
            first[name] = n_units
            for g, pieces in enumerate(groups):
                for k in range(nk // 2):
                    unit.append((name, mat, k, pieces))
            n_units = len(unit)
            count[name] = n_units - first[name]
        load_value, at_slot = {}, [0] * RING
        for u in range(n_units):
            at_slot[u % RING] += 16 * len(unit[u][3])
            load_value[u] = at_slot[u % RING]

        w_loaded = [sem(f"w_loaded{s}") for s in range(RING)]
        hi_done = sem("hi_done")
        lo_done = sem("lo_done")
        w_used = sem("w_used")
        x_loaded = [sem(f"x_loaded{i}") for i in range(KT // 2)]
        c_loaded = sem("c_loaded")
        m_loaded = sem("m_loaded")
        f_loaded = sem("f_loaded")
        b_loaded = sem("b_loaded")
        out_stored = sem("out_stored")
        h_upd = sem("h_upd")
        sq_done = sem("sq_done")
        x_hi = sem("x_hi")
        x_lo = sem("x_lo")
        acc_done = sem("acc_done")
        st_done = sem("st_done")
        ln_done = sem("ln_done")
        r_done = sem("r_done")
        lnc_done, rc_done = sem("lnc_done"), sem("rc_done")
        in0_z = sem("in0_z")
        f1_done = sem("f1_done")
        f1_out = sem("f1_out")
        f2_done = sem("f2_done")
        na_s, na_add, na_mn, na_exp, na_rr, na_p, na_t, na_pt, na_pv = [
            sem(f"na_{x}") for x in ("s", "add", "mn", "exp", "rr", "p", "t", "pt", "pv")]
        y0_hi, y0_lo = sem("y0_hi"), sem("y0_lo")
        b2_sel = sem("b2_sel")
        m_sq, m_acc, m_st, m_ln, m_r, m_hi, m_done = [
            sem(f"m_{x}") for x in ("sq", "acc", "st", "ln", "r", "hi", "done")]
        kv_out = sem("kv_out")
        q_out = sem("q_out")
        xa_s, xa_mx, xa_nm, xa_exp, xa_rr, xa_p, xa_t, xa_pt, xa_pv, xa_hi, xa_lo = [
            sem(f"xa_{x}") for x in ("s", "mx", "nm", "exp", "rr", "p", "t", "pt", "pv", "hi", "lo")]
        ffn_dve = sem("ffn_dve")
        ffn_act = sem("ffn_act")
        cm_dve = sem("cm_dve")
        cm_act = sem("cm_act")
        pad_zero = sem("pad_zero")
        pad_d = sem("pad_d")

        t_loaded = sem("t_loaded")
        l_loaded = sem("l_loaded")
        rqk_out, rv_out, rot_done, rot_out = [sem(x) for x in ("rqk_out", "rv_out", "rot_done", "rot_out")]
        ret_s, ret_sc, ret_dec, ret_o, ret_sq, ret_v, ret_ln, ret_rn, ret_ro = [
            sem(f"ret_{x}") for x in ("s", "sc", "dec", "o", "sq", "v", "ln", "rn", "ro")]
        rg_dve, rg_act, gr_dve, gr_act, rb_dve = [sem(x) for x in ("rg_dve", "rg_act", "gr_dve", "gr_act", "rb_dve")]
        ab_dve, ab_act, ab_t = sem("ab_dve"), sem("ab_act"), sem("ab_t")
        dq_dve, dq_act = sem("dq_dve"), sem("dq_act")
        l2_sq, l2_st, l2_ln, l2_r, l2_n = [sem(f"l2_{x}") for x in ("sq", "st", "ln", "r", "n")]
        dp_tr, dp_eg, dp_lt, dp_a, dp_dve, dp_kv, dp_late = [
            sem(f"dp_{x}") for x in ("tr", "eg", "lt", "a", "dve", "kv", "late")]
        lv_pe, lv_dve = sem("lv_pe"), sem("lv_dve")
        sc_ks, sc_vn, sc_su, sc_o, sc_y, sc_s, sc_vc = [sem(f"sc_{x}") for x in ("ks", "vn", "su", "o", "y", "s", "vc")]
        do_sq, do_st, do_ln, do_r, do_n = [sem(f"do_{x}") for x in ("sq", "st", "ln", "r", "n")]
        h_saved = sem("h_saved")
        h_back = sem("h_back")
        rows_saved = sem("rows_saved")
        gb_loaded = sem("gb_loaded")
        ga_dve, ga_act, dz_dve, dz_act, dn_dve, dn_act = [
            sem(x) for x in ("ga_dve", "ga_act", "dz_dve", "dz_act", "dn_dve", "dn_act")]
        up2_dve, up2_act = sem("up2_dve"), sem("up2_act")
        fin_dve = sem("fin_dve")
        g12_done = sem("g12_done")
        sq2_done, acc2_done = sem("sq2_done"), sem("acc2_done")
        bn_dve, bn_act = sem("bn_dve"), sem("bn_act")

        RPS = ["out0", "wo0", "down0", "out1", "wo1", "down1", "wo2", "down2"]
        rp_index = {n: i for i, n in enumerate(RPS)}
        gain_after = {"out0": "xa0", "wo0": "ffn0", "down0": "mix1", "out1": "xa1", "wo1": "ffn1", "down1": None,
                      "wo2": "ffn2", "down2": "final2"}
        norm_of = {"in0": 0, "q0": 1, "up0": 2, "in1": 3, "q1": 4, "up1": 5,
                   "rqk": 6, "up2": 7, "final": 8}
        FD = 10
        FA = 3
        FD2, FA2 = 15, 2

        def pair_step(p, k):
            return 3 * p + k if k <= 3 else 6 + 4 * p + k - 3

        rows_dram = nc.dram_tensor("rows_dram", (2, DN_H, T), F32, kind="Internal").ap()
        h_dram = nc.dram_tensor("h_dram", (P, KT * T), F32, kind="Internal").ap()
        def gain_of(name, c):
            return sm[:, 100 + c:101 + c] if name is None else pcol(name, c)

        def pair_banks(q):
            return lambda p: 4 * (1 - p) if q == 0 else 4 * p

        block = ctx.enter_context(nc.Block())

        @block.sync
        def _(sp):
            def load(mat, k, c_of, slot, freed):
                for s, v in freed:
                    sp.wait_ge(s, v)
                view = mat.rearrange("(k p) n -> p k n", p=P)
                at_col = 0
                for c, width in c_of:
                    sp.dma_start(w_raw[:, slot, :, at_col:at_col + width],
                                 view[:, 2 * k:2 * k + 2, c if isinstance(c, slice) else bass.ds(c, width)]
                                 ).then_inc(w_loaded[slot], 16)
                    at_col += width

            xv = ins["xT"].rearrange("(k p) t -> p k t", p=P)
            sp.dma_start(par[:, :], ins["params"]).then_inc(c_loaded, 16)
            for name, mat, nk, groups in phases:
                u0, per = first[name], nk // 2
                if name == "rqk":
                    sp.wait_ge(h_upd, KT * (rp_index["wo1"] + 1))
                    for tab, src in ((COS, "rot_cos"), (SIN, "rot_sin"), (AGE, "age")):
                        sp.dma_start(tab[:, :], ins[src]).then_inc(t_loaded, 16)
                if name == "dab":
                    u = u0
                    sp.wait_ge(lo_done, u - RING + 1)
                    view = mat.rearrange("(k p) n -> p k n", p=P)
                    dst = w_raw[:, u % RING, :, :].rearrange("p a (b c) -> p (a b) c", c=P)
                    at_col = 0
                    for c, width in groups[0]:
                        sp.dma_start(dst[:, :, at_col:at_col + width], view[:, :, c:c + width]
                                     ).then_inc(w_loaded[u % RING], 16)
                        at_col += width
                    sp.wait_ge(rg_dve, 6)
                    sp.dma_start(LVM[:, :, :], ins["levels"]).then_inc(l_loaded, 16)
                    continue
                if name == "rv":
                    sp.wait_ge(bn_dve, 4 + KT)
                    sp.dma_start(h_dram, H[:, :, :].rearrange("p k t -> p (k t)")).then_inc(h_saved, 16)
                for g in range(1 if name.startswith("up") else len(groups)):
                    if name == "wo2" and g == 1:
                        sp.wait_ge(dn_dve, 4)
                        sp.wait_ge(h_saved, 16)
                        sp.dma_start(H[:, :, :].rearrange("p k t -> p (k t)"), h_dram).then_inc(h_back, 16)
                    for k in range(per):
                        u = u0 + g * per + k
                        freed = [(lo_done, u - RING + 1)] if u >= RING else []
                        load(mat, k, groups[g], u % RING, freed)
                        if name == "out0" and (g, k) == (0, per - 1):
                            sp.wait_ge(f1_done, 8)
                            mv = ins["memT"].rearrange("(k p) t -> p k t", p=P)
                            sp.dma_start(M[:, :, :], mv).then_inc(m_loaded, 16)
                        if u < KT // 2:
                            sp.dma_start(H[:, 2 * u:2 * u + 2, :], xv[:, 2 * u:2 * u + 2, :]).then_inc(x_loaded[u], 16)
                        if u == 0:
                            sp.dma_start(cst[:, :, :], ins["consts"]).then_inc(c_loaded, 16)
                    if name == "in0" and g == 1:
                        sp.dma_start(FC[:, :, :, :], ins["fourier_seq"]).then_inc(f_loaded, 16)
                        sp.dma_start(GC[:, :], ins["fourier_grp"]).then_inc(f_loaded, 16)
                        rp = ins["rpb"]
                        for h in range(NA_H):
                            for i in range(2):
                                src = bass.AP(rp.tensor, (h * 15 + i) * RPB_PW, [[1, GRID_W], [RPB_PW, NA_ROWS], [1, GRID_W]])
                                sp.dma_start(B2[GRID_W * i:GRID_W * (i + 1), h, :, :], src).then_inc(b_loaded, 16)
                if name.startswith("up"):
                    with sp.Fori(1, len(groups)) as i:
                        for k in range(per):
                            load(mat, k, [(groups[0][q][0] + i * 256, 256) for q in range(2)],
                                 (u0 + k) % RING, [(lo_done, i * per + (u0 + k - RING + 1))])
            ov = out.rearrange("(k p) t -> p k t", p=P)
            for k in range(KT):
                sp.wait_ge(fin_dve, k + 1)
                sp.dma_start(ov[:, k, :], H[:, k, :]).then_inc(out_stored, 16)
            sp.wait_ge(out_stored, 16 * KT)

        @block.gpsimd
        def _(pool):
            nc.gpsimd.memset(eps_c[:, 0:1], EPS)
            nc.gpsimd.memset(eps_c[:, 1:2], GN_EPS).then_inc(pad_zero, 1)

            def lo(u, slot):
                pool.wait_ge(hi_done, u + 1)
                nc.gpsimd.tensor_tensor(w_lo[:, slot % LO_RING, :, :], w_raw[:, slot, :, :],
                                        w_hi[:, slot, :, :].bitcast(F32), ALU.subtract).then_inc(lo_done, 1)

            early = 4 * RING
            for u in range(early):
                if u >= LO_RING:
                    pool.wait_ge(w_used, u - LO_RING + 1)
                lo(u, u % RING)
            pool.wait_ge(b_loaded, 16 * 2 * NA_H)
            n = 0
            for i in range(2):
                half = B2[GRID_W * i:GRID_W * (i + 1), :, :, :].rearrange("p h s c -> p (h s) c")
                lowc = half[:, :, 0:GRID_W - NA_KW]
                nc.gpsimd.affine_select(out=lowc, in_=lowc, compare_op=ALU.is_ge, fill=-1e30,
                                        base=NA_KW // 2 - (GRID_W - 1),
                                        pattern=[[0, NA_H * NA_ROWS], [1, GRID_W - NA_KW]],
                                        channel_multiplier=1).then_inc(b2_sel, 1)
                n += 1
                pool.wait_ge(b2_sel, n)
                high = half[:, :, NA_KW:GRID_W]
                nc.gpsimd.affine_select(out=high, in_=high, compare_op=ALU.is_ge, fill=-1e30,
                                        base=NA_KW // 2 - 1 - NA_KW + GRID_W - 1,
                                        pattern=[[0, NA_H * NA_ROWS], [-1, GRID_W - NA_KW]],
                                        channel_multiplier=-1).then_inc(b2_sel, 1)
                n += 1
                pool.wait_ge(b2_sel, n)
            whole = n_units // RING
            with pool.Fori(early // RING, whole) as i:
                for s in range(RING):
                    pool.wait_ge(w_used, i * RING + (s - LO_RING + 1))
                    lo(i * RING + s, s)
            for u in range(whole * RING, n_units):
                pool.wait_ge(w_used, u - LO_RING + 1)
                lo(u, u % RING)

        @block.scalar
        def _(act):
            state = {"split": 0}

            def split(u, slot, loaded):
                act.wait_ge(w_loaded[slot], loaded)
                nc.scalar.activation(w_hi[:, slot, :, :], w_raw[:, slot, :, :], ACT.Copy).then_inc(hi_done, 1)

            def split_to(end):
                while state["split"] < min(end, n_units):
                    u = state["split"]
                    if u >= RING:
                        act.wait_ge(w_used, u - RING + 1)
                    split(u, u % RING, load_value[u])
                    state["split"] += 1

            def norm_inputs(j, c, gain):
                nc.scalar.activation(ACC[:, :] if c == 0 else SQ[:, :], H[:, c, :], ACT.Square).then_inc(sq_done, 1)
                if gain is None:
                    if c >= 2:
                        act.wait_ge(acc2_done, c - 1)
                    nc.scalar.activation(ACC2[:, :] if c == 0 else SQ2[:, :], H[:, c, :], ACT.Square,
                                         scale=pcol("final1", c)).then_inc(sq2_done, 1)
                if gain == "final2":
                    return
                nc.scalar.activation(XH[:, c, :], H[:, c, :], ACT.Copy, scale=gain_of(gain, c)).then_inc(x_hi, 1)

            def residual(name):
                j = rp_index[name]
                for g in range(2):
                    split_to(first[name] + count[name] // 2 * (g + 1) + RING)
                    for c in range(4 * g, 4 * g + 4):
                        act.wait_ge(h_upd, KT * j + c + 1)
                        if c >= 2:
                            act.wait_ge(acc_done, 7 * (j + 1) + c - 1)
                        norm_inputs(j + 1, c, gain_after[name])

            def rms(name, columns=False):
                n = norm_of[name]
                if name in first:
                    split_to(first[name] + (1 if name.startswith("up") else 3) + RING)
                bank = STAT_BANK
                act.wait_ge(st_done, n + 1)
                if name in BY_TOKEN:
                    nc.scalar.activation(LNC[:, :], ps[:, bank + 1, 0:NCH], ACT.Ln, bias=eps_c[:, 0:1]).then_inc(lnc_done, 1)
                nc.scalar.activation(LNT[:, :], ps[:, bank, :], ACT.Ln, bias=eps_c[:, 0:1]).then_inc(ln_done, 1)
                act.wait_ge(ln_done, n + 1)
                nc.scalar.activation(R[:, :], LNT[:, :], ACT.Exp, scale=-0.5).then_inc(r_done, 1)
                if name in BY_TOKEN:
                    act.wait_ge(lnc_done, BY_TOKEN.index(name) + 1)
                    nc.scalar.activation(RC[:, :], LNC[:, :], ACT.Exp, scale=-0.5).then_inc(rc_done, 1)

            act.wait_ge(pad_zero, 1)
            nc.scalar.activation(sm[:, 127:128], eps_c[:, 0:1], ACT.Square)
            split_to(1)
            act.wait_ge(c_loaded, 32)
            for c in range(KT):
                act.wait_ge(x_loaded[c // 2], 16)
                if c >= 2:
                    act.wait_ge(acc_done, c - 1)
                norm_inputs(0, c, "mix0")
                if c % 2:
                    split_to(min(c // 2 + 2, RING))
            rms("in0")
            split_to(first["in0"] + count["in0"] + RING)

            for b in range(8):
                act.wait_ge(f1_done, b + 1)
                nc.scalar.activation(ZC[:, b * T:(b + 1) * T], ps[:, b, :], ACT.Copy).then_inc(f1_out, 1)
            for g in range(NA_H):
                act.wait_ge(f2_done, g + 1)
                nc.scalar.activation(YH[:, g, :], ps[:, g, :], ACT.Copy).then_inc(y0_hi, 1)

            def na_e(i):
                act.wait_ge(na_mn, i + 1)
                if i >= 2:
                    act.wait_ge(na_t, i - 1)
                nc.scalar.activation(PR[:, i % 2, :], S[:, i % 2, :], ACT.Exp, bias=sm[:, i:i + 1], scale=-1.0,
                                     accum_out=sm[:, 16 + i:17 + i]).then_inc(na_exp, 1)

            def na_out(h):
                act.wait_ge(na_pv, h + 1)
                nc.scalar.activation(YH[:, NA_H + h, :].rearrange("p (t q) -> p t q", q=P), backwards(ps[:, h, :]),
                                     ACT.Copy).then_inc(y0_hi, 1)

            na_e(0)
            for i in range(16):
                if i + 1 < 16:
                    na_e(i + 1)
                h, t = i // 4, i % 4
                act.wait_ge(na_t, i + 1)
                if h >= 2:
                    act.wait_ge(na_pv, h - 1)
                nc.scalar.activation(PT[:, h % 2, :, t * P:(t + 1) * P],
                                     ps[:, 6 + i % 2, :].rearrange("p (k q) -> p k q", k=NCH),
                                     ACT.Copy).then_inc(na_pt, 1)
                if t == 0 and h >= 1:
                    na_out(h - 1)
            act.wait_ge(m_loaded, 16)
            act.wait_ge(na_s, 16)
            nc.scalar.activation(MSQ[:, :, :], M[:, :, :], ACT.Square).then_inc(m_sq, 1)
            na_out(NA_H - 1)

            def kv_evac(l):
                u0 = first[f"kv{l}"]
                for g in range(4):
                    split_to(u0 + 4 * g + 4 + RING)
                    act.wait_ge(w_used, u0 + 4 * g + 4)
                    b = 4 * (g % 2)
                    if g < 2:
                        nc.scalar.activation(KX[:, 4 * g:4 * g + 4, :], ps[:, b:b + 4, 0:NMEM], ACT.Copy).then_inc(kv_out, 1)
                    else:
                        nc.scalar.activation(VX[:, :, (g - 2) * T:(g - 1) * T], ps[:, b:b + 2, :], ACT.Copy).then_inc(kv_out, 1)

            def cross(l):
                def xe(h):
                    n = 4 * l + h
                    act.wait_ge(xa_nm, n + 1)
                    if h >= 2:
                        act.wait_ge(xa_t, n - 1)
                    for t in range(NCH):
                        b = 2 * (h % 2) + t // 2
                        nc.scalar.activation(PX[:, h % 2, t, :], ps[:, b, (t % 2) * NMEM:(t % 2 + 1) * NMEM],
                                             ACT.Exp, bias=sm[:, 48 + 4 * (h % 2) + t:49 + 4 * (h % 2) + t],
                                             scale=SCALE_X,
                                             accum_out=sm[:, 56 + 4 * (h % 2) + t:57 + 4 * (h % 2) + t]
                                             ).then_inc(xa_exp, 1)
                def out_hi(h):
                    act.wait_ge(xa_pv, 4 * l + h + 1)
                    b = 4 + 2 * (h % 2)
                    nc.scalar.activation(YH[:, 2 * h:2 * h + 2, :], ps[:, b:b + 2, :], ACT.Copy).then_inc(xa_hi, 1)

                def probs_t(h):
                    act.wait_ge(xa_t, 4 * l + h + 1)
                    if h >= 2:
                        act.wait_ge(xa_pv, 4 * l + h - 1)
                    b = 4 + 2 * (h % 2)
                    nc.scalar.activation(PTX[:, h % 2, :, :], ps[:, b:b + 2, :], ACT.Copy).then_inc(xa_pt, 1)

                for step, h in ((xe, 0), (xe, 1), (probs_t, 0), (xe, 2), (probs_t, 1), (xe, 3), (out_hi, 0), (out_hi, 1),
                                (probs_t, 2), (probs_t, 3), (out_hi, 2), (out_hi, 3)):
                    step(h)

            def ffn(l):
                name = f"up{l}"
                u0, ng = first[name], FF1 // 256
                nd = FD * ng * l

                def group(g, inner):
                    if inner:
                        for k in range(1, 5):
                            act.wait_ge(w_used, g * 4 + (u0 + k + 1))
                            split(g * 4 + (u0 + 4 + k), (u0 + k) % RING, g * 32 + load_value[u0 + 4 + k])
                    for q in range(2):
                        act.wait_ge(ffn_dve, g * FD + (nd + 6 + q))
                        act_bar()
                        nc.scalar.activation(EG[:, q, :], CV[:, q, :], ACT.Gelu,
                                             bias=par[:, bass.ds(g * 2 + (PARAM_COLS[f"ffn_b{l}"][0] + q), 1)]
                                             ).then_inc(ffn_act, 1)
                    act.wait_ge(ffn_dve, g * FD + (nd + 9))
                    act_bar()
                    nc.scalar.activation(HID[:, bass.ds(g * 2, 2), :], HF[:, :, :], ACT.Copy).then_inc(ffn_act, 1)

                def act_bar():
                    act.wait_ge(c_loaded, 32)

                with act.Fori(0, ng - 2) as g:
                    group(g, True)
                state["split"] = u0 + 4 * ng - 3
                split_to(u0 + 4 * ng + 1)
                group(ng - 2, False)
                split_to(u0 + 4 * ng + RING)
                group(ng - 1, False)

            def conv_mixer():
                u0 = first["in1"]
                for q in range(2):
                    for g in range(3):
                        split_to(u0 + 4 * (3 * q + g + 1) + RING)
                    act.wait_ge(cm_dve, 18 * q + 17)
                    nc.scalar.activation(YH[:, 4 * q:4 * q + 4, :], TY[:, :, :], ACT.Copy).then_inc(cm_act, 1)

            split_to(first["out0"] + 3 + RING)
            act.wait_ge(m_st, 1)
            nc.scalar.activation(MLN[:, :], ps[:, MEM_BANK, 0:NMEM], ACT.Ln, bias=eps_c[:, 0:1]).then_inc(m_ln, 1)
            act.wait_ge(m_ln, 1)
            nc.scalar.activation(MR[:, :], MLN[:, :], ACT.Exp, scale=-0.5).then_inc(m_r, 1)
            act.wait_ge(m_done, 1)
            nc.scalar.activation(MH[:, :, :], M[:, :, :], ACT.Copy).then_inc(m_hi, 1)
            residual("out0")
            for l in range(2):
                if l == 1:
                    rms("in1")
                    conv_mixer()
                    residual("out1")
                kv_evac(l)
                rms(f"q{l}")
                split_to(first[f"q{l}"] + count[f"q{l}"] + RING)
                cross(l)
                residual(f"wo{l}")
                rms(f"up{l}")
                ffn(l)
                if l == 1:
                    act.wait_ge(g12_done, 1)
                residual(f"down{l}")

            def retention():
                def decay(h):
                    if h >= 2:
                        act.wait_ge(ret_sc, 4 * (h - 1))
                    nc.scalar.activation(DEC[:, h % 2, :], AGE[:, :], ACT.Exp, scale=LOG_GAMMA[h]).then_inc(ret_dec, 1)
                half = P // 4
                for b, x in enumerate((RQ, RK)):
                    split_to(first["rqk"] + 4 * (b + 1) + RING)
                    act.wait_ge(rqk_out, b + 1)
                    if b:
                        act.wait_ge(rot_out, 3)
                    for i in range(4):
                        o = i ^ 1
                        moved = nc.scalar.activation(RT[o * half:(o + 1) * half, :, :], x[i * half:(i + 1) * half, :, :],
                                                     ACT.Copy, scale=-1.0 if i % 2 else 1.0)
                    moved.then_inc(rot_done, 1)
                split_to(first["rv"] + 4 + RING)
                act.wait_ge(t_loaded, 48)
                decay(0)
                decay(1)
                for g in range(2):
                    split_to(first["rgate"] + 4 * (g + 1) + RING)
                    act.wait_ge(rg_dve, g + 1)
                    nc.scalar.activation(RG[:, 4 * g:4 * g + 4, :], RG[:, 4 * g:4 * g + 4, :], ACT.Silu).then_inc(rg_act, 1)
                for h in range(RET_H):
                    act.wait_ge(ret_o, h + 1)
                    if h >= 1:
                        act.wait_ge(ret_v, h)
                    nc.scalar.activation(RSQ[:, :], ps[:, 6 + h % 2, :], ACT.Square).then_inc(ret_sq, 1)
                    if h + 2 < RET_H:
                        decay(h + 2)
                    act.wait_ge(ret_v, h + 1)
                    nc.scalar.activation(RLN[:, :], ps[:, 3 * (h % 2) + 1, :], ACT.Ln, scale=float(D) / P,
                                         bias=eps_c[:, 1:2]).then_inc(ret_ln, 1)
                    act.wait_ge(ret_ln, h + 1)
                    if h >= 1:
                        act.wait_ge(ret_ro, h)
                    nc.scalar.activation(RN[:, :], RLN[:, :], ACT.Exp, scale=-0.5).then_inc(ret_rn, 1)

            def decay_rows():
                B1, A1, A3, SPR, BEG, EGL, EG8 = [rows[i][:, :] for i in (0, 1, 2, 3, 4, 5, 6)]
                act.wait_ge(ab_dve, 1)
                nc.scalar.activation(BR[:, :], B1, ACT.Sigmoid).then_inc(ab_act, 1)
                act.wait_ge(ab_dve, 3)
                nc.scalar.activation(A3, A1, ACT.Abs).then_inc(ab_act, 1)
                act.wait_ge(ab_act, 2)
                nc.scalar.activation(A3, A3, ACT.Exp, scale=-1.0).then_inc(ab_act, 1)
                act.wait_ge(ab_act, 3)
                nc.scalar.activation(A3, A3, ACT.Ln, bias=1.0).then_inc(ab_act, 1)
                nc.scalar.activation(sm[0:DN_H, 80:81], pcol("a_log")[0:DN_H, :], ACT.Exp).then_inc(ab_act, 1)
                act.wait_ge(ab_dve, 9)
                nc.scalar.activation(EG8, GR[:, :], ACT.Exp).then_inc(ab_act, 1)
                act.wait_ge(ab_dve, 14)
                nc.scalar.activation(EGL, EGL, ACT.Exp).then_inc(ab_act, 1)
                nc.scalar.dma_start(rows_dram[0], GR[:, :]).then_inc(rows_saved, 16)
                nc.scalar.dma_start(rows_dram[1], BR[:, :]).then_inc(rows_saved, 16)
                act.wait_ge(ab_t, 1)
                nc.scalar.activation(TC[:, :, :, :], ps[:, 1, 0:4 * NCH * DN_H].rearrange("p (a n h) -> p a n h", a=4, n=NCH),
                                     ACT.Copy).then_inc(ab_act, 1)

            def spread(i):
                act.wait_ge(rows_saved, 32)
                src = bass.AP(rows_dram.tensor, 2 * i * T, [[0, P], [DN_H * T, 2], [T, 2], [1, T]])
                nc.scalar.dma_start(GB[:, :, :, :], src).then_inc(gb_loaded, 16)

            def delta(q):
                u0 = first[f"dvqk{q}"]
                pb = pair_banks(q)

                def silu(i, x):
                    act.wait_ge(dq_dve, 51 * q + 17 * i + 17)
                    nc.scalar.activation(x[:, :, :], x[:, :, :], ACT.Silu).then_inc(dq_act, 1)

                def square(i, x, sq):
                    act.wait_ge(dq_act, 3 * q + i + 2)
                    nc.scalar.activation(sq[:, :, :], x[:, :, :], ACT.Square).then_inc(l2_sq, 1)

                def inverse_norm(i, ln):
                    b = 0 if q == 0 else 4
                    act.wait_ge(l2_st, 2 * q + i + 1)
                    nc.scalar.activation(ln[:, :, :], ps[:, b:b + 4, :], ACT.Ln, scale=float(D),
                                         bias=eps_c[:, 0:1]).then_inc(l2_ln, 1)
                    act.wait_ge(l2_ln, 2 * q + i + 1)
                    for part in (slice(0, 2), slice(2, 4)):
                        nc.scalar.activation(ln[:, part, :], ln[:, part, :], ACT.Exp, scale=-0.5).then_inc(l2_r, 1)

                split_to(u0 + 4 + RING)
                silu(0, VB)
                split_to(u0 + 8 + RING)
                silu(1, QN)
                square(0, QN, SQq)
                split_to(u0 + 12 + RING)
                inverse_norm(0, LNq)
                silu(2, KN)
                square(1, KN, SQk)
                split_to(u0 + 16 + RING)
                inverse_norm(1, LNk)
                for pr in range(2):
                    m = 4 * q + 2 * pr
                    n = 14 * (2 * q + pr)
                    for p in range(2):
                        act.wait_ge(gb_loaded, 16 * (2 * q + pr + 1))
                        if pr or q:
                            act.wait_ge(dp_late, 6 * (2 * q + pr))
                        nc.scalar.activation(EGA[p][:, :], GB[:, 0, p, :], ACT.Exp).then_inc(dp_eg, 1)
                        act.wait_ge(dp_dve, n + pair_step(p, 3))
                        nc.scalar.activation(DL[:, p, :], DL[:, p, :], ACT.Exp).then_inc(dp_lt, 1)
                    if 2 * q + pr < 3:
                        act.wait_ge(dp_eg, m + 2)
                        spread(2 * q + pr + 1)
                    for dst, bank, a in ((KD, 2, 3), (VB, 3, 0)):
                        for p in range(2):
                            h, hh = m + p, 2 * pr + p
                            act.wait_ge(dp_tr, m + p + 1)
                            for c in range(NCH):
                                last = nc.scalar.activation(dst[:, hh, c * P:(c + 1) * P],
                                                            ps[:, pb(p) + bank, c * P:(c + 1) * P], ACT.Copy,
                                                            scale=TC[:, a, c, h:h + 1])
                            last.then_inc(dp_kv, 1)
                for n in range(NCH):
                    for hh in range(4):
                        act.wait_ge(sc_vn, 16 * q + 4 * n + hh + 1)
                        nc.scalar.activation(VS[:, hh, :], ps[:, hh, P:2 * P], ACT.Copy).then_inc(sc_vc, 1)
                act.wait_ge(sc_o, q + 1)
                nc.scalar.activation(SQo[:, :, :], ps[:, 4:8, :], ACT.Square).then_inc(do_sq, 1)
                nc.scalar.activation(DO[:, 4 * q:4 * q + 4, :], ps[:, 4:8, :], ACT.Copy).then_inc(do_sq, 1)
                split_to(first["dvqk1" if q == 0 else "dz"] + 3 + RING)
                act.wait_ge(do_st, q + 1)
                nc.scalar.activation(LNo[:, :, :], ps[:, 4:8, :], ACT.Ln, scale=float(D) / P,
                                     bias=eps_c[:, 0:1]).then_inc(do_ln, 1)
                act.wait_ge(do_ln, q + 1)
                nc.scalar.activation(LNo[:, :, :], LNo[:, :, :], ACT.Exp, scale=-0.5).then_inc(do_r, 1)

            def ffn2():
                u0, ng = first["up2"], FF2 // 256

                def group(g, inner):
                    if inner:
                        for k in range(1, 5):
                            act.wait_ge(w_used, g * 4 + (u0 + k + 1))
                            split(g * 4 + (u0 + 4 + k), (u0 + k) % RING, g * 32 + load_value[u0 + 4 + k])
                    act.wait_ge(up2_dve, g * FD2 + 11)
                    nc.scalar.activation(SA[:, :, :], CV4[:, 0:2, :], ACT.Silu).then_inc(up2_act, 1)
                    act.wait_ge(up2_dve, g * FD2 + 14)
                    act.wait_ge(c_loaded, 32)
                    nc.scalar.activation(HID[:, bass.ds(g * 2, 2), :], HF2[:, :, :], ACT.Copy).then_inc(up2_act, 1)

                with act.Fori(0, ng - 2) as g:
                    group(g, True)
                state["split"] = u0 + 4 * ng - 3
                split_to(u0 + 4 * ng + 1)
                group(ng - 2, False)
                split_to(u0 + 4 * ng + RING)
                group(ng - 1, False)

            def block2():
                rms("rqk")
                for i, (dst, src) in enumerate(((LNT[:, :], SQ[:, :]), (LNC[:, :], sm[:, 108:112]))):
                    act.wait_ge(bn_dve, 2 * i + 2)
                    act.wait_ge(r_done, norm_of["rqk"] + 1)
                    act.wait_ge(rc_done, 2)
                    nc.scalar.activation(dst, src, ACT.Ln, bias=eps_c[:, 0:1]).then_inc(bn_act, 1)
                for i, (dst, src) in enumerate(((SQ[:, :], LNT[:, :]), (sm[:, 108:112], LNC[:, :]))):
                    act.wait_ge(bn_act, i + 1)
                    nc.scalar.activation(dst, src, ACT.Exp, scale=-0.5).then_inc(bn_act, 1)
                retention()
                for g in range(2):
                    act.wait_ge(rg_dve, 2 * g + 3)
                    nc.scalar.activation(YH[:, 4 * g:4 * g + 4, :], TG[:, 4 * g:4 * g + 4, :], ACT.Copy).then_inc(rg_act, 1)
                for g in range(2):
                    split_to(first["gater"] + 4 * (g + 1) + RING)
                    act.wait_ge(gr_dve, g + 1)
                    nc.scalar.activation(MG[:, 4 * g:4 * g + 4, :], MG[:, 4 * g:4 * g + 4, :],
                                         ACT.Sigmoid).then_inc(gr_act, 1)
                split_to(first["dab"] + 1 + RING)
                decay_rows()
                spread(0)
                delta(0)
                delta(1)
                for g in range(2):
                    split_to(first["dz"] + 4 * (g + 1) + RING)
                    act.wait_ge(dz_dve, 3 * g + 1)
                    nc.scalar.activation(TZ[:, :, :], TZ[:, :, :], ACT.Silu).then_inc(dz_act, 1)
                    act.wait_ge(dz_dve, 3 * g + 2)
                    nc.scalar.activation(YH[:, 4 * g:4 * g + 4, :], DO[:, 4 * g:4 * g + 4, :], ACT.Copy).then_inc(dz_act, 1)
                for g in range(2):
                    act.wait_ge(ga_dve, g + 1)
                    nc.scalar.activation(SGD[:, 4 * g:4 * g + 4, :], SGD[:, 4 * g:4 * g + 4, :],
                                         ACT.Sigmoid).then_inc(ga_act, 1)
                for g in range(2):
                    split_to(first["dnbr"] + 4 * (g + 1) + RING)
                    act.wait_ge(dn_dve, 3 * g + 2)
                    nc.scalar.activation(NH[:, 4 * g:4 * g + 4, :], MG[:, 4 * g:4 * g + 4, :], ACT.Copy).then_inc(dn_act, 1)
                residual("wo2")
                rms("up2")
                ffn2()
                residual("down2")
                rms("final")

            block2()

        @block.tensor
        def _(pe):
            def products(u, slot, k, bank, x_hi_t, x_lo_t, tokens_out, start, stop):
                pe.wait_ge(lo_done, u + 1)
                for m in range(4):
                    for j in range(2):
                        kt = 2 * k + j
                        for n in range(3):
                            wt = w_lo[:, slot % LO_RING, j, :] if n == 2 else w_hi[:, slot, j, :]
                            xt = x_lo_t[:, kt, :] if n == 1 else x_hi_t[:, kt, :]
                            if tokens_out:
                                a, b = xt[:, m * P:(m + 1) * P], wt
                            else:
                                a, b = wt[:, m * P:(m + 1) * P], xt
                            mm = nc.tensor.matmul(ps[:, bank + m, :], a, b, start=start and j == 0 and n == 0,
                                                  stop=stop and j == 1 and n == 2)
                mm.then_inc(w_used, 1)

            def group(u0, units, bank, xh, xl, ready=None, tokens_out=False, after=None):
                for k in range(units):
                    if ready is not None:
                        for kt in (2 * k, 2 * k + 1):
                            for s, v in ready(kt):
                                pe.wait_ge(s, v)
                    products(u0 + k, (u0 + k) % RING, k, bank, xh, xl, tokens_out, k == 0, k == units - 1)
                    if after is not None and k == 2:
                        after()

            def stats(name, freed=()):
                n = norm_of[name]

                def emit():
                    for s, v in freed:
                        pe.wait_ge(s, v)
                    pe.wait_ge(acc_done, 7 * (n + 1))
                    mm = nc.tensor.matmul(ps[:, STAT_BANK, :], ones, ACC[:, :], start=True, stop=True)
                    for t in range(NCH if name in BY_TOKEN else 0):
                        mm = nc.tensor.matmul(ps[:, STAT_BANK + 1, t:t + 1], ACC[:, t * P:(t + 1) * P], ones[:, 0:1],
                                              start=True, stop=True)
                    if name == "rqk":
                        pe.wait_ge(acc2_done, 7)
                        nc.tensor.matmul(ps[:, STAT_BANK + 2, :], ones, ACC2[:, :], start=True, stop=True)
                        for t in range(NCH):
                            mm = nc.tensor.matmul(ps[:, STAT_BANK + 1, NCH + t:NCH + t + 1], ACC2[:, t * P:(t + 1) * P],
                                                  ones[:, 0:1], start=True, stop=True)
                    mm.then_inc(st_done, 1)
                return emit

            def x_ready(name):
                before = {"up0": "wo0", "up1": "wo1", "up2": "wo2", "in1": "down0", "rqk": "down1"}.get(name)
                first_half = [(h_upd, KT * rp_index[before] + 4)] if before else []
                return lambda kt: (first_half if kt == 0 else []) + [(x_lo, KT * norm_of[name] + kt + 1)]

            def stat_read(name):
                pe.wait_ge(ln_done, norm_of[name] + 1)

            pe.wait_ge(c_loaded, 32)
            u0 = first["in0"]
            group(u0, 4, 0, XH, XL, x_ready("in0"), after=stats("in0"))
            stat_read("in0")
            group(u0 + 4, 4, 4, XH, XL)
            pe.wait_ge(in0_z, 1)
            group(u0 + 8, 4, 0, XH, XL)
            pe.wait_ge(in0_z, 2)
            group(u0 + 12, 4, 4, XH, XL, tokens_out=True)
            pe.wait_ge(f_loaded, 32)
            pe.wait_ge(in0_z, 3)
            for g in range(NA_H):
                if g == 2:
                    pe.wait_ge(in0_z, 7)
                for t in range(NCH):
                    i = g * NCH + t
                    mm = nc.tensor.matmul(ps[:, i // 2, (i % 2) * 256:(i % 2 + 1) * 256],
                                          Z[:, g, t * P:(t + 1) * P], GC[:, :], start=True, stop=True)
                    if i % 2:
                        mm.then_inc(f1_done, 1)
            for g in range(NA_H):
                pe.wait_ge(f1_out, 2 * g + 2)
                for t in range(NCH):
                    for cs in range(2):
                        a = ((g * NCH + t) * 2 + cs) * P
                        mm = nc.tensor.matmul(ps[:, g, :], ZC[:, a:a + P], FC[:, t, cs, :],
                                              start=t == 0 and cs == 0, stop=t == NCH - 1 and cs == 1)
                mm.then_inc(f2_done, 1)

            def scores(i):
                h, t = i // 4, i % 4
                if i >= 2:
                    pe.wait_ge(na_add, i - 1)
                nc.tensor.matmul(ps[:, 4 + i % 2, :], Q[:, h, t * P:(t + 1) * P], K[:, h, :],
                                 start=True, stop=True).then_inc(na_s, 1)

            def values(h):
                pe.wait_ge(na_pt, 4 * h + 4)
                pe.wait_ge(y0_lo, h + 1)
                for k in range(NCH):
                    mm = nc.tensor.matmul(ps[:, h, :], V[:, k, h * P:(h + 1) * P], PT[:, h % 2, k, :],
                                          start=k == 0, stop=k == NCH - 1)
                mm.then_inc(na_pv, 1)

            pe.wait_ge(f1_out, 8)
            scores(0)
            scores(1)
            for i in range(16):
                h = i // 4
                if i + 2 < 16:
                    scores(i + 2)
                if i % 4 == 0 and i:
                    values(h - 1)
                pe.wait_ge(na_p, i + 1)
                if i >= 2:
                    pe.wait_ge(na_pt, i - 1)
                for k in range(NCH):
                    mm = nc.tensor.transpose(ps[:, 6 + i % 2, k * P:(k + 1) * P], PR[:, i % 2, k * P:(k + 1) * P], ident)
                mm.then_inc(na_t, 1)
            values(NA_H - 1)

            def residual(name, units, xh, xl, ready, after=None):
                u = first[name]
                group(u, units, 0, xh, xl, ready, after=after)
                if after is not None:
                    pe.wait_ge(m_ln, 1)
                group(u + units, units, 4, xh, xl)

            def mem_stat():
                pe.wait_ge(m_acc, 1)
                nc.tensor.matmul(ps[:, MEM_BANK, 0:NMEM], ones, MACC[:, :], start=True, stop=True).then_inc(m_st, 1)

            def kv(l):
                u0 = first[f"kv{l}"]
                rp = KT * (rp_index[f"out{l}"] + 1)
                pe.wait_ge(m_done, 2)
                for g in range(4):
                    if g < 2:
                        pe.wait_ge(h_upd, rp - 4 + 4 * g)
                    else:
                        pe.wait_ge(kv_out, 4 * l + g - 1)
                    bank = 4 * (g % 2)
                    for k in range(4):
                        u = u0 + 4 * g + k
                        s = u % RING
                        pe.wait_ge(lo_done, u + 1)
                        for m in range(4 if g < 2 else 2):
                            for j in range(2):
                                kt = 2 * k + j
                                for n in range(3):
                                    wt = w_lo[:, s % LO_RING, j, :] if n == 2 else w_hi[:, s, j, :]
                                    xt = ML[:, kt, :] if n == 1 else MH[:, kt, :]
                                    begin, end = kt == 0 and n == 0, kt == KT - 1 and n == 2
                                    if g < 2:
                                        mm = nc.tensor.matmul(ps[:, bank + m, 0:NMEM], wt[:, m * P:(m + 1) * P], xt,
                                                              start=begin, stop=end)
                                    else:
                                        mm = nc.tensor.matmul(ps[:, bank + m, :], xt[:, m * P:(m + 1) * P], wt,
                                                              start=begin, stop=end)
                        mm.then_inc(w_used, 1)

            def cross(l):
                def xs(h):
                    n = 4 * l + h
                    pe.wait_ge(q_out, 2 * l + 1 + h // 2)
                    if h >= 2:
                        pe.wait_ge(xa_exp, 4 * (n - 1))
                    for t in range(NCH):
                        for c in range(2):
                            mm = nc.tensor.matmul(ps[:, 2 * (h % 2) + t // 2, (t % 2) * NMEM:(t % 2 + 1) * NMEM],
                                                  QX[:, 2 * h + c, t * P:(t + 1) * P], KX[:, 2 * h + c, :],
                                                  start=c == 0, stop=c == 1)
                    mm.then_inc(xa_s, 1)

                def xt(h):
                    n = 4 * l + h
                    pe.wait_ge(xa_p, n + 1)
                    pe.wait_ge(q_out, 2 * l + 2)
                    if h >= 2:
                        pe.wait_ge(xa_lo, n - 1)
                    for k in range(2):
                        for t in range(NCH):
                            mm = nc.tensor.transpose(ps[:, 4 + 2 * (h % 2) + k, t * P:(t + 1) * P],
                                                     PX[:, h % 2, t, k * P:(k + 1) * P], ident)
                    mm.then_inc(xa_t, 1)

                def xv(h):
                    n = 4 * l + h
                    pe.wait_ge(xa_pt, n + 1)
                    for c in range(2):
                        for k in range(2):
                            a = h * 2 * P + c * P
                            mm = nc.tensor.matmul(ps[:, 4 + 2 * (h % 2) + c, :], VX[:, k, a:a + P], PTX[:, h % 2, k, :],
                                                  start=k == 0, stop=k == 1)
                    mm.then_inc(xa_pv, 1)

                for step, h in ((xs, 0), (xs, 1), (xs, 2), (xt, 0), (xs, 3), (xt, 1), (xv, 0), (xv, 1),
                                (xt, 2), (xt, 3), (xv, 2), (xv, 3)):
                    step(h)

            def ffn(l):
                name = f"up{l}"
                u0, ng = first[name], FF1 // 256
                nd = FD * ng * l
                group(u0, 4, 0, XH, XL, x_ready(name), after=stats(name))
                stat_read(name)
                group(u0 + 4, 4, 4, XH, XL)
                with pe.Fori(1, ng // 2) as i:
                    for g in range(2):
                        pe.wait_ge(ffn_dve, i * (2 * FD) + (nd + FD * (g - 2) + 8))
                        for k in range(4):
                            products(i * 8 + (u0 + 4 * g + k), k, k, 4 * g, XH, XL, False, k == 0, k == 3)
                u0 = first[f"down{l}"]
                nf = FF1 // P
                pe.wait_ge(ffn_dve, nd + FD * (ng - 2) + 8)
                group(u0, nf // 2, 0, HID[:, 0:nf, :], HID[:, nf:2 * nf, :],
                      lambda kt: [(ffn_dve, nd + FD * (kt // 2 + 1))])
                group(u0 + nf // 2, nf // 2, 4, HID[:, 0:nf, :], HID[:, nf:2 * nf, :])

            for l in range(2):
                if l == 0:
                    pe.wait_ge(na_pt, 16)
                    residual("out0", 4, YH, YL, lambda kt: [(y0_lo, 8)], after=mem_stat)
                else:
                    u0 = first["in1"]
                    for g in range(6):
                        if g == 0:
                            group(u0, 4, 0, XH, XL, x_ready("in1"), after=stats("in1"))
                            stat_read("in1")
                        else:
                            if g >= 2:
                                pe.wait_ge(cm_dve, 18 * ((g - 2) // 3) + (1, 2, 16)[(g - 2) % 3])
                            group(u0 + 4 * g, 4, 4 * (g % 2), XH, XL)
                    pe.wait_ge(cm_dve, 18 + 16)
                    residual("out1", 4, YH, YL, lambda kt: [(cm_dve, 18 * (kt // 4) + 18)])
                kv(l)
                pe.wait_ge(kv_out, 4 * l + 3)
                u0 = first[f"q{l}"]
                group(u0, 4, 0, XH, XL, x_ready(f"q{l}"), after=stats(f"q{l}", [(kv_out, 4 * l + 4)]))
                stat_read(f"q{l}")
                group(u0 + 4, 4, 4, XH, XL)
                cross(l)
                residual(f"wo{l}", 4, YH, YL, lambda kt: [(xa_lo, 4 * l + kt // 2 + 1)])
                ffn(l)

            def retention():
                pe.wait_ge(rv_out, 4)
                group(first["rgate"], 4, 0, XH, XL)
                pe.wait_ge(rv_out, 11)
                group(first["rgate"] + 4, 4, 4, XH, XL)

                def s(h):
                    c, r = h // 2, (h % 2) * 64
                    if h >= 2:
                        pe.wait_ge(ret_ln, h - 1)
                    for j in range(NCH):
                        w = T - j * P
                        b, o = ((0, 0), (1, 0), (2, 0), (2, 256))[j]
                        mm = nc.tensor.matmul(ps[:, 3 * (h % 2) + b, o:o + w], RK[r:r + 64, c, j * P:(j + 1) * P],
                                              RQ[r:r + 64, c, j * P:T], start=True, stop=True)
                        if j != 2:
                            mm.then_inc(ret_s, 1)

                def o(h):
                    pe.wait_ge(rv_out, 14)
                    if h >= 2:
                        pe.wait_ge(ret_ro, h - 1)
                    for j in range(NCH):
                        w = T - j * P
                        a = (0, 512, 896, 1152)[j]
                        pe.wait_ge(ret_sc, 4 * h + j + 1)
                        mm = nc.tensor.matmul(ps[:, 6 + h % 2, j * P:T], RV[:, j, h * P:(h + 1) * P],
                                              SCO[:, h % 2, a:a + w], start=j == 0, stop=j == NCH - 1)
                    mm.then_inc(ret_o, 1)

                def v(h):
                    pe.wait_ge(ret_sq, h + 1)
                    nc.tensor.matmul(ps[:, 3 * (h % 2) + 1, :], ones, RSQ[:, :], start=True, stop=True).then_inc(ret_v, 1)

                pe.wait_ge(rot_out, 6)
                pe.wait_ge(rg_dve, 1)
                s(0)
                pe.wait_ge(rg_dve, 2)
                s(1)
                for h in range(RET_H):
                    if h >= 1:
                        v(h - 1)
                    o(h)
                    if 1 <= h < RET_H - 1:
                        s(h + 1)
                v(RET_H - 1)

            def delta(q):
                u0 = first[f"dvqk{q}"]
                pb = pair_banks(q)
                bv, bq = (4, 0) if q == 0 else (0, 4)
                if q == 0:
                    pe.wait_ge(rb_dve, 2)
                group(u0, 4, bv, XH, XL, after=decay_columns if q == 0 else out_stats(0))
                if q == 0:
                    pe.wait_ge(ab_act, 8)
                else:
                    pe.wait_ge(do_ln, 1)
                group(u0 + 4, 4, bq, XH, XL)
                pe.wait_ge(dq_dve, 51 * q + 1)
                group(u0 + 8, 4, bv, XH, XL)

                def l2(i, sq):
                    pe.wait_ge(l2_sq, 2 * q + i + 1)
                    for c in range(4):
                        mm = nc.tensor.matmul(ps[:, bq + c, :], ones, sq[:, c, :], start=True, stop=True)
                    mm.then_inc(l2_st, 1)

                pe.wait_ge(dq_dve, 51 * q + 18)
                l2(0, SQq)
                pe.wait_ge(dq_dve, 51 * q + 35)
                group(first[f"gated{q}"], 4, bv, XH, XL)
                pe.wait_ge(l2_ln, 2 * q + 1)
                l2(1, SQk)
                pe.wait_ge(ga_dve, q + 1)
                pe.wait_ge(dq_act, 3 * q + 3)
                for pr in range(2):
                    m = 4 * q + 2 * pr
                    nd = 14 * (2 * q + pr)
                    nl = 34 * (2 * q + pr)
                    for p in range(2):
                        h, hh = m + p, 2 * pr + p
                        if pr == 1:
                            pe.wait_ge(lv_dve, nl)
                            pe.wait_ge(dp_late, 6 * (2 * q + 1))
                        elif p == 1:
                            pe.wait_ge(l2_ln, 2 * q + 2)
                        for n in range(NCH):
                            nc.tensor.transpose(ps[:, pb(p) + 3, n * P:(n + 1) * P], VB[:, hh, n * P:(n + 1) * P], ident)
                    pe.wait_ge(l2_n, 4 * q + 3 + pr)
                    for p in range(2):
                        hh = 2 * pr + p
                        for n in range(NCH):
                            mm = nc.tensor.transpose(ps[:, pb(p) + 2, n * P:(n + 1) * P], KN[:, hh, n * P:(n + 1) * P], ident)
                        mm.then_inc(dp_tr, 1)
                    for p in range(2):
                        hh = 2 * pr + p
                        pe.wait_ge(dp_dve, nd + pair_step(p, 1))
                        for n in range(NCH):
                            cols_ = slice(n * P, (n + 1) * P)
                            nc.tensor.matmul(ps[:, pb(p) + 1, cols_], KN[:, hh, cols_], T1[:, p, cols_], start=True, stop=True)
                            mm = nc.tensor.matmul(ps[:, pb(p), cols_], KN[:, hh, cols_], QN[:, hh, cols_], start=True, stop=True)
                        mm.then_inc(dp_a, 1)
                    for li, b in enumerate(LEVELS[1:]):
                        for p in range(2):
                            if li == 0:
                                pe.wait_ge(dp_dve, nd + pair_step(p, 7))
                                pe.wait_ge(dp_kv, 4 * (2 * q + pr) + 4)
                            else:
                                pe.wait_ge(lv_dve, nl + 6 * (li - 1) + 4 + 2 * p)
                            for n in range(NCH):
                                cols_ = slice(n * P, (n + 1) * P)
                                mm = nc.tensor.matmul(ps[:, pb(p) + 2, cols_], AT[:, p, cols_], MM[:, p, cols_],
                                                      start=True, stop=True)
                            mm.then_inc(lv_pe, 1)
                        for p in range(2):
                            hh = 2 * pr + p
                            pe.wait_ge(lv_dve, nl + 6 * li + p + 1)
                            for n in range(NCH):
                                cols_ = slice(n * P, (n + 1) * P)
                                if b == 32:
                                    nc.tensor.matmul(ps[:, pb(p) + 1, cols_], MT[:, hh, cols_], T1[:, p, cols_],
                                                     start=True, stop=True)
                                mm = nc.tensor.matmul(ps[:, pb(p) + 3, cols_], T1[:, p, cols_], MT[:, hh, cols_],
                                                      start=True, stop=True)
                            mm.then_inc(lv_pe, 1)
                pe.wait_ge(lv_dve, 34 * (2 * q + 2))
                pe.wait_ge(dp_late, 6 * (2 * q + 2))
                for n in range(NCH):
                    cols_ = slice(n * P, (n + 1) * P)
                    if n:
                        for hh in range(4):
                            pe.wait_ge(sc_s, 12 * q + 4 * (n - 1) + hh + 1)
                            nc.tensor.matmul(ps[:, hh, 0:P], KN[:, hh, cols_], SS[:, hh, :],
                                             start=True, stop=True).then_inc(sc_ks, 1)
                    for hh in range(4):
                        if n:
                            pe.wait_ge(sc_y, 12 * q + 4 * (n - 1) + hh + 1)
                            pe.wait_ge(sc_vc, 16 * q + 4 * (n - 1) + hh + 1)
                        nc.tensor.matmul(ps[:, hh, P:2 * P], MT[:, hh, cols_],
                                         YS[:, hh, :] if n else VB[:, hh, cols_], start=True, stop=True).then_inc(sc_vn, 1)
                    for hh in range(4):
                        pe.wait_ge(sc_vc, 16 * q + 4 * n + hh + 1)
                        if n:
                            nc.tensor.matmul(ps[:, 4 + hh, cols_], SS[:, hh, :], QN[:, hh, cols_], start=True, stop=False)
                        mm = nc.tensor.matmul(ps[:, 4 + hh, cols_], VS[:, hh, :], ATT[:, hh, cols_], start=n == 0, stop=True)
                        if n < NCH - 1:
                            nc.tensor.matmul(ps[:, hh, 2 * P:3 * P], KD[:, hh, cols_], VS[:, hh, :],
                                             start=True, stop=True).then_inc(sc_su, 1)
                mm.then_inc(sc_o, 1)

            def out_stats(q):
                def emit():
                    pe.wait_ge(do_sq, 2 * q + 2)
                    for c in range(4):
                        mm = nc.tensor.matmul(ps[:, 4 + c, :], ones, SQo[:, c, :], start=True, stop=True)
                    mm.then_inc(do_st, 1)
                return emit

            def decay_columns():
                pe.wait_ge(ab_act, 7)
                pe.wait_ge(ab_dve, 14)
                for a, row in enumerate((BR, GR, rows[4], rows[5])):
                    for n in range(NCH):
                        o = (a * NCH + n) * DN_H
                        mm = nc.tensor.transpose(ps[:, 1, o:o + DN_H], row[:, n * P:(n + 1) * P], ident[0:DN_H, 0:DN_H])
                mm.then_inc(ab_t, 1)

            def ffn2():
                u0, ng = first["up2"], FF2 // 256
                group(u0, 4, 0, XH, XL, x_ready("up2"), after=stats("up2"))
                stat_read("up2")
                group(u0 + 4, 4, 4, XH, XL)
                with pe.Fori(1, ng // 2) as i:
                    for g in range(2):
                        pe.wait_ge(up2_dve, i * (2 * FD2) + (FD2 * (g - 2) + 1))
                        for k in range(4):
                            products(i * 8 + (u0 + 4 * g + k), (u0 + k) % RING, k, 4 * g, XH, XL, False, k == 0, k == 3)
                pe.wait_ge(up2_dve, FD2 * (ng - 3) + 1)
                group(u0 + 4 * (ng - 1), 4, 0, XH, XL)
                u0 = first["down2"]
                nf = FF2 // P
                pe.wait_ge(up2_dve, FD2 * (ng - 2) + 1)
                ready = lambda kt: [(up2_dve, FD2 * (kt // 2 + 1))]
                group(u0, nf // 2, 4, HID[:, 0:nf, :], HID[:, nf:2 * nf, :], ready)
                group(u0 + nf // 2, nf // 2, 0, HID[:, 0:nf, :], HID[:, nf:2 * nf, :])

            def pair(name, freed, xh=XH, xl=XL, ready=None, after=None):
                for g in range(2):
                    for s, v in freed[g]:
                        pe.wait_ge(s, v)
                    group(first[name] + 4 * g, 4, 4 * g, xh, xl, ready, after=after if g == 0 else None)

            def block2():
                u0 = first["rqk"]
                group(u0, 4, 0, XH, XL, x_ready("rqk"), after=stats("rqk"))
                stat_read("rqk")
                pe.wait_ge(bn_dve, 3)
                group(u0 + 4, 4, 4, XH, XL)
                for g in range(2):
                    pe.wait_ge(rqk_out, g + 1)
                    group(first["rv"] + 4 * g, 4, 4 * g, XH, XL, tokens_out=True)
                retention()
                pair("gater", [[(ret_ln, 8)], [(ret_ro, 8)]])
                pair("retbr", [[(gr_dve, 1)], [(gr_dve, 2)]], YH, YL, lambda kt: [(rg_dve, 2 * (kt // 4) + 4)])
                u = first["dab"]
                pe.wait_ge(lo_done, u + 1)
                pe.wait_ge(rb_dve, 1)
                hi = w_hi[:, u % RING, :, :].rearrange("p a (b c) -> p (a b) c", c=P)
                lo = w_lo[:, u % RING, :, :].rearrange("p a (b c) -> p (a b) c", c=P)
                for kt in range(KT):
                    for n, (a, b) in enumerate(((hi, XH), (hi, XL), (lo, XH))):
                        mm = nc.tensor.matmul(ps[:, 0, :], a[:, kt, :], b[:, kt, :], start=kt == 0 and n == 0,
                                              stop=kt == KT - 1 and n == 2)
                mm.then_inc(w_used, 1)
                delta(0)
                delta(1)
                pair("dz", [[], [(do_ln, 2)]], after=out_stats(1))
                pair("dnbr", [[(dz_dve, 1)], [(dz_dve, 4)]], YH, YL, lambda kt: [(dz_dve, 3 * (kt // 4) + 3)])
                pair("wo2", [[(dn_dve, 1)], [(dn_dve, 4)]], NH, NL, lambda kt: [(dn_dve, 3 * (kt // 4) + 3)])
                ffn2()
                stats("final")()

            block2()

        @block.vector
        def _(dve):
            def over(ap, n):
                return ap.unsqueeze(1).broadcast_to([P, n, ap.shape[-1]])

            def add_square(j, c):
                dve.wait_ge(sq_done, KT * j + c + 1)
                if c >= 2:
                    dve.wait_ge(acc_done, 7 * j + c - 1)
                nc.vector.tensor_tensor(ACC[:, :], ACC[:, :], SQ[:, :], ALU.add).then_inc(acc_done, 1)

            def norm_inputs(j, c, gain):
                if c >= 1:
                    add_square(j, c)
                if gain is None and c >= 1:
                    dve.wait_ge(sq2_done, c + 1)
                    if c >= 2:
                        dve.wait_ge(acc2_done, c - 1)
                    nc.vector.tensor_tensor(ACC2[:, :], ACC2[:, :], SQ2[:, :], ALU.add).then_inc(acc2_done, 1)
                if gain == "final2":
                    return
                dve.wait_ge(x_hi, KT * j + c + 1)
                nc.vector.scalar_tensor_tensor(out=XL[:, c, :], in0=H[:, c, :], scalar=gain_of(gain, c),
                                               in1=XH[:, c, :].bitcast(F32), op0=ALU.mult,
                                               op1=ALU.subtract).then_inc(x_lo, 1)

            def residual(name, flip=0):
                j = rp_index[name]
                for g in range(2):
                    dve.wait_ge(w_used, first[name] + count[name] // 2 * (g + 1))
                    for c in range(4 * g, 4 * g + 4):
                        nc.vector.tensor_tensor(H[:, c, :], ps[:, (c + flip) % 8, :], H[:, c, :],
                                                ALU.add).then_inc(h_upd, 1)
                        if c > 4 * g:
                            norm_inputs(j + 1, c - 1, gain_after[name])
                    norm_inputs(j + 1, 4 * g + 3, gain_after[name])

            dve.wait_ge(c_loaded, 32)
            nc.vector.tensor_tensor(sm[:, 100:100 + KT], pcol("final1", 0, KT), pcol("mix2", 0, KT),
                                    ALU.mult).then_inc(g12_done, 1)
            for c in range(KT):
                dve.wait_ge(x_loaded[c // 2], 16)
                norm_inputs(0, c, "mix0")
            u0 = first["in0"]
            dve.wait_ge(r_done, 1)
            dve.wait_ge(rc_done, 1)
            for g, dst in enumerate((Z, Q, K)):
                dve.wait_ge(w_used, u0 + 4 * g + 4)
                b = 4 * (g % 2)
                if dst is not Q:
                    nc.vector.tensor_tensor(dst[:, :, :], ps[:, b:b + 4, :], over(R[:, :], 4), ALU.mult).then_inc(in0_z, 1)
                    continue
                for h in range(NA_H):
                    q_done = nc.vector.tensor_tensor(backwards(Q[:, h, :]), ps[:, b + h, :].rearrange("p (t q) -> p t q", q=P),
                                                     R[:, :].rearrange("p (t q) -> p t q", q=P), ALU.mult)
                q_done.then_inc(in0_z, 1)
            dve.wait_ge(w_used, u0 + 16)
            for t in range(NCH):
                nc.vector.tensor_scalar(V[:, t, :], ps[:, 4 + t, :], RC[:, t:t + 1], None, ALU.mult).then_inc(in0_z, 1)
            for g in range(NA_H):
                dve.wait_ge(y0_hi, g + 1)
                nc.vector.tensor_tensor(YL[:, g, :], ps[:, g, :], YH[:, g, :].bitcast(F32),
                                        ALU.subtract).then_inc(y0_lo, 1)

            def na_a(i):
                h, t = i // 4, i % 4
                dve.wait_ge(na_s, i + 1)
                if i >= 2:
                    dve.wait_ge(na_exp, i - 1)
                s0 = NA_KH - 2 - 2 * t
                nc.vector.scalar_tensor_tensor(out=S[:, i % 2, :], in0=ps[:, 4 + i % 2, :], scalar=-SCALE_NA,
                                               in1=B2[:, h, s0:s0 + ROWS, :].rearrange("p r c -> p (r c)"),
                                               op0=ALU.mult, op1=ALU.subtract).then_inc(na_add, 1)
                dve.wait_ge(na_add, i + 1)
                nc.vector.tensor_reduce(sm[:, i:i + 1], S[:, i % 2, :], AX.X, ALU.min).then_inc(na_mn, 1)

            def na_out(h):
                dve.wait_ge(y0_hi, NA_H + h + 1)
                nc.vector.tensor_tensor(YL[:, NA_H + h, :].rearrange("p (t q) -> p t q", q=P), backwards(ps[:, h, :]),
                                        YH[:, NA_H + h, :].bitcast(F32).rearrange("p (t q) -> p t q", q=P),
                                        ALU.subtract).then_inc(y0_lo, 1)

            dve.wait_ge(b2_sel, 4)
            na_a(0)
            for i in range(16):
                if i + 1 < 16:
                    na_a(i + 1)
                dve.wait_ge(na_exp, i + 1)
                nc.vector.reciprocal(sm[:, 32 + i:33 + i], sm[:, 16 + i:17 + i]).then_inc(na_rr, 1)
                dve.wait_ge(na_rr, i + 1)
                nc.vector.tensor_scalar(PR[:, i % 2, :], PR[:, i % 2, :], sm[:, 32 + i:33 + i], None,
                                        ALU.mult).then_inc(na_p, 1)
                if i % 4 == 1 and i > 1:
                    na_out(i // 4 - 1)
            dve.wait_ge(m_sq, 1)
            nc.vector.tensor_reduce(MACC[:, :], MSQ[:, :, :].rearrange("p k t -> p t k"), AX.X, ALU.add).then_inc(m_acc, 1)
            na_out(NA_H - 1)
            dve.wait_ge(m_r, 1)
            for k in range(KT):
                mm = nc.vector.scalar_tensor_tensor(out=M[:, k, :], in0=M[:, k, :], scalar=pcol("mem", k),
                                                    in1=MR[:, :], op0=ALU.mult, op1=ALU.mult)
            mm.then_inc(m_done, 1)
            dve.wait_ge(m_hi, 1)
            nc.vector.tensor_tensor(ML[:, :, :], M[:, :, :], MH[:, :, :].bitcast(F32), ALU.subtract).then_inc(m_done, 1)

            def cross(l):
                u0 = first[f"q{l}"]
                for g in range(2):
                    dve.wait_ge(r_done, norm_of[f"q{l}"] + 1)
                    dve.wait_ge(w_used, u0 + 4 * g + 4)
                    nc.vector.tensor_tensor(QX[:, 4 * g:4 * g + 4, :], ps[:, 4 * g:4 * g + 4, :], over(R[:, :], 4),
                                            ALU.mult).then_inc(q_out, 1)

                def mx(h):
                    n = 4 * l + h
                    dve.wait_ge(xa_s, n + 1)
                    b = 2 * (h % 2)
                    c = 4 * (h % 2)
                    nc.vector.tensor_reduce(sm[:, 72 + c:76 + c], ps[:, b:b + 2, :].rearrange("p b (t m) -> p (b t) m", t=2),
                                            AX.X, ALU.max).then_inc(xa_mx, 1)
                    dve.wait_ge(xa_mx, n + 1)
                    if h >= 2:
                        dve.wait_ge(xa_exp, 4 * (n - 1))
                    nc.vector.tensor_scalar(sm[:, 48 + c:52 + c], sm[:, 72 + c:76 + c], -SCALE_X, None,
                                            ALU.mult).then_inc(xa_nm, 1)
                def out_lo(h):
                    dve.wait_ge(xa_hi, 4 * l + h + 1)
                    b = 4 + 2 * (h % 2)
                    nc.vector.tensor_tensor(YL[:, 2 * h:2 * h + 2, :], ps[:, b:b + 2, :],
                                            YH[:, 2 * h:2 * h + 2, :].bitcast(F32), ALU.subtract).then_inc(xa_lo, 1)

                def probs(h):
                    n = 4 * l + h
                    c = 4 * (h % 2)
                    dve.wait_ge(xa_exp, 4 * n + 4)
                    nc.vector.reciprocal(sm[:, 64 + c:68 + c], sm[:, 56 + c:60 + c]).then_inc(xa_rr, 1)
                    dve.wait_ge(xa_rr, n + 1)
                    nc.vector.tensor_tensor(PX[:, h % 2, :, :], PX[:, h % 2, :, :],
                                            sm[:, 64 + c:68 + c].unsqueeze(2).broadcast_to([P, NCH, NMEM]),
                                            ALU.mult).then_inc(xa_p, 1)

                for step, h in ((mx, 0), (mx, 1), (probs, 0), (probs, 1), (mx, 2), (mx, 3), (probs, 2), (probs, 3),
                                (out_lo, 0), (out_lo, 1), (out_lo, 2), (out_lo, 3)):
                    step(h)

            def ffn(l):
                name = f"up{l}"
                u0, ng = first[name], FF1 // 256
                nd, na = FD * ng * l, FA * ng * l
                w0, nf = PARAM_COLS[f"ffn_w{l}"][0], FF1 // P

                def group(g, bank):
                    def tap(i, q):
                        return par[:, bass.ds(g * 2 + (w0 + i * nf + q), 1)]

                    def step(n):
                        dve.wait_ge(ffn_dve, g * FD + (nd + n))
                    dve.wait_ge(w_used, g * 4 + (u0 + 4))
                    nc.vector.tensor_tensor(GP[:, :, 1:T + 1], ps[:, bank + 2:bank + 4, :], over(R[:, :], 2),
                                            ALU.mult).then_inc(ffn_dve, 1)
                    for q in range(2):
                        step(1)
                        nc.vector.tensor_scalar(CV[:, q, :], GP[:, q, 0:T], tap(0, q), None,
                                                ALU.mult).then_inc(ffn_dve, 1)
                    for i in (1, 2):
                        for q in range(2):
                            step(2 * i + q)
                            nc.vector.scalar_tensor_tensor(out=CV[:, q, :], in0=GP[:, q, i:T + i], scalar=tap(i, q),
                                                           in1=CV[:, q, :], op0=ALU.mult,
                                                           op1=ALU.add).then_inc(ffn_dve, 1)
                    nc.vector.tensor_tensor(UU[:, :, :], ps[:, bank:bank + 2, :], over(R[:, :], 2),
                                            ALU.mult).then_inc(ffn_dve, 1)
                    step(8)
                    dve.wait_ge(ffn_act, g * FA + (na + 2))
                    nc.vector.tensor_tensor(HF[:, :, :], UU[:, :, :], EG[:, :, :], ALU.mult).then_inc(ffn_dve, 1)
                    dve.wait_ge(ffn_act, g * FA + (na + 3))
                    nc.vector.tensor_tensor(HID[:, bass.ds(g * 2 + nf, 2), :], HF[:, :, :],
                                            HID[:, bass.ds(g * 2, 2), :].bitcast(F32),
                                            ALU.subtract).then_inc(ffn_dve, 1)

                nc.vector.memset(GP[:, :, 0:1], 0.0)
                nc.vector.memset(GP[:, :, T + 1:T + 2], 0.0).then_inc(pad_d, 1)
                dve.wait_ge(pad_d, 2 * l + 1)
                dve.wait_ge(r_done, norm_of[name] + 1)
                with dve.Fori(0, ng // 2) as i:
                    for s in range(2):
                        group(i * 2 + s, 4 * s)

            def conv_mixer():
                u0 = first["in1"]
                nc.vector.memset(VP[:, :, 0:1], 0.0)
                nc.vector.memset(VP[:, :, T + 1:T + 2], 0.0).then_inc(pad_d, 1)
                dve.wait_ge(pad_d, 2)
                dve.wait_ge(r_done, norm_of["in1"] + 1)
                for q in range(2):
                    n = 18 * q

                    def bank(g):
                        b = 4 * ((3 * q + g) % 2)
                        return ps[:, b:b + 4, :]

                    def used(g):
                        dve.wait_ge(w_used, u0 + 4 * (3 * q + g) + 4)
                    used(0)
                    nc.vector.tensor_tensor(CS[:, :, :], bank(0), over(R[:, :], 4), ALU.mult).then_inc(cm_dve, 1)
                    used(1)
                    nc.vector.tensor_tensor(VP[:, :, 1:T + 1], bank(1), over(R[:, :], 4), ALU.mult).then_inc(cm_dve, 1)
                    dve.wait_ge(cm_dve, n + 2)
                    nc.vector.tensor_tensor(VP[:, :, 1:T + 1], VP[:, :, 1:T + 1], CS[:, :, :], ALU.mult).then_inc(cm_dve, 1)
                    dve.wait_ge(cm_dve, n + 3)
                    for i in range(3):
                        for c in range(4):
                            tap = pcol("conv_c", i * KT + 4 * q + c)
                            if i == 0:
                                nc.vector.tensor_scalar(CVC[:, c, :], VP[:, c, 0:T], tap, None,
                                                        ALU.mult).then_inc(cm_dve, 1)
                            else:
                                dve.wait_ge(cm_dve, n + 4 * i + c)
                                nc.vector.scalar_tensor_tensor(out=CVC[:, c, :], in0=VP[:, c, i:T + i], scalar=tap,
                                                               in1=CVC[:, c, :], op0=ALU.mult,
                                                               op1=ALU.add).then_inc(cm_dve, 1)
                    used(2)
                    nc.vector.tensor_tensor(TY[:, :, :], bank(2), over(R[:, :], 4), ALU.mult).then_inc(cm_dve, 1)
                    dve.wait_ge(cm_dve, n + 16)
                    nc.vector.tensor_tensor(TY[:, :, :], TY[:, :, :], CVC[:, :, :], ALU.mult).then_inc(cm_dve, 1)
                    dve.wait_ge(cm_act, q + 1)
                    nc.vector.tensor_tensor(YL[:, 4 * q:4 * q + 4, :], TY[:, :, :],
                                            YH[:, 4 * q:4 * q + 4, :].bitcast(F32), ALU.subtract).then_inc(cm_dve, 1)

            residual("out0")
            for l in range(2):
                if l == 1:
                    conv_mixer()
                    residual("out1")
                cross(l)
                residual(f"wo{l}")
                ffn(l)
                residual(f"down{l}")

            def banks(b):
                return ps[:, b:b + 4, :]

            def scaled(dst, b, done):
                nc.vector.tensor_tensor(dst, banks(b), over(R[:, :], 4), ALU.mult).then_inc(done, 1)

            def retention():
                dve.wait_ge(r_done, norm_of["rqk"] + 1)
                dve.wait_ge(w_used, first["rqk"] + 4)
                scaled(RQ[:, :, :], 0, rqk_out)
                dve.wait_ge(w_used, first["rqk"] + 8)
                nc.vector.scalar_tensor_tensor(out=RK[:, :, :], in0=banks(4), scalar=0.125, in1=over(R[:, :], 4),
                                               op0=ALU.mult, op1=ALU.mult).then_inc(rqk_out, 1)
                dve.wait_ge(t_loaded, 48)

                def rotate(b, x):
                    dve.wait_ge(rot_done, b + 1)
                    nc.vector.tensor_tensor(RT[:, :, :], RT[:, :, :], over(SIN[:, :], 4), ALU.mult).then_inc(rot_out, 1)
                    nc.vector.tensor_tensor(x[:, :, :], x[:, :, :], over(COS[:, :], 4), ALU.mult).then_inc(rot_out, 1)
                    dve.wait_ge(rot_out, 3 * b + 2)
                    nc.vector.tensor_tensor(x[:, :, :], x[:, :, :], RT[:, :, :], ALU.add).then_inc(rot_out, 1)

                for g in range(2):
                    rotate(g, (RQ, RK)[g])
                    dve.wait_ge(w_used, first["rv"] + 4 * g + 4)
                    part = RV[:, :, g * T:(g + 1) * T]
                    for t in range(NCH):
                        nc.vector.tensor_scalar(part[:, t, :], ps[:, 4 * g + t, :], RC[:, t:t + 1], None,
                                                ALU.mult).then_inc(rv_out, 1)
                    v4 = part.rearrange("p t (h d) -> p t h d", d=P)
                    mean = RVM[:, :, 4 * g:4 * g + 4]
                    dve.wait_ge(rv_out, 7 * g + 4)
                    nc.vector.tensor_reduce(mean, v4, AX.X, ALU.add).then_inc(rv_out, 1)
                    dve.wait_ge(rv_out, 7 * g + 5)
                    nc.vector.tensor_scalar(mean, mean, -1.0 / P, None, ALU.mult).then_inc(rv_out, 1)
                    dve.wait_ge(rv_out, 7 * g + 6)
                    for t in range(NCH):
                        ins_ = nc.vector.tensor_tensor(v4[:, t], v4[:, t], mean[:, t].unsqueeze(2).broadcast_to([P, 4, P]),
                                                       ALU.add)
                    ins_.then_inc(rv_out, 1)
                dve.wait_ge(h_saved, 16)
                for g in range(2):
                    dve.wait_ge(w_used, first["rgate"] + 4 * g + 4)
                    scaled(RG[:, 4 * g:4 * g + 4, :], 4 * g, rg_dve)

                def norm(h):
                    dve.wait_ge(ret_rn, h + 1)
                    nc.vector.scalar_tensor_tensor(out=RO[:, h, :], in0=ps[:, 6 + h % 2, :], scalar=pcol("ret_g", h),
                                                   in1=RN[:, :], op0=ALU.mult, op1=ALU.mult).then_inc(ret_ro, 1)

                for h in range(RET_H):
                    dve.wait_ge(ret_dec, h + 1)
                    if h >= 2:
                        dve.wait_ge(ret_o, h - 1)
                    for j in range(NCH):
                        w = T - j * P
                        dve.wait_ge(ret_s, 3 * h + min(j, 2) + 1)
                        b, o = ((0, 0), (1, 0), (2, 0), (2, 256))[j]
                        a = (0, 512, 896, 1152)[j]
                        nc.vector.tensor_tensor(SCO[:, h % 2, a:a + w], ps[:, 3 * (h % 2) + b, o:o + w],
                                                DEC[:, h % 2, 0:w], ALU.mult).then_inc(ret_sc, 1)
                    if h >= 2:
                        norm(h - 2)
                norm(RET_H - 2)
                norm(RET_H - 1)

            def decay_rows():
                B1, A1, A3, SPR, BEG, EGL, EG8, ONE = [rows[i][:, :] for i in range(8)]
                step = lambda n: dve.wait_ge(ab_dve, n)
                dve.wait_ge(w_used, first["dab"] + 1)
                nc.vector.tensor_tensor(B1, ps[0:DN_H, 0, :], R[0:DN_H, :], ALU.mult).then_inc(ab_dve, 1)
                nc.vector.tensor_tensor(A1, ps[32:32 + DN_H, 0, :], R[32:32 + DN_H, :], ALU.mult).then_inc(ab_dve, 1)
                step(2)
                nc.vector.tensor_scalar(A1, A1, pcol("dt_bias")[0:DN_H, :], None, ALU.add).then_inc(ab_dve, 1)
                nc.vector.memset(ONE, 1.0)
                dve.wait_ge(ab_act, 4)
                step(3)
                nc.vector.scalar_tensor_tensor(out=SPR, in0=A1, scalar=0.0, in1=A3, op0=ALU.max,
                                               op1=ALU.add).then_inc(ab_dve, 1)
                dve.wait_ge(ab_act, 5)
                step(4)
                nc.vector.tensor_scalar(SPR, SPR, sm[0:DN_H, 80:81], -1.0, ALU.mult, ALU.mult).then_inc(ab_dve, 1)
                step(5)
                for n in range(NCH):
                    c = slice(n * P, (n + 1) * P)
                    nc.vector.tensor_tensor_scan(GR[:, c], ONE[:, c], SPR[:, c], 0.0, ALU.mult, ALU.add).then_inc(ab_dve, 1)
                step(9)
                for n in range(NCH):
                    c = slice(n * P, (n + 1) * P)
                    nc.vector.tensor_scalar(EGL[:, c], GR[:, c], GR[:, (n + 1) * P - 1:(n + 1) * P], -1.0,
                                            ALU.subtract, ALU.mult).then_inc(ab_dve, 1)
                dve.wait_ge(ab_act, 6)
                nc.vector.scalar_tensor_tensor(out=BEG, in0=EG8, scalar=-1.0, in1=BR[:, :], op0=ALU.mult,
                                               op1=ALU.mult).then_inc(ab_dve, 1)

            def delta(q):
                u0 = first[f"dvqk{q}"]
                pb = pair_banks(q)
                nd = 51 * q
                bv, bq = (4, 0) if q == 0 else (0, 4)
                if q == 0:
                    dve.wait_ge(ab_act, 8)
                nc.vector.memset(GP3[:, :, 0:3], 0.0).then_inc(pad_d, 1)
                dve.wait_ge(pad_d, 4 + q)
                for i, (g, dst, bank) in enumerate(((2, VB, bv), (0, QN, bq), (1, KN, bv))):
                    dve.wait_ge(w_used, u0 + 4 * i + 4)
                    if nd + i:
                        dve.wait_ge(dq_dve, nd + 17 * i)
                    nc.vector.tensor_tensor(GP3[:, :, 3:T + 3], banks(bank), over(R[:, :], 4),
                                            ALU.mult).then_inc(dq_dve, 1)
                    for j in range(4):
                        for c in range(4):
                            tap = pcol("dn_conv", j * 3 * DN_H + g * DN_H + 4 * q + c)
                            dve.wait_ge(dq_dve, nd + 17 * i + max(1, 4 * j - 2 + c))
                            if j == 0:
                                nc.vector.tensor_scalar(dst[:, c, :], GP3[:, c, 0:T], tap, None, ALU.mult).then_inc(dq_dve, 1)
                            else:
                                nc.vector.scalar_tensor_tensor(out=dst[:, c, :], in0=GP3[:, c, j:T + j], scalar=tap,
                                                               in1=dst[:, c, :], op0=ALU.mult, op1=ALU.add).then_inc(dq_dve, 1)

                def normalise(i, x, ln, scale):
                    for n, part in enumerate((slice(0, 2), slice(2, 4))):
                        dve.wait_ge(l2_r, 4 * q + 2 * i + n + 1)
                        nc.vector.scalar_tensor_tensor(out=x[:, part, :], in0=x[:, part, :], scalar=scale,
                                                       in1=ln[:, part, :], op0=ALU.mult, op1=ALU.mult).then_inc(l2_n, 1)

                normalise(0, QN, LNq, float(P) ** -0.5)
                dve.wait_ge(w_used, first[f"gated{q}"] + 4)
                dve.wait_ge(h_saved, 16)
                dve.wait_ge(x_lo, KT * (norm_of["rqk"] + 1))
                dve.wait_ge(rg_dve, 6)
                scaled(SGD[:, 4 * q:4 * q + 4, :], bv, ga_dve)
                normalise(1, KN, LNk, 1.0)
                dve.wait_ge(l_loaded, 16)

                def chunks(ap):
                    return ap.rearrange("p (n c) -> p n c", n=NCH)

                def column(a, h):
                    return TC[:, a, :, h:h + 1].broadcast_to([P, NCH, P])

                for pr in range(2):
                    m = 4 * q + 2 * pr
                    n0 = 14 * (2 * q + pr)
                    for p in range(2):
                        h, hh = m + p, 2 * pr + p
                        step = lambda k: dve.wait_ge(dp_dve, n0 + pair_step(p, k))
                        dve.wait_ge(gb_loaded, 16 * (2 * q + pr + 1))
                        if p == 0:
                            dve.wait_ge(l2_n, 4 * q + 4)
                        nc.vector.tensor_tensor(T1[:, p, :], KN[:, hh, :], GB[:, 1, p, :], ALU.mult).then_inc(dp_dve, 1)
                        nc.vector.tensor_tensor(chunks(DL[:, p, :]), chunks(GB[:, 0, p, :]), column(1, h),
                                                ALU.subtract).then_inc(dp_dve, 1)
                        step(2)
                        nc.vector.scalar_tensor_tensor(out=chunks(DL[:, p, :]), in0=chunks(DL[:, p, :]), scalar=0.0,
                                                       in1=over(cst[:, CONSTS["causal"], :], NCH), op0=ALU.min,
                                                       op1=ALU.add).then_inc(dp_dve, 1)
                    for p in range(2):
                        h, hh = m + p, 2 * pr + p
                        step = lambda k: dve.wait_ge(dp_dve, n0 + pair_step(p, k))
                        dve.wait_ge(dp_a, m + p + 1)
                        dve.wait_ge(dp_lt, m + p + 1)
                        nc.vector.tensor_tensor(AT[:, p, :], ps[:, pb(p) + 1, :], DL[:, p, :], ALU.mult).then_inc(dp_dve, 1)
                        step(4)
                        nc.vector.tensor_tensor(chunks(MT[:, hh, :]), chunks(AT[:, p, :]), over(LVM[:, 0, :], NCH),
                                                ALU.mult).then_inc(dp_dve, 1)
                        step(5)
                        nc.vector.tensor_tensor(chunks(MT[:, hh, :]), chunks(MT[:, hh, :]), over(ident, NCH),
                                                ALU.add).then_inc(dp_dve, 1)
                        step(6)
                        nc.vector.transpose(MM[:, p, :], MT[:, hh, :]).then_inc(dp_dve, 1)

                    def late(i):
                        p = i % 2
                        hh = 2 * pr + p
                        if i < 2:
                            nc.vector.tensor_tensor(ATT[:, hh, :], ps[:, pb(p), :], DL[:, p, :], ALU.mult).then_inc(dp_late, 1)
                        else:
                            dve.wait_ge(dp_late, 6 * (2 * q + pr) + i - 1)
                            nc.vector.tensor_tensor(QN[:, hh, :], QN[:, hh, :], EGA[p][:, :], ALU.mult).then_inc(dp_late, 1)
                            nc.vector.tensor_copy(sm[:, 84 + 4 * hh:88 + 4 * hh], EGA[p][:, P - 1:T:P]).then_inc(dp_late, 1)

                    nl, npe = 34 * (2 * q + pr), 24 * (2 * q + pr)
                    for li, b in enumerate(LEVELS[1:]):
                        for p in range(2):
                            dve.wait_ge(lv_pe, npe + 4 * li + p + 1)
                            nc.vector.tensor_tensor(chunks(T1[:, p, :]), chunks(ps[:, pb(p) + 2, :]),
                                                    over(LVM[:, li + 1, :], NCH), ALU.mult).then_inc(lv_dve, 1)
                        for p in range(2):
                            hh = 2 * pr + p
                            dve.wait_ge(lv_pe, npe + 4 * li + 3 + p)
                            if li == 0:
                                dve.wait_ge(dp_dve, n0 + 14)
                            else:
                                dve.wait_ge(lv_dve, nl + 6 * li)
                            nc.vector.tensor_tensor(MT[:, hh, :], MT[:, hh, :], ps[:, pb(p) + 3, :],
                                                    ALU.subtract).then_inc(lv_dve, 1)
                            if b <= 16:
                                dve.wait_ge(lv_dve, nl + 6 * li + 3 + 2 * p)
                                nc.vector.transpose(MM[:, p, :], MT[:, hh, :]).then_inc(lv_dve, 1)
                            elif b == 32:
                                nc.vector.tensor_tensor(MM[:, p, :], MM[:, p, :], ps[:, pb(p) + 1, :],
                                                        ALU.subtract).then_inc(lv_dve, 1)
                        if li < 4:
                            late(li)
                for n in range(NCH):
                    for hh in range(4):
                        h = 4 * q + hh
                        if n:
                            dve.wait_ge(sc_ks, 12 * q + 4 * (n - 1) + hh + 1)
                            nc.vector.scalar_tensor_tensor(out=YS[:, hh, :], in0=ps[:, hh, 0:P],
                                                           scalar=TC[:, 2, n, h:h + 1], in1=VB[:, hh, n * P:(n + 1) * P],
                                                           op0=ALU.mult, op1=ALU.add).then_inc(sc_y, 1)
                    if n == NCH - 1:
                        continue
                    for hh in range(4):
                        dve.wait_ge(sc_su, 12 * q + 4 * n + hh + 1)
                        if n == 0:
                            nc.vector.tensor_copy(SS[:, hh, :], ps[:, hh, 2 * P:3 * P]).then_inc(sc_s, 1)
                        else:
                            dve.wait_ge(sc_s, 12 * q + 4 * (n - 1) + hh + 1)
                            nc.vector.scalar_tensor_tensor(out=SS[:, hh, :], in0=SS[:, hh, :],
                                                           scalar=sm[:, 84 + 4 * hh + n:85 + 4 * hh + n],
                                                           in1=ps[:, hh, 2 * P:3 * P], op0=ALU.mult,
                                                           op1=ALU.add).then_inc(sc_s, 1)
                dve.wait_ge(do_r, q + 1)
                nc.vector.scalar_tensor_tensor(out=DO[:, 4 * q:4 * q + 4, :], in0=DO[:, 4 * q:4 * q + 4, :], scalar=pcol("dn_g"),
                                               in1=LNo[:, :, :], op0=ALU.mult, op1=ALU.mult).then_inc(do_n, 1)

            def ffn2():
                u0, ng = first["up2"], FF2 // 256
                w0, b0, nf = PARAM_COLS["ffn_w2"][0], PARAM_COLS["ffn_b2"][0], FF2 // P
                nc.vector.memset(GP4[:, :, 0:2], 0.0).then_inc(pad_d, 1)
                dve.wait_ge(pad_d, 6)
                dve.wait_ge(r_done, norm_of["up2"] + 1)

                def group(g, bank):
                    def of(col, q):
                        return par[:, bass.ds(g * 2 + (col + (q // 2) * nf + q % 2), 1)]

                    def step(n):
                        dve.wait_ge(up2_dve, g * FD2 + n)
                    dve.wait_ge(w_used, g * 4 + (u0 + 4))
                    nc.vector.tensor_tensor(GP4[:, :, 2:T + 2], banks(bank), over(R[:, :], 4), ALU.mult).then_inc(up2_dve, 1)
                    for q in range(4):
                        step(1)
                        nc.vector.tensor_scalar(CV4[:, q, :], GP4[:, q, 0:T], of(w0, q), of(b0, q),
                                                ALU.mult, ALU.add).then_inc(up2_dve, 1)
                    for i in (1, 2):
                        for q in range(4):
                            step(4 * i - 2 + q)
                            nc.vector.scalar_tensor_tensor(out=CV4[:, q, :], in0=GP4[:, q, i:T + i],
                                                           scalar=of(w0 + 2 * nf * i, q), in1=CV4[:, q, :],
                                                           op0=ALU.mult, op1=ALU.add).then_inc(up2_dve, 1)
                    step(13)
                    dve.wait_ge(up2_act, g * FA2 + 1)
                    nc.vector.tensor_tensor(HF2[:, :, :], SA[:, :, :], CV4[:, 2:4, :], ALU.mult).then_inc(up2_dve, 1)
                    dve.wait_ge(up2_act, g * FA2 + 2)
                    nc.vector.tensor_tensor(HID[:, bass.ds(g * 2 + nf, 2), :], HF2[:, :, :],
                                            HID[:, bass.ds(g * 2, 2), :].bitcast(F32),
                                            ALU.subtract).then_inc(up2_dve, 1)

                with dve.Fori(0, ng // 2) as i:
                    for s in range(2):
                        group(i * 2 + s, 4 * s)
                group(ng - 1, 0)

            def between():
                n = norm_of["rqk"]
                mean2 = sm[:, 108:112]
                dve.wait_ge(r_done, n + 1)
                nc.vector.tensor_tensor(SQ[:, :], ps[:, STAT_BANK + 2, :], R[:, :], ALU.mult).then_inc(bn_dve, 1)
                dve.wait_ge(bn_dve, 1)
                nc.vector.tensor_tensor(SQ[:, :], SQ[:, :], R[:, :], ALU.mult).then_inc(bn_dve, 1)
                dve.wait_ge(rc_done, 2)
                nc.vector.tensor_tensor(mean2, ps[:, STAT_BANK + 1, NCH:2 * NCH], RC[:, :], ALU.mult).then_inc(bn_dve, 1)
                dve.wait_ge(bn_dve, 3)
                nc.vector.tensor_tensor(mean2, mean2, RC[:, :], ALU.mult).then_inc(bn_dve, 1)
                for c in range(KT):
                    nc.vector.scalar_tensor_tensor(out=H[:, c, :], in0=H[:, c, :], scalar=pcol("final1", c),
                                                   in1=R[:, :], op0=ALU.mult, op1=ALU.mult).then_inc(bn_dve, 1)
                dve.wait_ge(bn_act, 4)
                dve.wait_ge(bn_dve, 4 + KT)
                nc.vector.tensor_tensor(R[:, :], R[:, :], SQ[:, :], ALU.mult).then_inc(bn_dve, 1)
                nc.vector.tensor_tensor(RC[:, :], RC[:, :], mean2, ALU.mult).then_inc(bn_dve, 1)
                dve.wait_ge(bn_dve, 6 + KT)

            def block2():
                between()
                retention()
                for g in range(2):
                    part = slice(4 * g, 4 * g + 4)
                    dve.wait_ge(rg_act, g + 1)
                    nc.vector.tensor_tensor(TG[:, part, :], RG[:, part, :], RO[:, part, :], ALU.mult).then_inc(rg_dve, 1)
                    dve.wait_ge(rg_act, g + 3)
                    nc.vector.tensor_tensor(YL[:, part, :], TG[:, part, :], YH[:, part, :].bitcast(F32),
                                            ALU.subtract).then_inc(rg_dve, 1)
                for g in range(2):
                    dve.wait_ge(w_used, first["gater"] + 4 * g + 4)
                    scaled(MG[:, 4 * g:4 * g + 4, :], 4 * g, gr_dve)
                for g in range(2):
                    dve.wait_ge(w_used, first["retbr"] + 4 * g + 4)
                    dve.wait_ge(gr_act, g + 1)
                    nc.vector.tensor_tensor(MG[:, 4 * g:4 * g + 4, :], MG[:, 4 * g:4 * g + 4, :], banks(4 * g),
                                            ALU.mult).then_inc(rb_dve, 1)
                decay_rows()
                delta(0)
                delta(1)
                for g in range(2):
                    part = slice(4 * g, 4 * g + 4)
                    dve.wait_ge(w_used, first["dz"] + 4 * g + 4)
                    if g:
                        dve.wait_ge(dz_dve, 3)
                    scaled(TZ[:, :, :], 4 * g, dz_dve)
                    dve.wait_ge(dz_act, 2 * g + 1)
                    nc.vector.tensor_tensor(DO[:, part, :], DO[:, part, :], TZ[:, :, :], ALU.mult).then_inc(dz_dve, 1)
                    dve.wait_ge(dz_act, 2 * g + 2)
                    nc.vector.tensor_tensor(YL[:, part, :], DO[:, part, :], YH[:, part, :].bitcast(F32),
                                            ALU.subtract).then_inc(dz_dve, 1)
                for g in range(2):
                    part = slice(4 * g, 4 * g + 4)
                    dve.wait_ge(w_used, first["dnbr"] + 4 * g + 4)
                    dve.wait_ge(ga_act, 2)
                    if g:
                        dve.wait_ge(dn_dve, 3)
                    else:
                        dve.wait_ge(dz_dve, 6)
                    nc.vector.tensor_tensor(TZ[:, :, :], SGD[:, part, :], banks(4 * g), ALU.mult).then_inc(dn_dve, 1)
                    dve.wait_ge(dn_dve, 3 * g + 1)
                    dve.wait_ge(rb_dve, 2)
                    nc.vector.tensor_tensor(MG[:, part, :], MG[:, part, :], TZ[:, :, :], ALU.add).then_inc(dn_dve, 1)
                    dve.wait_ge(dn_act, g + 1)
                    nc.vector.tensor_tensor(NL[:, part, :], MG[:, part, :], NH[:, part, :].bitcast(F32),
                                            ALU.subtract).then_inc(dn_dve, 1)
                dve.wait_ge(h_back, 16)
                residual("wo2")
                ffn2()
                residual("down2", flip=4)
                dve.wait_ge(r_done, norm_of["final"] + 1)
                for c in range(KT):
                    nc.vector.scalar_tensor_tensor(out=H[:, c, :], in0=H[:, c, :], scalar=pcol("final2", c),
                                                   in1=R[:, :], op0=ALU.mult, op1=ALU.mult).then_inc(fin_dve, 1)

            block2()


def shape_constants():
    c = {}
    ident = np.eye(P)
    half = P // 4
    m = np.arange(P)
    causal = np.where(np.arange(P)[None, :] >= np.arange(P)[:, None], 0.0, -1e30)
    tiles = {"ident": ident, "ones": np.full((P, P), 1.0 / D), "causal": causal}
    c["consts"] = np.stack([tiles[n] for n in CONSTS], axis=1).astype(np.float32)
    inv = 10000.0 ** (-np.arange(half, dtype=np.float32) * 2 / (2 * half))
    ang = (np.arange(T, dtype=np.float32)[None, :] * inv.astype(np.float32)[m % half][:, None]).astype(np.float32)
    c["rot_cos"] = np.cos(ang.astype(np.float64)).astype(np.float32)
    c["rot_sin"] = np.sin(ang.astype(np.float64)).astype(np.float32)
    age = np.arange(T)[None, :] - np.arange(P)[:, None]
    c["age"] = np.where(age >= 0, age, 1e9).astype(np.float32)
    i, j = np.arange(P)[:, None], np.arange(P)[None, :]
    lv = [np.where((i // (2 * b) == j // (2 * b)) & (i % (2 * b) >= b) & (j % (2 * b) < b), 1.0, 0.0) for b in LEVELS]
    lv[0] = -lv[0].T
    c["levels"] = np.stack(lv, axis=1).astype(np.float32)
    s = np.arange(T)
    ang = 2 * np.pi * ((s[:, None] * s[None, :]) % T) / T
    seq = np.stack([np.cos(ang), -np.sin(ang)], axis=1)
    c["fourier_seq"] = seq.reshape(NCH, P, 2, T).transpose(1, 0, 2, 3).astype(np.float32)
    g = np.arange(P)
    ang = 2 * np.pi * ((g[:, None] * g[None, :]) % P) / P
    c["fourier_grp"] = (np.concatenate([np.cos(ang), np.sin(ang)], axis=1) / np.sqrt(T * P)).astype(np.float32)
    return {k: np.ascontiguousarray(v) for k, v in c.items()}


def lay_out(inputs):
    a = {k: np.asarray(v) for k, v in inputs.items()}
    feat = lambda v: v.reshape(-1, P).T
    f = {"mem": feat(a["mem_norm_g"]), "final1": feat(a["final_norm_g"]), "mix2": feat(a["g_mix_2"][0]),
         "ffn2": feat(a["g_ffn_2"][0]), "final2": feat(a["g_final_2"]), "conv_c": feat(a["conv_c"][0]),
         "ret_g": feat(a["ret_norm_g_2"][0]), "dn_conv": feat(a["dn_conv_w_2"][0]), "dn_g": feat(a["dn_norm_g_2"][0]),
         "ffn_w2": feat(a["ffn_conv_w_2"][0]), "ffn_b2": feat(a["ffn_conv_b_2"][0]),
         "a_log": np.pad(a["dn_a_log_2"].T, ((0, P - DN_H), (0, 0))),
         "dt_bias": np.pad(a["dn_dt_bias_2"].T, ((0, P - DN_H), (0, 0)))}
    for l in range(2):
        f[f"mix{l}"] = feat(a["mix_norm_g"][l])
        f[f"xa{l}"] = feat(a["xa_norm_g"][l])
        f[f"ffn{l}"] = feat(a["ffn_norm_g"][l])
        f[f"ffn_w{l}"] = feat(a["ffn_conv_w"][l])
        f[f"ffn_b{l}"] = feat(a["ffn_conv_b"][l])
    out = {"xT": a["x"][0].T, "memT": a["mem"][0].T,
           "params": np.concatenate([f[n] for n in PARAM_COLS], axis=1),
           "rpb": np.pad(a["rpb"][0], ((0, 0), (0, 0), (RPB_PAD, RPB_PAD)))}
    for n in WEIGHTS:
        out[n] = a[n]
    out.update(shape_constants())
    return {k: np.ascontiguousarray(v) for k, v in out.items()}


WEIGHTS = ("w_in_ab", "w_out_ab", "w_in_c", "w_out_c", "xa_wq", "xa_wkv", "xa_wo", "ffn_w_up", "ffn_w_down",
           "w_in_2", "w_ret_br_2", "w_dn_br_2", "w_o_2", "w_up_2", "w_down_2")
C_DB, C_DA, C_GR, C_GD = 7168, 7176, 7184, 8208
LOG_GAMMA = [float(np.log(1.0 - 2.0 ** (-5.0 - h))) for h in range(RET_H)]
SCALE_NA = float(P) ** -0.5
SCALE_X = float(2 * P) ** -0.5
STAT_BANK = 4
BY_TOKEN = ("in0", "rqk")
MEM_BANK = 6


def build(nc, arrays):
    ins = {n: nc.dram_tensor(n, a.shape, F32, kind="ExternalInput").ap() for n, a in arrays.items()}
    out = nc.dram_tensor("outT", (D, T), F32, kind="ExternalOutput").ap()
    program(nc, ins, out)


def kernel(**inputs):
    import concourse.bacc as _bacc
    from concourse.bass_utils import run_bass_kernel_spmd as _run

    arrays = lay_out(inputs)
    nc = _bacc.Bacc("TRN2", target_bir_lowering=False, num_devices=1, dynamic_dma_scratch_size=1024)
    build(nc, arrays)
    r = _run(nc, [arrays], core_ids=[0])
    return np.ascontiguousarray(r.results[0]["outT"].T)[None]
```
